# Optimizing a Trainium2 kernel written in Bass

```python
import math
import jax, jax.numpy as jnp
from jax import lax
import numpy as np

D_MODEL = 1024
BATCH = 1
SEQ = 256
DEPTH = 1

D_CONV = D_MODEL // 2
CONV_WIDTH = 31
N_RNN_HEADS = 4
RNN_HEAD_DIM = 128
D_RNN = N_RNN_HEADS * RNN_HEAD_DIM
RNN_CHUNK = 64
N_ATT_HEADS = 8
D_LATENT = 128
ATT_HEAD_DIM = 64
D_ATT = N_ATT_HEADS * ATT_HEAD_DIM
N_IDX_HEADS = 4
IDX_HEAD_DIM = 64
TOPK_MAX = 256
Q_BLOCK = 128
N_BUCKETS = 32
MAX_EXACT = N_BUCKETS // 2
MAX_DISTANCE = 128
N_EXPERTS = 32
TOPK_EXPERTS = 4
D_EXPERT = 256
D_SHARED = 256
ROUTE_SCALE = 2.5
MOE_BLOCK = 128
N_BRANCH = 3
DEEPNORM_ALPHA = (2 * DEPTH) ** 0.25
DEEPNORM_BETA = (8 * DEPTH) ** -0.25
LN_EPS = 1e-5
SPLITS = (2 * D_CONV,
          D_RNN, D_RNN, D_RNN, D_RNN,
          N_ATT_HEADS * D_LATENT, D_LATENT,
          N_IDX_HEADS * IDX_HEAD_DIM, IDX_HEAD_DIM, N_IDX_HEADS,
          N_BRANCH * D_MODEL)
N_IN = sum(SPLITS)

kernel_name = "hybrid_conv_hgrn2_dsa_moe_deepnorm"

def layer_norm(x, g, b):
    xf = x.astype(jnp.float32)
    mu = jnp.mean(xf, axis=-1, keepdims=True)
    var = jnp.mean(jnp.square(xf - mu), axis=-1, keepdims=True)
    return ((xf - mu) * lax.rsqrt(var + LN_EPS) * g.astype(jnp.float32) + b.astype(jnp.float32)).astype(x.dtype)

def rms_norm(x, g):
    xf = x.astype(jnp.float32)
    return xf * lax.rsqrt(jnp.mean(jnp.square(xf), axis=-1, keepdims=True) + LN_EPS) * g.astype(jnp.float32)

def t5_bucket(n):
    nf = jnp.maximum(n, 1).astype(jnp.float32)
    large = MAX_EXACT + (jnp.log(nf / MAX_EXACT) / math.log(MAX_DISTANCE / MAX_EXACT)
                         * (N_BUCKETS - MAX_EXACT)).astype(jnp.int32)
    large = jnp.minimum(large, N_BUCKETS - 1)
    return jnp.where(n < MAX_EXACT, n, large)

def conformer_conv(glu_in, dw, db, ln_g, ln_b, w_proj):
    a, gate = jnp.split(glu_in, 2, axis=-1)
    u = a * jax.nn.sigmoid(gate)
    u = lax.conv_general_dilated(u, dw[:, None, :], window_strides=(1,),
                                 padding=[(CONV_WIDTH - 1, 0)],
                                 dimension_numbers=('NWC', 'WIO', 'NWC'),
                                 feature_group_count=D_CONV) + db
    u = jax.nn.silu(layer_norm(u, ln_g, ln_b))
    return u @ w_proj

def hgrn2(q, fz, i, g, lb, norm_g, w_proj, out_dtype):
    B, S, _ = q.shape
    H, Dh, C = N_RNN_HEADS, RNN_HEAD_DIM, RNN_CHUNK
    nC = S // C
    fzf = fz.astype(jnp.float32)
    log_f = jnp.logaddexp(jnp.log(lb), jnp.log1p(-lb) + jax.nn.log_sigmoid(fzf))
    k = (1.0 - lb) * jax.nn.sigmoid(-fzf)

    def chunks(t):
        return t.astype(jnp.float32).reshape(B, nC, C, H, Dh).transpose(1, 0, 3, 2, 4)

    causal = jnp.tril(jnp.ones((C, C), dtype=bool))

    def step(state, inp):
        qc, kc, vc, lfc = inp
        A = jnp.cumsum(lfc, axis=2)
        o_inter = jnp.einsum('bhtd,bhde->bhte', qc * jnp.exp(A), state)
        rel = A[:, :, :, None, :] - A[:, :, None, :, :]
        decay = jnp.exp(jnp.where(causal[:, :, None], rel, -jnp.inf))
        P = jnp.einsum('bhtd,bhsd,bhtsd->bhts', qc, kc, decay)
        o = o_inter + jnp.einsum('bhts,bhse->bhte', P, vc)
        A_last = A[:, :, -1:, :]
        new_state = (jnp.exp(A_last[:, :, 0, :])[..., None] * state
                     + jnp.einsum('bhsd,bhse->bhde', kc * jnp.exp(A_last - A), vc))
        return new_state, o

    s0 = jnp.zeros((B, H, Dh, Dh), jnp.float32)
    _, o = lax.scan(step, s0, (chunks(q), chunks(k), chunks(i), chunks(log_f)))
    o = o.transpose(1, 0, 3, 2, 4).reshape(B, S, H, Dh)
    o = rms_norm(o, norm_g.reshape(H, Dh)) * jax.nn.sigmoid(g.astype(jnp.float32)).reshape(B, S, H, Dh)
    return o.reshape(B, S, D_RNN).astype(out_dtype) @ w_proj

def dsa_attention(q, c_raw, qi, ki, wi, kv_g, w_uv, rel_bias, w_proj, out_dtype):
    B, S, _ = q.shape
    H, DL = N_ATT_HEADS, D_LATENT
    K = min(TOPK_MAX, S // 4)
    nb = S // Q_BLOCK
    scale = DL ** -0.5
    q = q.astype(jnp.float32).reshape(B, S, H, DL)
    c = rms_norm(c_raw, kv_g)
    qi = qi.astype(jnp.float32).reshape(B, S, N_IDX_HEADS, IDX_HEAD_DIM)
    ki = ki.astype(jnp.float32)
    wi = wi.astype(jnp.float32)
    s_pos = jnp.arange(S)

    def blocks(t):
        return t.reshape(B, nb, Q_BLOCK, *t.shape[2:]).swapaxes(0, 1)

    def attend_block(inp):
        qb, qib, wb, t0 = inp
        t_pos = t0 + jnp.arange(Q_BLOCK)
        score = jnp.einsum('bth,bths->bts', wb, jax.nn.relu(jnp.einsum('bthd,bsd->bths', qib, ki)))
        score = jnp.where(s_pos[None, None, :] <= t_pos[None, :, None], score, -jnp.inf)
        _, sel = lax.top_k(score, K)
        c_sel = jax.vmap(lambda cb, ib: cb[ib])(c, sel)
        dist = t_pos[None, :, None] - sel
        bias = rel_bias[t5_bucket(jnp.maximum(dist, 0))]
        logits = jnp.einsum('bthc,btkc->bthk', qb, c_sel) * scale + bias.transpose(0, 1, 3, 2)
        logits = jnp.where((dist >= 0)[:, :, None, :], logits, -jnp.inf)
        p = jax.nn.softmax(logits, axis=-1)
        return jnp.einsum('bthk,btkc->bthc', p, c_sel)

    o = lax.map(attend_block, (blocks(q), blocks(qi), blocks(wi), jnp.arange(nb) * Q_BLOCK))
    o = o.swapaxes(0, 1).reshape(B, S, H, DL)
    o = jnp.einsum('bshc,hcv->bshv', o.astype(out_dtype), w_uv).reshape(B, S, D_ATT)
    return o @ w_proj

def moe(x, router_w, router_b, w_gu, w_dn, ws_gu, ws_dn):
    B, S, D = x.shape
    nb = S // MOE_BLOCK
    xc = x.reshape(B, nb, MOE_BLOCK, D).swapaxes(0, 1).reshape(nb, B * MOE_BLOCK, D)

    def expert_block(xb):
        scores = jax.nn.sigmoid((xb @ router_w).astype(jnp.float32))
        _, sel = lax.top_k(scores + router_b.astype(jnp.float32), TOPK_EXPERTS)
        w = jnp.take_along_axis(scores, sel, axis=-1)
        w = w / jnp.sum(w, axis=-1, keepdims=True) * ROUTE_SCALE
        gates = jnp.sum(jax.nn.one_hot(sel, N_EXPERTS, dtype=jnp.float32) * w[..., None], axis=1)
        a, u = jnp.split(jnp.einsum('td,edf->tef', xb, w_gu), 2, axis=-1)
        h = jax.nn.silu(a) * u * gates[..., None].astype(xb.dtype)
        routed = jnp.einsum('tef,efd->td', h, w_dn)
        a_s, u_s = jnp.split(xb @ ws_gu, 2, axis=-1)
        return routed + (jax.nn.silu(a_s) * u_s) @ ws_dn

    y = lax.map(expert_block, xc)
    return y.reshape(nb, B, MOE_BLOCK, D).swapaxes(0, 1).reshape(B, S, D)

def setup_inputs(seed: int = 0) -> dict:
    key = jax.random.key(seed)
    ks = jax.random.split(key, 32)
    f32 = jnp.float32

    def nrm(k, shape, scale):
        return jax.random.normal(k, shape, f32) * scale

    L, D, B = DEPTH, D_MODEL, DEEPNORM_BETA
    return {
        "x": nrm(ks[0], (BATCH, SEQ, D), 1.0),
        "ln_in_g": 1.0 + nrm(ks[1], (D,), 0.05),
        "ln_in_b": nrm(ks[2], (D,), 0.02),
        "w_in": nrm(ks[3], (L, D, N_IN), D ** -0.5),
        "b_in": nrm(ks[4], (L, N_IN), 0.02),
        "conv_dw": nrm(ks[5], (L, CONV_WIDTH, D_CONV), CONV_WIDTH ** -0.5),
        "conv_b": nrm(ks[6], (L, D_CONV), 0.02),
        "conv_ln_g": 1.0 + nrm(ks[7], (L, D_CONV), 0.05),
        "conv_ln_b": nrm(ks[8], (L, D_CONV), 0.02),
        "w_conv_proj": nrm(ks[9], (L, D_CONV, D), B * D_CONV ** -0.5),
        "hgrn_gamma": nrm(ks[10], (L, D_RNN), 0.5),
        "hgrn_norm_g": 1.0 + nrm(ks[11], (L, D_RNN), 0.05),
        "w_rnn_proj": nrm(ks[12], (L, D_RNN, D), B * D_RNN ** -0.5),
        "kv_norm_g": 1.0 + nrm(ks[13], (L, D_LATENT), 0.05),
        "w_uv": nrm(ks[14], (L, N_ATT_HEADS, D_LATENT, ATT_HEAD_DIM), B * D_LATENT ** -0.5),
        "w_att_proj": nrm(ks[15], (L, D_ATT, D), B * D_ATT ** -0.5),
        "rel_bias": nrm(ks[16], (N_BUCKETS, N_ATT_HEADS), 0.5),
        "w_out": nrm(ks[17], (L, D, D), B * D ** -0.5),
        "ln_mix_g": 1.0 + nrm(ks[18], (L, D), 0.05),
        "ln_mix_b": nrm(ks[19], (L, D), 0.02),
        "router_w": nrm(ks[20], (L, D, N_EXPERTS), D ** -0.5),
        "router_b": nrm(ks[21], (L, N_EXPERTS), 0.01),
        "w_expert_gu": nrm(ks[22], (L, N_EXPERTS, D, 2 * D_EXPERT), D ** -0.5),
        "w_expert_dn": nrm(ks[23], (L, N_EXPERTS, D_EXPERT, D), B * D_EXPERT ** -0.5),
        "w_shared_gu": nrm(ks[24], (L, D, 2 * D_SHARED), D ** -0.5),
        "w_shared_dn": nrm(ks[25], (L, D_SHARED, D), B * D_SHARED ** -0.5),
        "ln_ffn_g": 1.0 + nrm(ks[26], (L, D), 0.05),
        "ln_ffn_b": nrm(ks[27], (L, D), 0.02),
    }

def reference(x, ln_in_g, ln_in_b, w_in, b_in, conv_dw, conv_b, conv_ln_g, conv_ln_b, w_conv_proj,
              hgrn_gamma, hgrn_norm_g, w_rnn_proj, kv_norm_g, w_uv, w_att_proj, rel_bias, w_out,
              ln_mix_g, ln_mix_b, router_w, router_b, w_expert_gu, w_expert_dn, w_shared_gu,
              w_shared_dn, ln_ffn_g, ln_ffn_b):
    Bsz, S, D = x.shape
    split_points = [int(p) for p in np.cumsum(SPLITS)[:-1]]
    lb_all = jnp.cumsum(jax.nn.softmax(hgrn_gamma.astype(jnp.float32), axis=0), axis=0)
    lb_all = lb_all - lb_all[0]

    h = layer_norm(x, ln_in_g, ln_in_b)
    for l in range(DEPTH):
        proj = h @ w_in[l] + b_in[l]
        (conv_in, r_q, r_f, r_i, r_g, a_q, a_c, i_q, i_k, i_w, gate_in) = jnp.split(proj, split_points, axis=-1)
        y_conv = conformer_conv(conv_in, conv_dw[l], conv_b[l], conv_ln_g[l], conv_ln_b[l], w_conv_proj[l])
        y_rnn = hgrn2(r_q, r_f, r_i, r_g, lb_all[l], hgrn_norm_g[l], w_rnn_proj[l], h.dtype)
        y_att = dsa_attention(a_q, a_c, i_q, i_k, i_w, kv_norm_g[l], w_uv[l], rel_bias,
                              w_att_proj[l], h.dtype)
        g = jax.nn.sigmoid(gate_in).reshape(Bsz, S, N_BRANCH, D)
        merged = g[:, :, 0] * y_conv + g[:, :, 1] * y_rnn + g[:, :, 2] * y_att
        h = layer_norm(DEEPNORM_ALPHA * h + merged @ w_out[l], ln_mix_g[l], ln_mix_b[l])
        y_ffn = moe(h, router_w[l], router_b[l], w_expert_gu[l], w_expert_dn[l],
                    w_shared_gu[l], w_shared_dn[l])
        h = layer_norm(DEEPNORM_ALPHA * h + y_ffn, ln_ffn_g[l], ln_ffn_b[l])
    return h


_drawn_inputs = setup_inputs


def setup_inputs(seed=0):
    import zlib

    import numpy as np

    out = dict(_drawn_inputs(seed))
    spreads = {}
    factors = {'conv_b': 2.786,
     'conv_ln_b': 5.554,
     'hgrn_norm_g': 3.3,
     'kv_norm_g': 8.0,
     'ln_ffn_b': 3.12}
    for name, (base, spread) in spreads.items():
        noise = np.random.default_rng([zlib.crc32(name.encode()), seed]).standard_normal(out[name].shape)
        drawn = base * np.exp(spread * noise) if base else spread * noise
        out[name] = __import__('jax').numpy.asarray(drawn.astype(out[name].dtype))
    for name, factor in factors.items():
        out[name] = (out[name] * factor).astype(out[name].dtype)
    return out
```

```python
import math
from contextlib import ExitStack

import concourse.bass as bass
from concourse import mybir

F32 = mybir.dt.float32
BF16 = mybir.dt.bfloat16
U32 = mybir.dt.uint32
I32 = mybir.dt.int32
U8 = mybir.dt.uint8
ALU = mybir.AluOpType
ACT = mybir.ActivationFunctionType
AX = mybir.AxisListType

P = 128
D = 1024
SEQ = 256
TB = SEQ // P
KD = D // P
D_CONV = 512
TAPS = 31
NH_R = 4
NH_A = 8
NH_I = 4
D_IDX = 64
TOPK = 64
NBUCKET = 32
NDIST = 384
NE = 32
TOPE = 4
F_E = 256
ROUTE_SCALE = 2.5
ALPHA = 2.0 ** 0.25
EPS = 1e-5
CAP = 64
NPAIR = NE // 2
COL_RQ, COL_RF, COL_RI, COL_RG = 1024, 1536, 2048, 2560
COL_AQ, COL_IDX, COL_GATE = 3072, 4096, 4548
N_IDX_COLS = COL_GATE - COL_IDX
WSLOTS = 6
SLOT = 4096
BANNED = -3.0e38
TAKEN = -3.4e38
OFF = -1.0e30
TINY = 2.0 ** -60
POOL_F = 22912
HALVES = [1, 2, 4, 8, 16, 32, 64]


def build(nc, x, ln_in_g, ln_in_b, w_in, b_in, conv_dw, conv_b, conv_ln_g, conv_ln_b, w_conv_proj,
          hgrn_gamma, hgrn_norm_g, w_rnn_proj, kv_norm_g, w_uv, w_att_proj, rel_bias, w_out,
          ln_mix_g, ln_mix_b, router_w, router_b, w_expert_gu, w_expert_dn, w_shared_gu,
          w_shared_dn, ln_ffn_g, ln_ffn_b, c_f32, c_level, c_onehot, out):
    h2_rows = nc.dram_tensor("h2_rows", (SEQ, D), F32, kind="Internal").ap()
    ye_rows = nc.dram_tensor("ye_rows", (NE * CAP, D), F32, kind="Internal").ap()
    bias_by_dist = nc.dram_tensor("bias_by_dist", (NH_A, NDIST), F32, kind="Internal")
    bias_ap = bias_by_dist.ap()

    ctx = ExitStack()
    with ctx:
        def sb(name, shape, dt=F32):
            return ctx.enter_context(nc.sbuf_tensor(name, shape, dt))

        def sem(name):
            return ctx.enter_context(nc.semaphore(name))

        ring = sb("ring", [P, WSLOTS, SLOT])
        h = sb("h", [P, TB, D])
        hT = sb("hT", [P, KD, SEQ])
        consts = sb("consts", [P, 7, P])
        level_mask = sb("level_mask", [P, 8, P], U8)
        params = sb("params", [P, P])
        stats = sb("stats", [P, 4, 6])
        mv = sb("mv", [P, 4, 2])
        rstd = sb("rstd", [P, 4])
        small = sb("small", [P, 64])
        ident, ones, before, can, never, mean_w, mean_o = (consts[:, i, :] for i in range(7))

        pool = sb("pool", [P, POOL_F])
        used = [0]

        def part(n):
            used[0] += n
            assert used[0] <= POOL_F, used
            return pool[:, used[0] - n:used[0]]

        gb_conv = part(2 * D + 160)
        gb = gb_conv[:, 0:2 * D].rearrange("p (a d) -> p a d", a=2)
        UW = SEQ + TAPS - 1
        u_pad = gb_conv[:, 0:4 * UW].rearrange("p (c t) -> p c t", c=4)
        conv = gb_conv[:, 4 * UW:4 * UW + 1024].rearrange("p (c t) -> p c t", c=4)
        cvs = gb_conv[:, 0:1024]
        conv_sq = cvs.rearrange("p (c t) -> p c t", c=4)
        aq_merged = part(2048)
        aqT = aq_merged.rearrange("p (h t) -> p h t", h=NH_A)
        merged = aq_merged.rearrange("p (m t) -> p m t", m=KD)
        c_tok_major = part(256).rearrange("p (b c) -> p b c", b=TB)
        cT = part(256)
        qi_wuv = part(512)
        qiT = qi_wuv.rearrange("p (a t) -> p a t", a=2)
        wuv = qi_wuv.rearrange("p (h v) -> p h v", h=NH_A)
        kiT = part(256)
        sel_add = part(512).rearrange("p (b s) -> p b s", b=TB)
        r1 = part(6144)
        logits1 = r1[:, 0:2048].rearrange("p (h s) -> p h s", h=NH_A)
        relu_i = r1[:, 0:1024].rearrange("p (h s) -> p h s", h=NH_I)
        oT_att = r1[:, 0:2048].rearrange("p (h t) -> p h t", h=NH_A)
        logits0 = r1[:, 2048:3072].rearrange("p (h s) -> p h s", h=NH_A)
        score = r1[:, 2048:2304]
        probsT = r1[:, 3072:6144].rearrange("p (b h t) -> p b h t", b=3, h=NH_A)
        Xl = [r1[:, 2048 * i:2048 * i + 1024] for i in range(2)]
        Yl = [r1[:, 2048 * i + 1024:2048 * i + 2048] for i in range(2)]
        inter = r1[:, 4096:4608].rearrange("p (h t) -> p h t", h=NH_R)
        aT = r1[:, 5120:6144].rearrange("p (c t) -> p c t", c=4)
        t_region = part(2048)
        dist_bias = t_region.rearrange("p (h s) -> p h s", h=NH_A)
        inner = t_region[:, 0:1024].rearrange("p (h c t) -> p h c t", h=NH_R, c=2)
        oT_rnn = t_region[:, 1024:2048].rearrange("p (h t) -> p h t", h=NH_R)
        fz, cum, ls, kT, qT, sgT = (part(1024) for _ in range(6))
        v_tok = part(1024).rearrange("p (b n) -> p b n", b=TB)
        gate_tmp = part(512).rearrange("p (a t) -> p a t", a=2)
        ri_bias = part(512)
        row_bias = part(132)
        kvg = part(128)
        wi = part(8).rearrange("p (b h) -> p b h", b=TB)
        dw = part(4 * TAPS).rearrange("p (c k) -> p c k", c=4)

        def hd(t, i):
            return t[:, i * SEQ:(i + 1) * SEQ]

        e_mem = pool[:, 2208:]
        acc = e_mem[:, 0:2048].rearrange("p (b d) -> p b d", b=TB)
        xg = [e_mem[:, 2048 + 1024 * i:3072 + 1024 * i] for i in range(2)]
        xT = e_mem[:, 4096:5120].rearrange("p (k s) -> p k s", k=KD)
        yo = [e_mem[:, 5120 + 1024 * i:6144 + 1024 * i] for i in range(2)]
        G = [e_mem[:, 7168 + 1024 * i:8192 + 1024 * i] for i in range(4)]
        hid = [e_mem[:, 11264 + 256 * i:11520 + 256 * i].rearrange("p (e f s) -> p e f s", e=2, f=2)
               for i in range(2)]
        silu_e = [e_mem[:, 11776 + 256 * i:12032 + 256 * i].rearrange("p (e f s) -> p e f s", e=2, f=2)
                  for i in range(2)]
        hid_s = e_mem[:, 12288:12800].rearrange("p (f t) -> p f t", f=2)
        silu_s = e_mem[:, 12800:13312].rearrange("p (f t) -> p f t", f=2)
        slot_of = e_mem[:, 13312:15360].bitcast(BF16).rearrange("p (b e c) -> p b e c", b=TB, e=NE)
        rw = e_mem[:, 15360:15616].rearrange("p (k e) -> p k e", k=KD)
        m_small = e_mem[:, 15616:18688]
        off = [0]

        def mpart(*shape):
            n = math.prod(shape)
            off[0] += n
            v = m_small[:, off[0] - n:off[0]]
            if len(shape) == 2:
                return v.rearrange("p (a b) -> p a b", a=shape[0])
            if len(shape) == 3:
                return v.rearrange("p (a b c) -> p a b c", a=shape[0], b=shape[1])
            return v
        scores = mpart(TB, NE)
        biased = mpart(TB, NE)
        top8 = mpart(TB, 8)
        idx8f = mpart(TB, 8)
        onehot = mpart(TB * TOPE, NE)
        oh4 = onehot.rearrange("p (b j) e -> p b j e", b=TB)
        prod = mpart(TB * TOPE, NE)
        prod4 = prod.rearrange("p (b j) e -> p b j e", b=TB)
        sel = mpart(TB, NE)
        rank = mpart(TB, NE)
        rank_in = mpart(TB, NE)
        wj = mpart(TB, TOPE)
        gate = mpart(TB, TOPE)
        gate_main = mpart(TB, TOPE)
        gate_over = mpart(TB, TOPE)
        rank_j = mpart(TB, TOPE)
        fits = mpart(TB, TOPE)
        row_f = mpart(TB, TOPE)
        wsum = mpart(TB)
        g_over = mpart(TB, NE)
        iota_e = mpart(NE)
        iota_c = mpart(CAP)
        rb = mpart(NE)
        cmax = mpart(1)
        idx8 = sb("idx8", [P, TB, 8], U32)
        row_of = sb("row_of", [P, TB * TOPE], U32)
        ids = sb("ids", [P, NPAIR], U32)
        tok_id = sb("tok_id", [P, TB], BF16)
        count = sb("count", [1, 1], I32)

        ps = ctx.enter_context(nc.psum_tensor("ps", [P, 8, 512], F32))

        def banks(a, n=1):
            return ps[:, a:a + n, :].rearrange("p b n -> p (b n)")

        s_x = sem("x_loaded"); s_gb = sem("ln_in_params_loaded"); s_par = sem("small_params_loaded")
        s_con = sem("consts_loaded"); s_tok = sem("tok_id_ready")
        s_w = [sem(f"weights_in_slot{i}") for i in range(WSLOTS)]
        s_h = sem("h_ready"); s_hTp = sem("hT_in_psum"); s_hT = sem("hT_ready")
        s_prT = sem("params_in_psum"); s_pr = sem("params_ready")
        s_pin = sem("power_base_ready"); s_pout = sem("power_ready")
        s_bd = sem("bias_by_dist_ready"); s_bdd = sem("bias_by_dist_in_dram"); s_T = sem("dist_bias_loaded"); s_uvl = sem("value_weights_loaded")
        s_turn = sem("turn_done")
        s_free = [sem("bank0_free"), sem("bank1_free")]
        s_sig = sem("sigmoid_ready")
        s_cr = sem("c_ready"); s_cTp = sem("cT_in_psum"); s_cT = sem("cT_ready")
        s_qk = sem("indexer_qk_ready"); s_sc = sem("indexer_products_ready"); s_relu = sem("relu_ready")
        s_reluf = sem("relu_used")
        s_upad = sem("u_pad_ready"); s_u = sem("conv_input_ready")
        s_conv = sem("conv_ready"); s_mean = sem("conv_mean_ready"); s_sqr = sem("conv_squares_ready")
        s_cen = sem("conv_centred"); s_var = sem("conv_var_ready"); s_cn = sem("conv_normed")
        s_cT2 = sem("conv_silu_ready")
        s_aq = sem("att_q_ready"); s_lg = sem("logits_ready"); s_la = sem("logits_biased")
        s_ex = sem("exp_ready"); s_pn = sem("probs_ready"); s_pTp = sem("probsT_in_psum")
        s_pT = sem("probsT_ready"); s_oTp = sem("att_oT_in_psum"); s_oT = sem("att_oT_ready")
        s_uvp = sem("att_values_in_psum"); s_aT = sem("att_values_ready")
        s_rf = sem("forget_ready"); s_hp = sem("hgrn_prep_vector"); s_ha = sem("hgrn_prep_scalar")
        s_lbv = sem("lower_bound_vector"); s_lba = sem("lower_bound_scalar")
        s_rq = sem("rnn_q_ready"); s_rv = sem("rnn_v_ready"); s_rg = sem("rnn_gate_ready")
        s_dl = sem("level_diff_ready"); s_el = sem("level_decay_ready"); s_xy = sem("level_xy_ready")
        s_pl = sem("level_products_ready"); s_pc = sem("level_products_taken")
        s_on = sem("rnn_o_in_psum"); s_osq = sem("rnn_o_squares_ready"); s_ms = sem("rnn_ms_ready")
        s_ot = sem("rnn_oT_ready")
        s_mg = sem("merged_ready"); s_rs = sem("mix_residual_ready")
        s_gb2 = sem("ln_mix_params_loaded"); s_gb3 = sem("ln_ffn_params_loaded")
        s_h2 = sem("h2_ready"); s_h2d = sem("h2_in_dram"); s_h2Tp = sem("h2T_in_psum"); s_h2T = sem("h2T_ready")
        s_ro = sem("router_loaded"); s_rl = sem("router_logits_ready"); s_rsg = sem("router_scores_ready")
        s_sel = sem("selection_ready"); s_rk = sem("ranks_ready"); s_so = sem("slot_map_ready")
        s_idp = sem("ids_in_psum"); s_ids = sem("ids_ready"); s_rows = sem("rows_ready")
        s_cnt = sem("count_ready")
        s_sgu = sem("shared_up_ready"); s_ssl = sem("shared_silu_ready"); s_sh = sem("shared_hidden_ready")
        s_sdn = sem("shared_down_ready"); s_acc = sem("shared_added")
        s_xg = [sem("tokens_gathered0"), sem("tokens_gathered1")]
        s_xp = sem("xT_in_psum"); s_xc = sem("xT_ready"); s_gu = sem("expert_up_ready")
        s_sl = sem("expert_silu_ready"); s_hid = [sem("expert_hidden0"), sem("expert_hidden1")]
        s_dn = sem("expert_down_ready"); s_yo = [sem("expert_out0"), sem("expert_out1")]
        s_st = [sem("expert_rows_stored0"), sem("expert_rows_stored1")]
        s_G = [sem(f"choice_rows_gathered{i}") for i in range(4)]
        s_Gu = sem("choice_rows_used")
        o_w = sem("over_weights_loaded"); o_up = sem("over_up_ready"); o_sl = sem("over_silu_ready")
        o_h = sem("over_hidden_ready"); o_dn = sem("over_down_ready"); o_acc = sem("over_added")
        s_y = sem("out_ready"); s_out = sem("out_stored")
        q_v = sem("vector_order"); q_a = sem("scalar_order"); q_g = sem("gpsimd_order")

        def strip(w, c0, n=512):
            return w[:, c0:c0 + n].rearrange("(k p) n -> p k n", p=P)

        w_in2 = w_in[0]
        stream = [(strip(w_in2, COL_IDX, N_IDX_COLS), KD, N_IDX_COLS)]
        free_at = [3]
        for c0, last in ((0, 7), (512, 7), (COL_AQ, 9), (COL_AQ + 512, 11), (COL_RF, 13), (COL_RQ, 15),
                         (COL_RI, 17), (COL_RG, 19)):
            stream.append((strip(w_in2, c0), KD, 512))
            free_at.append(last)
        BRANCH = [(2, w_att_proj), (0, w_conv_proj), (1, w_rnn_proj)]
        T_BR = [19, 27, 35]
        for (g, w), t0 in zip(BRANCH, T_BR):
            stream.append((w[0].rearrange("(k p) n -> p k n", p=P), 4, D))
            free_at.append(t0 + 8)
            for half in range(2):
                stream.append((strip(w_in2, COL_GATE + g * D + half * 512), KD, 512))
                free_at.append(t0 + 4 * half + 4)
        I_BR = [9, 12, 15]
        I_OUT = 18
        T_OUT = 43
        for half in range(2):
            stream.append((strip(w_out[0], half * 512), KD, 512))
            free_at.append(T_OUT + 2 * half + 2)
        I_SGU, I_SDN = 20, 21
        stream.append((strip(w_shared_gu[0], 0), KD, 512))
        stream.append((w_shared_dn[0].rearrange("(k p) n -> p k n", p=P), 2, D))
        T_SH = T_OUT + 4
        free_at += [T_SH + 2, T_SH + 6]
        N0 = len(stream)
        assert N0 == 22

        def slot(n, k, w):
            return ring[:, n % WSLOTS, 0:k * w].rearrange("p (k n) -> p k n", k=k)

        def arrived(eng, n):
            eng.wait_ge(s_w[n % WSLOTS], 16 * (n // WSLOTS + 1))

        def pair_item(i, q, j):
            n = N0 + 3 * q + j
            return n % WSLOTS, (i + (n // WSLOTS + 1)) * 16

        gu_d = w_expert_gu[0].rearrange("e (k p) n -> e p k n", p=P)
        dn_d = w_expert_dn[0].rearrange("e (f p) n -> e p f n", p=P)
        COUNT_MAX = SEQ

        def over(eng):
            eng.wait_ge(s_cnt, 1)
            return eng.value_load(count[0:1, 0:1], min_val=0, max_val=COUNT_MAX) > CAP

        prow = fz[:, 0:P]
        dw_rows = fz[:, P:P + 512]
        bdist = ls[:, 0:NDIST]
        buckets = ls[:, NDIST:2 * NDIST]
        relb = ls[:, 2 * NDIST:2 * NDIST + NH_A]
        B_RQ, B_RF, B_RG, B_AQ = COL_RQ // P, COL_RF // P, COL_RG // P, COL_AQ // P
        B_GATE, B_CB, B_CG, B_CLB, B_GAM, B_NG, B_QI, B_KI = 32, 56, 60, 64, 68, 72, 76, 78

        def col(i):
            return params[:, i:i + 1]

        lb_a, lb_ln = small[:, 0:4], small[:, 4:8]
        lb = small[:, 8:12]
        minus_half = small[:, 56:57]
        ssq, crs = small[:, 12:14], small[:, 14:16]
        m8 = small[:, 16:24]
        nmax = small[:, 24:40]
        esum = small[:, 40:56]

        def after_first(eng, s, value, i):
            if not (isinstance(i, int) and i == 0):
                eng.wait_ge(s, value)

        block = ctx.enter_context(nc.Block())

        @block.sync
        def _(sp):
            for n, (src, k, w) in enumerate(stream):
                if n >= WSLOTS:
                    sp.wait_ge(s_turn, free_at[n - WSLOTS])
                sp.dma_start(slot(n, k, w), src).then_inc(s_w[n % WSLOTS], 16)

            def load_pair(i, q):
                for j in range(3):
                    s, _ = pair_item(0, q, j)
                    if isinstance(i, int) and i == 0:
                        n = N0 + 3 * q + j
                        sp.wait_ge(s_turn, free_at[n - WSLOTS])
                    else:
                        sp.wait_ge(s_dn if j == 2 else s_gu, i * 2 + (q - 1))
                    if j < 2:
                        src = gu_d[i * 4 + (2 * q + j)]
                        sp.dma_start(ring[:, s, :].rearrange("p (k n) -> p k n", k=KD),
                                     src).then_inc(s_w[s], 16)
                    else:
                        src = dn_d[bass.ds(i * 4 + 2 * q, 2)].rearrange("e p f n -> p e f n") \
                            if not isinstance(i, int) else dn_d[4 * i + 2 * q:4 * i + 2 * q + 2].rearrange("e p f n -> p e f n")
                        sp.dma_start(ring[:, s, :].rearrange("p (e f n) -> p e f n", e=2, f=2),
                                     src).then_inc(s_w[s], 16)

            for q in range(2):
                load_pair(0, q)
            with sp.Fori(1, NPAIR // 2) as i:
                for q in range(2):
                    load_pair(i, q)
            with sp.If(over(sp)):
                sp.wait_ge(s_dn, NPAIR)

                def load(e):
                    after_first(sp, o_dn, e, e)
                    sp.dma_start(ring[:, 0, :].rearrange("p (k n) -> p k n", k=KD), gu_d[e]).then_inc(o_w, 16)
                    sp.dma_start(ring[:, 1, 0:2 * D].rearrange("p (f n) -> p f n", f=2), dn_d[e]).then_inc(o_w, 16)

                load(0)
                with sp.Fori(1, NE) as e:
                    load(e)
            for b in range(TB):
                sp.wait_ge(s_y, b + 1)
                sp.dma_start(out[0, b * P:(b + 1) * P, :], h[:, b, :]).then_inc(s_out, 16)
            sp.wait_ge(s_out, 16 * TB)

        @block.gpsimd
        def _(pool_e):
            def rows(ap, n):
                return ap.rearrange("(a n) -> a n", a=1).to_broadcast((P, n))

            powers = [0]

            def power(t):
                powers[0] += 1
                pool_e.wait_ge(s_pin, powers[0])
                pool_e.tensor_tensor(t, t, minus_half.to_broadcast((P, t.shape[1])), ALU.pow).then_inc(s_pout, 1)

            pool_e.dma_start(prow[0:32, :], b_in[0, 0:4096].rearrange("(m p) -> m p", p=P)).then_inc(s_par, 16)
            pool_e.dma_start(prow[32:56, :], b_in[0, COL_GATE:COL_GATE + 3072].rearrange("(m p) -> m p", p=P)).then_inc(s_par, 16)
            for r, a in ((56, conv_b), (60, conv_ln_g), (64, conv_ln_b), (68, hgrn_gamma), (72, hgrn_norm_g)):
                pool_e.dma_start(prow[r:r + 4, :], a[0].rearrange("(m p) -> m p", p=P)).then_inc(s_par, 16)
            pool_e.dma_start(prow[76:78, :], b_in[0, COL_IDX + 128:COL_IDX + 384].rearrange("(m p) -> m p", p=P)).then_inc(s_par, 16)
            for z in range(2):
                pool_e.dma_start(prow[78:79, 64 * z:64 * z + 64],
                                 b_in[0, COL_IDX + 384:COL_IDX + 448].rearrange("(m p) -> m p", p=64)).then_inc(s_par, 16)
            pool_e.dma_start(dw_rows[0:TAPS, :], conv_dw[0]).then_inc(s_par, 16)
            pool_e.dma_start(relb[0:NBUCKET, :], rel_bias).then_inc(s_par, 16)
            pool_e.dma_start(buckets[0:NBUCKET, :], c_onehot).then_inc(s_par, 16)
            pool_e.dma_start(row_bias[:, 0:128], rows(b_in[0, COL_IDX:COL_IDX + 128], 128)).then_inc(s_par, 16)
            pool_e.dma_start(row_bias[:, 128:132], rows(b_in[0, COL_GATE - 4:COL_GATE], 4)).then_inc(s_par, 16)
            pool_e.dma_start(ri_bias, rows(b_in[0, COL_RI:COL_RI + 512], 512)).then_inc(s_par, 16)
            pool_e.dma_start(kvg, rows(kv_norm_g[0], 128)).then_inc(s_par, 16)
            pool_e.iota(tok_id[:, :], [[P, TB]], base=0, channel_multiplier=1,
                        allow_small_or_imprecise_dtypes=True).then_inc(s_tok, 1)
            pool_e.memset(minus_half, -0.5).then_inc(q_g, 1)
            pool_e.wait_ge(q_g, 1)
            pool_e.wait_ge(s_con, 32)
            pool_e.tensor_copy(level_mask[:, :, :].rearrange("p n t -> p (n t)"), kT).then_inc(q_g, 1)
            for b in range(TB):
                power(rstd[:, b:b + 1])
            pool_e.wait_ge(s_bd, 1)
            pool_e.dma_start(bias_ap, bdist[0:NH_A, :]).then_inc(s_bdd, 16)
            pool_e.wait_ge(s_bdd, 16)
            pool_e.dma_start(dist_bias, bass.AP(bias_by_dist, 0, [[1, P], [NDIST, NH_A], [1, SEQ]])).then_inc(s_T, 16)

            power(crs)
            pool_e.wait_ge(s_relu, 2)
            pool_e.dma_start(wuv, w_uv[0].rearrange("h c v -> c h v")).then_inc(s_uvl, 16)
            power(cvs[:, 0:SEQ])
            power(ls)
            pool_e.wait_ge(s_turn, T_BR[1] + KD)
            for i, a in enumerate((ln_mix_g, ln_mix_b)):
                pool_e.dma_start(gb[:, i, :], rows(a[0], D)).then_inc(s_gb2, 16)

            pool_e.wait_ge(s_rs, 4)
            pool_e.dma_start(rw, router_w[0].rearrange("(k p) e -> p k e", p=P)).then_inc(s_ro, 16)
            pool_e.dma_start(rb, rows(router_b[0], NE)).then_inc(s_ro, 16)
            pool_e.iota(iota_e, [[1, NE]], base=0, channel_multiplier=0,
                        allow_small_or_imprecise_dtypes=True).then_inc(q_g, 1)
            pool_e.iota(iota_c, [[1, CAP]], base=0, channel_multiplier=0,
                        allow_small_or_imprecise_dtypes=True).then_inc(q_g, 1)
            for b in range(TB):
                power(rstd[:, b:b + 1])
                pool_e.wait_ge(s_h2, b + 1)
                pool_e.dma_start(h2_rows[b * P:(b + 1) * P, :], h[:, b, :]).then_inc(s_h2d, 16)
            for i, a in enumerate((ln_ffn_g, ln_ffn_b)):
                pool_e.dma_start(gb[:, i, :], rows(a[0], D)).then_inc(s_gb3, 16)
            pool_e.wait_ge(s_h2d, 16 * TB)
            pool_e.wait_ge(s_ids, 1)
            for p in range(NPAIR):
                if p >= 2:
                    pool_e.wait_ge(s_xp, p - 1)
                pool_e.indirect_dma_start(
                    out=xg[p % 2], out_offset=None, in_=h2_rows,
                    in_offset=bass.IndirectOffsetOnAxis(ap=ids[:, p:p + 1], axis=0)).then_inc(s_xg[p % 2], 16)
            for q in range(2):
                pool_e.wait_ge(s_st[q], 16 * NPAIR // 2)
            pool_e.wait_ge(s_rows, 1)
            for n in range(TB * TOPE):
                if n >= 4:
                    pool_e.wait_ge(s_Gu, n - 3)
                pool_e.indirect_dma_start(
                    out=G[n % 4], out_offset=None, in_=ye_rows,
                    in_offset=bass.IndirectOffsetOnAxis(ap=row_of[:, n:n + 1], axis=0)).then_inc(s_G[n % 4], 16)
            for b in range(TB):
                power(rstd[:, b:b + 1])

        @block.scalar
        def _(act):
            q = [0]

            def link(ins):
                q[0] += 1
                ins.then_inc(q_a, 1)
                act.wait_ge(q_a, q[0])

            for b in range(TB):
                act.dma_start(h[:, b, :], x[0, b * P:(b + 1) * P, :]).then_inc(s_x, 16)
            for i, a in enumerate((ln_in_g, ln_in_b)):
                act.dma_start(gb[:, i, :], a.rearrange("(a n) -> a n", a=1).to_broadcast((P, D))).then_inc(s_gb, 16)
            act.dma_start(consts[:, :, :], c_f32).then_inc(s_con, 16)
            act.dma_start(kT.rearrange("p (n t) -> p n t", n=8), c_level).then_inc(s_con, 16)

            for i in range(2):
                act.wait_ge(s_hTp, 2 * i + 1)
                nc.scalar.copy(hT[:, 4 * i:4 * i + 2, :].rearrange("p k t -> p (k t)"), banks(2 + 2 * i)).then_inc(s_hT, 1)
            act.wait_ge(s_prT, 1)
            nc.scalar.copy(params[:, 0:79], banks(6)[:, 0:79]).then_inc(s_pr, 1)
            nc.scalar.copy(dw.rearrange("p c k -> p (c k)"), banks(7)[:, 0:4 * TAPS]).then_inc(s_pr, 1)
            nc.scalar.copy(bdist[0:NH_A, :], banks(6)[0:NH_A, 128:512]).then_inc(s_bd, 1)
            act.wait_ge(s_pr, 2)

            def evac(t, outs, sem_out):
                act.wait_ge(s_turn, t + 1)
                for n, (dst, bias) in enumerate(outs):
                    ins = nc.scalar.activation(dst, banks(t % 2)[:, n * SEQ:(n + 1) * SEQ], ACT.Identity, bias=bias)
                    ins.then_inc(sem_out, 1)
                done[sem_out] = done.get(sem_out, 0) + len(outs)
                act.wait_ge(sem_out, done[sem_out])
                act.sem_inc(s_free[t % 2], 1)

            done = {}

            evac(1, [(qiT[:, 0, :], col(B_QI)), (qiT[:, 1, :], col(B_QI + 1))], s_qk)
            evac(2, [(kiT, col(B_KI))], s_qk)
            def conv_gate(c):
                t = 3 + c
                act.wait_ge(s_turn, t + 1)
                if c >= 2:
                    act.wait_ge(s_u, c - 1)
                nc.scalar.activation(gate_tmp[:, c % 2, :], banks(t % 2)[:, SEQ:2 * SEQ], ACT.Sigmoid,
                                     bias=col(4 + c)).then_inc(s_sig, 1)

            conv_gate(0)
            act.wait_ge(s_cTp, 1)
            nc.scalar.copy(cT, banks(5)[:, 0:SEQ]).then_inc(s_cT, 1)
            conv_gate(1)
            act.wait_ge(s_sc, 1)
            nc.scalar.activation(relu_i[:, :, 0:P].rearrange("p (y z) s -> p y z s", y=2),
                                 ps[:, 2:4, 0:2 * P].rearrange("p y (z s) -> p y z s", z=2),
                                 ACT.Relu).then_inc(s_relu, 1)
            conv_gate(2)
            act.wait_ge(s_sc, 2)
            act.wait_ge(s_reluf, 1)
            nc.scalar.activation(relu_i, banks(4, 2).rearrange("p (h s) -> p h s", h=NH_I),
                                 ACT.Relu).then_inc(s_relu, 1)
            conv_gate(3)
            for i in range(4):
                evac(7 + i, [(aqT[:, 2 * i + z, :], col(B_AQ + 2 * i + z)) for z in range(2)], s_aq)
            act.wait_ge(s_lbv, 1)
            nc.scalar.activation(lb, lb, ACT.Exp).then_inc(s_lba, 1)
            act.wait_ge(s_lbv, 2)
            nc.scalar.activation(lb_a, lb_a, ACT.Ln)
            link(nc.scalar.activation(lb_ln, lb, ACT.Ln, bias=1.0, scale=-1.0))
            act.sem_inc(s_lba, 1)
            act.wait_ge(s_bdd, 16)
            for i in range(2):
                evac(11 + i, [(hd(fz, 2 * i + z), col(B_RF + 2 * i + z)) for z in range(2)], s_rf)
            def exps(b):
                lg, w = (logits0, P) if b == 0 else (logits1, SEQ)
                act.wait_ge(s_la, b + 1)
                for hh in range(NH_A):
                    ins = nc.scalar.activation(lg[:, hh, :], lg[:, hh, :], ACT.Exp, bias=nmax[:, 8 * b + hh:8 * b + hh + 1],
                                               accum_out=esum[:, 8 * b + hh:8 * b + hh + 1])
                ins.then_inc(s_ex, 1)

            exps(0)
            exps(1)
            act.wait_ge(s_hp, 1)
            link(nc.scalar.activation(cum, cum, ACT.Exp))
            nc.scalar.activation(cum, cum, ACT.Ln, bias=1.0).then_inc(s_ha, 1)
            evac(13, [(hd(qT, z), col(B_RQ + z)) for z in range(2)], s_rq)
            act.wait_ge(s_hp, 2)
            act.wait_ge(q_g, 2)
            for i in range(4):
                ins = nc.scalar.activation(hd(kT, i), hd(cum, i), ACT.Exp, bias=lb_ln[:, i:i + 1])
            ins.then_inc(s_ha, 1)
            act.wait_ge(s_hp, 3)
            link(nc.scalar.activation(fz, fz, ACT.Exp))
            nc.scalar.activation(fz, fz, ACT.Ln, bias=1.0).then_inc(s_ha, 1)
            evac(14, [(hd(qT, 2 + z), col(B_RQ + 2 + z)) for z in range(2)], s_rq)

            for n, bk in enumerate((2, 6, 2)):
                act.wait_ge(s_pTp, n + 1)
                nc.scalar.copy(probsT[:, n].rearrange("p h t -> p (h t)"), banks(bk, 2)).then_inc(s_pT, 1)
            for b in range(TB):
                act.wait_ge(s_oTp, b + 1)
                for half in range(2):
                    ins = nc.scalar.copy(oT_att[:, 4 * half:4 * half + 4, b * P:(b + 1) * P],
                                         banks(4 + half).rearrange("p (h t) -> p h t", h=4))
                ins.then_inc(s_oT, 1)
            for i in range(2):
                t = 17 + i
                act.wait_ge(s_turn, t + 1)
                for z in range(2):
                    ins = nc.scalar.activation(hd(sgT, 2 * i + z), banks(t % 2)[:, z * SEQ:(z + 1) * SEQ], ACT.Sigmoid,
                                               bias=col(B_RG + 2 * i + z))
                    ins.then_inc(s_rg, 1)
                act.wait_ge(s_rg, 2 * i + 2)
                act.sem_inc(s_free[t % 2], 1)
            act.wait_ge(s_uvp, 1)
            nc.scalar.copy(aT.rearrange("p c t -> p (c t)"), banks(6, 2)).then_inc(s_aT, 1)

            def branch_gate(br, m):
                t = T_BR[br] + m
                n = 8 * br + m
                act.wait_ge(s_turn, t + 1)
                if n >= 2:
                    act.wait_ge(s_mg, n - 1)
                else:
                    act.wait_ge(s_u, 3 + n)
                nc.scalar.activation(gate_tmp[:, n % 2, :], banks(t % 2)[:, 0:SEQ], ACT.Sigmoid,
                                     bias=col(B_GATE + 8 * BRANCH[br][0] + m)).then_inc(s_sig, 1)

            def decay(lv):
                act.wait_ge(s_dl, lv + 1)
                e = (fz, ls)[lv % 2]
                nc.scalar.activation(e, e, ACT.Exp).then_inc(s_el, 1)

            for m in range(KD):
                branch_gate(0, m)
                decay(m)
                if m == 5:
                    act.wait_ge(s_cn, 1)
                    for c in range(4):
                        ins = nc.scalar.activation(conv[:, c, :], conv[:, c, :], ACT.Silu, bias=col(B_CLB + c), scale=col(B_CG + c))
                    ins.then_inc(s_cT2, 1)
            for m in range(KD):
                branch_gate(1, m)
                if m == 2:
                    act.wait_ge(s_on, 1)
                    nc.scalar.activation(fz, banks(6, 2), ACT.Square).then_inc(s_osq, 1)
            for m in range(KD):
                branch_gate(2, m)

            for i in range(2):
                act.wait_ge(s_h2Tp, 2 * i + 1)
                nc.scalar.copy(hT[:, 4 * i:4 * i + 2, :].rearrange("p k t -> p (k t)"), banks(2 + 2 * i)).then_inc(s_h2T, 1)
            act.wait_ge(s_rl, 1)
            nc.scalar.activation(scores.rearrange("p b e -> p (b e)"), banks(6)[:, 0:2 * NE], ACT.Sigmoid).then_inc(s_rsg, 1)
            act.wait_ge(s_turn, T_SH + 1)
            nc.scalar.activation(silu_s.rearrange("p f t -> p (f t)"), banks(T_SH % 2), ACT.Silu).then_inc(s_ssl, 1)
            act.wait_ge(s_ssl, 1)
            act.sem_inc(s_free[T_SH % 2], 1)
            act.wait_ge(s_xp, 1)
            nc.scalar.copy(xT.rearrange("p k s -> p (k s)"), banks(0, 2)).then_inc(s_xc, 1)

            def pair(i, qq, last=False):
                p = i * 2 + qq
                act.wait_ge(s_gu, p + 1)
                nc.scalar.activation(silu_e[qq], banks(2 + qq).rearrange("p (e g f s) -> p e g f s", e=2, g=2, f=2)[:, :, 0],
                                     ACT.Silu).then_inc(s_sl, 1)
                if not last:
                    act.wait_ge(s_xp, p + 2)
                    nc.scalar.copy(xT.rearrange("p k s -> p (k s)"), banks(0, 2)).then_inc(s_xc, 1)
                act.wait_ge(s_yo[qq], i + 1)
                act.dma_start(ye_rows[bass.ds(p * P, P), :] if not isinstance(i, int) else ye_rows[p * P:(p + 1) * P, :],
                              yo[qq]).then_inc(s_st[qq], 16)

            with act.Fori(0, NPAIR // 2 - 1) as i:
                pair(i, 0)
                pair(i, 1)
            pair(NPAIR // 2 - 1, 0)
            pair(NPAIR // 2 - 1, 1, last=True)
            with act.If(over(act)):

                def over_silu(e):
                    act.wait_ge(o_up, e + 1)
                    after_first(act, o_h, e, e)
                    nc.scalar.activation(silu_s.rearrange("p f t -> p (f t)"), banks(0), ACT.Silu).then_inc(o_sl, 1)

                over_silu(0)
                with act.Fori(1, NE) as e:
                    over_silu(e)

        @block.vector
        def _(dve):
            q = [0]
            V = nc.vector

            def step(ins):
                q[0] += 1
                ins.then_inc(q_v, 1)

            def sync():
                dve.wait_ge(q_v, q[0])

            def link(ins):
                step(ins)
                sync()

            def rsqrt(dst, src, scale=1.0):
                rs[0] += 1
                V.tensor_scalar(dst, src, scale, EPS, ALU.mult, ALU.add).then_inc(s_pin, 1)
                dve.wait_ge(s_pout, rs[0])

            rs = [0]

            def layer_norm(t, i, done):
                for half in range(2):
                    step(V.bn_stats(stats[:, 2 * i + half, :], t[:, half * 512:(half + 1) * 512]))
                sync()
                link(V.bn_aggr(mv[:, i, :], stats[:, 2 * i:2 * i + 2, :].rearrange("p a s -> p (a s)")))
                rsqrt(rstd[:, i:i + 1], mv[:, i, 1:2])
                link(V.tensor_scalar(t, t, mv[:, i, 0:1], rstd[:, i:i + 1], ALU.subtract, ALU.mult))
                link(V.tensor_tensor(t, t, gb[:, 0, :], ALU.mult))
                V.tensor_tensor(t, t, gb[:, 1, :], ALU.add).then_inc(done, 1)

            dve.wait_ge(s_gb, 32)
            dve.wait_ge(s_x, 32)
            for b in range(TB):
                layer_norm(h[:, b, :], b, s_h)
            dve.wait_ge(s_h, 2)
            step(V.memset(u_pad[:, :, 0:TAPS - 1], 0.0))
            for i in range(2):
                dve.wait_ge(s_hTp, 2 * i + 2)
                V.tensor_copy(hT[:, 4 * i + 2:4 * i + 4, :].rearrange("p k t -> p (k t)"), banks(3 + 2 * i)).then_inc(s_hT, 1)

            dve.wait_ge(s_turn, 1)
            dve.wait_ge(s_par, 16 * 17)
            for b in range(TB):
                step(V.tensor_tensor(c_tok_major[:, b, :], banks(0)[:, 256 * b:256 * b + 128], row_bias[:, 0:128], ALU.add))
                step(V.tensor_tensor(wi[:, b, :], banks(0)[:, 256 * b + 128:256 * b + 132], row_bias[:, 128:132], ALU.add))
            sync()
            dve.sem_inc(s_free[0], 1)
            for b in range(TB):
                step(V.scalar_tensor_tensor(cum[:, 128 * b:128 * b + 128], c_tok_major[:, b, :], 1.0, c_tok_major[:, b, :],
                                            ALU.mult, ALU.mult))
            sync()
            link(V.tensor_reduce(ssq, cum[:, 0:256].rearrange("p (b c) -> p b c", b=TB), AX.X, ALU.add))
            rsqrt(crs, ssq, 1.0 / P)
            for b in range(TB):
                V.scalar_tensor_tensor(c_tok_major[:, b, :], c_tok_major[:, b, :], crs[:, b:b + 1], kvg,
                                       ALU.mult, ALU.mult).then_inc(s_cr, 1)

            def conv_in(c):
                t = 3 + c
                dve.wait_ge(s_sig, c + 1)
                V.scalar_tensor_tensor(u_pad[:, c, TAPS - 1:UW], banks(t % 2)[:, 0:SEQ], col(c),
                                       gate_tmp[:, c % 2, :], ALU.add, ALU.mult).then_inc(s_u, 1)
                dve.wait_ge(s_u, c + 1)
                dve.sem_inc(s_free[t % 2], 1)

            def top_keys(b):
                w = (b + 1) * P
                sc = score[:, 0:w]
                dve.wait_ge(s_relu, b + 1)
                link(V.tensor_scalar(sc, relu_i[:, 0, 0:w], wi[:, b, 0:1], None, ALU.mult))
                for hh in range(1, NH_I):
                    w_h = 2 * (hh % 2) + hh // 2
                    ins = V.scalar_tensor_tensor(sc, relu_i[:, hh, 0:w], wi[:, b, w_h:w_h + 1], sc, ALU.mult, ALU.add)
                    if hh < NH_I - 1:
                        link(ins)
                ins.then_inc(s_reluf, 1)
                dve.wait_ge(s_reluf, b + 1)
                link(V.tensor_tensor(score[:, b * P:w], score[:, b * P:w], can, ALU.min))
                for _ in range(TOPK // 8):
                    link(V.max(m8, sc))
                    link(V.match_replace(sc, m8, sc, TAKEN))
                link(V.tensor_scalar(sel_add[:, b, 0:w], sc, (BANNED + TAKEN) / 2, OFF, ALU.is_gt, ALU.mult))
                link(V.tensor_tensor(sel_add[:, b, b * P:w], sel_add[:, b, b * P:w], never, ALU.add))

            dve.wait_ge(s_con, 32)
            dve.wait_ge(s_pr, 2)
            conv_in(0)
            conv_in(1)
            top_keys(0)
            conv_in(2)
            conv_in(3)
            top_keys(1)
            for k in range(TAPS):
                for c in range(4):
                    src = u_pad[:, c, k:k + SEQ]
                    if k == 0:
                        ins = V.tensor_scalar(conv[:, c, :], src, dw[:, c, 0:1], col(B_CB + c), ALU.mult, ALU.add)
                    else:
                        ins = V.scalar_tensor_tensor(conv[:, c, :], src, dw[:, c, k:k + 1], conv[:, c, :], ALU.mult, ALU.add)
                    if k == TAPS - 1 and c == 3:
                        ins.then_inc(s_conv, 1)
                    else:
                        step(ins)
                        if k < TAPS - 1 or c < 3:
                            if q[0] > 3:
                                dve.wait_ge(q_v, q[0] - 3)
            link(V.tensor_tensor(lb, params[:, B_GAM:B_GAM + 4], params[:, B_GAM:B_GAM + 4], ALU.subtract))
            dve.sem_inc(s_lbv, 1)
            dve.wait_ge(s_lba, 1)
            link(V.reciprocal(lb_ln, lb))
            link(V.tensor_tensor(lb, lb, lb_ln, ALU.mult))
            link(V.tensor_tensor(lb, lb, lb, ALU.subtract))
            link(V.tensor_scalar(lb_a, lb, TINY, None, ALU.max))
            dve.sem_inc(s_lbv, 1)
            dve.wait_ge(s_lba, 2)
            link(V.tensor_scalar(lb, lb, TINY, OFF, ALU.is_lt, ALU.mult))
            link(V.tensor_tensor(lb_a, lb_a, lb, ALU.add))

            dve.wait_ge(s_T, 16)
            for b, (lg, w, bk) in enumerate(((logits0, P, 2), (logits1, SEQ, 4))):
                dve.wait_ge(s_lg, b + 1)
                nb = w // P
                src = banks(bk, 2 * nb).rearrange("p (h s) -> p h s", h=NH_A)
                tb_ = dist_bias[:, :, 0:w][:, :, ::-1]
                link(V.scalar_tensor_tensor(lg, src, float(P) ** -0.5, tb_, ALU.mult, ALU.add))
                link(V.tensor_tensor(lg, lg, sel_add[:, b:b + 1, 0:w].to_broadcast((P, NH_A, w)), ALU.add))
                V.tensor_reduce(nmax[:, 8 * b:8 * b + 8], lg, AX.X, ALU.max, negate=True).then_inc(s_la, 1)

            dve.wait_ge(s_rf, 4)
            V.scalar_tensor_tensor(cum, fz, -1.0, fz, ALU.mult, ALU.min).then_inc(s_hp, 1)
            for b, (lg, w) in enumerate(((logits0, P), (logits1, SEQ))):
                dve.wait_ge(s_ex, b + 1)
                link(V.reciprocal(esum[:, 8 * b:8 * b + 8], esum[:, 8 * b:8 * b + 8]))
                V.tensor_tensor(lg, lg, esum[:, 8 * b:8 * b + 8].rearrange("p (h o) -> p h o", o=1).to_broadcast((P, NH_A, w)),
                                ALU.mult).then_inc(s_pn, 1)
            dve.wait_ge(s_ha, 1)
            link(V.scalar_tensor_tensor(ls, fz, 0.0, cum, ALU.min, ALU.subtract))
            V.tensor_tensor(cum, ls, fz, ALU.subtract).then_inc(s_hp, 1)
            dve.wait_ge(s_hp, 2)
            for i in range(4):
                step(V.tensor_scalar(hd(ls, i), hd(ls, i), lb_ln[:, i:i + 1], None, ALU.add))
            sync()
            for i in range(4):
                step(V.tensor_scalar(hd(fz, i), hd(ls, i), lb_a[:, i:i + 1], None, ALU.subtract))
            sync()
            V.scalar_tensor_tensor(fz, fz, -1.0, fz, ALU.mult, ALU.min).then_inc(s_hp, 1)
            dve.wait_ge(s_ha, 3)
            for i in range(4):
                step(V.scalar_tensor_tensor(hd(ls, i), hd(ls, i), lb_a[:, i:i + 1], hd(fz, i), ALU.max, ALU.add))
            sync()
            for n in range(8):
                step(V.tensor_tensor_scan(cum[:, n * P:(n + 1) * P], ones, ls[:, n * P:(n + 1) * P], 0.0, ALU.mult, ALU.add))
            sync()
            for b in range(TB):
                t = 15 + b
                dve.wait_ge(s_turn, t + 1)
                V.tensor_tensor(v_tok[:, b, :], banks(t % 2), ri_bias, ALU.add).then_inc(s_rv, 1)
                dve.wait_ge(s_rv, b + 1)
                dve.sem_inc(s_free[t % 2], 1)

            def level_diff(lv):
                d = (fz, ls)[lv % 2]
                if lv < 7:
                    half = HALVES[lv]
                    a = cum.rearrange("p (n w) -> p n w", w=2 * half)
                    dd = d.rearrange("p (n w) -> p n w", w=2 * half)
                    mid = a[:, :, half - 1:half].to_broadcast((P, SEQ * 4 // (2 * half), 2 * half))
                    link(V.tensor_tensor(dd, a, mid, ALU.subtract))
                    V.scalar_tensor_tensor(d, d, -1.0, d, ALU.mult, ALU.min).then_inc(s_dl, 1)
                else:
                    a = cum.rearrange("p (h t) -> p h t", h=NH_R)
                    dd = d.rearrange("p (h t) -> p h t", h=NH_R)
                    mid = a[:, :, P - 1:P].to_broadcast((P, NH_R, P))
                    step(V.tensor_tensor(dd[:, :, 0:P], a[:, :, 0:P], mid, ALU.subtract))
                    step(V.tensor_copy(dd[:, :, P:SEQ], a[:, :, P:SEQ]))
                    sync()
                    V.scalar_tensor_tensor(d, d, -1.0, d, ALU.mult, ALU.min).then_inc(s_dl, 1)

            def level_xy(lv):
                e = (fz, ls)[lv % 2]
                dve.wait_ge(s_el, lv + 1)
                if lv >= 2:
                    dve.wait_ge(s_pl, lv - 1 + 1)
                step(V.tensor_tensor(Xl[lv % 2], e, qT, ALU.mult))
                V.tensor_tensor(Yl[lv % 2], e, kT, ALU.mult).then_inc(s_xy, 1)

            inner_f = inner.rearrange("p h c t -> p (h c) t")

            def take(n):
                bk = 2 + 2 * (n % 2)
                dve.wait_ge(s_pl, n + 1)
                m = level_mask[:, n:n + 1, :].to_broadcast((P, 8, P))
                V.copy_predicated(inner_f, m, banks(bk, 2).rearrange("p (n t) -> p n t", n=8)).then_inc(s_pc, 1)

            def merge(br, m):
                n = 8 * br + m
                t = T_BR[br] + m
                dve.wait_ge(s_sig, 4 + n + 1)
                y = banks(t % 2)[:, SEQ:2 * SEQ]
                if br == 0:
                    V.tensor_tensor(merged[:, m, :], gate_tmp[:, n % 2, :], y, ALU.mult).then_inc(s_mg, 1)
                    dve.wait_ge(s_mg, n + 1)
                    dve.sem_inc(s_free[t % 2], 1)
                else:
                    link(V.tensor_tensor(gate_tmp[:, n % 2, :], gate_tmp[:, n % 2, :], y, ALU.mult))
                    dve.sem_inc(s_free[t % 2], 1)
                    V.tensor_tensor(merged[:, m, :], merged[:, m, :], gate_tmp[:, n % 2, :], ALU.add).then_inc(s_mg, 1)

            def over_blocks(row):
                return row.rearrange("p (o t) -> p o t", o=1).to_broadcast((P, 4, SEQ))

            dve.wait_ge(s_uvp, 1)
            link(V.memset(t_region[:, 0:1024], 0.0))
            dve.wait_ge(s_rq, 4)
            dve.wait_ge(s_ha, 3)
            level_diff(0)
            dve.wait_ge(s_dl, 1)
            for m in range(KD):
                if m < 7:
                    level_diff(m + 1)
                level_xy(m)
                take(m)
                merge(0, m)
                if m == 1:
                    dve.wait_ge(s_mean, 1)
                    V.tensor_tensor(conv, conv, over_blocks(banks(7)[:, 0:SEQ]), ALU.subtract).then_inc(s_cen, 1)
                    dve.wait_ge(s_cen, 1)
                    V.tensor_tensor(conv_sq, conv, conv, ALU.mult).then_inc(s_sqr, 1)
                if m == 4:
                    dve.wait_ge(s_var, 1)
                    rsqrt(cvs[:, 0:SEQ], banks(7)[:, SEQ:2 * SEQ])
                    V.tensor_tensor(conv, conv, over_blocks(cvs[:, 0:SEQ]), ALU.mult).then_inc(s_cn, 1)
            dve.wait_ge(s_pl, 9)
            V.tensor_copy(inter.rearrange("p h t -> p (h t)"), banks(2)).then_inc(s_pc, 1)
            for m in range(KD):
                merge(1, m)
                if m == 4:
                    dve.wait_ge(s_ms, 1)
                    rsqrt(ls, banks(2, 2))
                    link(V.tensor_tensor(ls, ls, sgT, ALU.mult))
                    for i in range(4):
                        ins = V.scalar_tensor_tensor(oT_rnn[:, i, :], banks(6, 2)[:, i * SEQ:(i + 1) * SEQ],
                                                     col(B_NG + i), hd(ls, i), ALU.mult, ALU.mult)
                        if i < 3:
                            step(ins)
                    ins.then_inc(s_ot, 1)
            for m in range(KD):
                merge(2, m)

            for half in range(2):
                for b in range(TB):
                    n = 2 * half + b
                    t = T_OUT + n
                    dve.wait_ge(s_turn, t + 1)
                    hh = h[:, b, half * 512:(half + 1) * 512]
                    V.scalar_tensor_tensor(hh, hh, ALPHA, banks(t % 2), ALU.mult, ALU.add).then_inc(s_rs, 1)
                    dve.wait_ge(s_rs, n + 1)
                    dve.sem_inc(s_free[t % 2], 1)
            dve.wait_ge(s_gb2, 32)
            for b in range(TB):
                layer_norm(h[:, b, :], b, s_h2)
            dve.wait_ge(s_h2, 2)
            for i in range(2):
                dve.wait_ge(s_h2Tp, 2 * i + 2)
                V.tensor_copy(hT[:, 4 * i + 2:4 * i + 4, :].rearrange("p k t -> p (k t)"), banks(3 + 2 * i)).then_inc(s_h2T, 1)

            dve.wait_ge(s_rsg, 1)
            dve.wait_ge(s_ro, 32)
            dve.wait_ge(q_g, 4)
            link(V.tensor_tensor(biased, scores, rb.rearrange("p (o e) -> p o e", o=1).to_broadcast((P, TB, NE)), ALU.add))
            for b in range(TB):
                step(V.max(top8[:, b, :], biased[:, b, :]))
            sync()
            for b in range(TB):
                step(V.max_index(idx8[:, b, :], top8[:, b, :], biased[:, b, :]))
            sync()
            link(V.tensor_copy(idx8f, idx8[:, :, :]))
            for b in range(TB):
                step(V.tensor_tensor(oh4[:, b], iota_e.rearrange("p (o e) -> p o e", o=1).to_broadcast((P, TOPE, NE)),
                                     idx8f[:, b, 0:TOPE].rearrange("p (j o) -> p j o", o=1).to_broadcast((P, TOPE, NE)),
                                     ALU.is_equal))
            sync()
            V.tensor_reduce(sel, onehot.rearrange("p (b j) e -> p b e j", b=TB), AX.X, ALU.add).then_inc(s_sel, 1)
            for b in range(TB):
                step(V.tensor_tensor(prod4[:, b], oh4[:, b], scores[:, b:b + 1, :].to_broadcast((P, TOPE, NE)), ALU.mult))
            sync()
            link(V.tensor_reduce(wj.rearrange("p b j -> p (b j)"), prod, AX.X, ALU.add))
            link(V.tensor_reduce(wsum, wj, AX.X, ALU.add))
            link(V.reciprocal(wsum, wsum))
            link(V.scalar_tensor_tensor(gate, wj, ROUTE_SCALE, wsum.rearrange("p (b o) -> p b o", o=1).to_broadcast((P, TB, TOPE)),
                                        ALU.mult, ALU.mult))
            dve.wait_ge(s_rk, 1)
            step(V.tensor_copy(rank, banks(7)[:, 0:2 * NE].rearrange("p (b e) -> p b e", b=TB)))
            step(V.tensor_scalar(rank_in, sel, -1000.0, 1000.0, ALU.mult, ALU.add))
            sync()
            link(V.tensor_tensor(rank_in, rank_in, rank, ALU.add))
            for b in range(TB):
                ins = V.tensor_tensor(slot_of[:, b], rank_in[:, b, :].rearrange("p (e o) -> p e o", o=1).to_broadcast((P, NE, CAP)),
                                      iota_c.rearrange("p (o c) -> p o c", o=1).to_broadcast((P, NE, CAP)), ALU.is_equal)
                ins.then_inc(s_so, 1)
            dve.wait_ge(s_so, 2)
            link(V.tensor_reduce(cmax[0:1, :], banks(7)[0:1, 64:64 + NE], AX.X, ALU.max))
            V.tensor_copy(count[:, :], cmax[0:1, :]).then_inc(s_cnt, 1)
            dve.wait_ge(s_idp, 1)
            V.tensor_copy(ids[:, :], banks(6)[:, 128:128 + NPAIR]).then_inc(s_ids, 1)
            for b in range(TB):
                step(V.tensor_tensor(prod4[:, b], oh4[:, b], rank[:, b:b + 1, :].to_broadcast((P, TOPE, NE)), ALU.mult))
            sync()
            link(V.tensor_reduce(rank_j.rearrange("p b j -> p (b j)"), prod, AX.X, ALU.add))
            link(V.tensor_scalar(fits, rank_j, float(CAP), None, ALU.is_lt))
            link(V.tensor_tensor(gate_main, gate, fits, ALU.mult))
            link(V.tensor_tensor(gate_over, gate, gate_main, ALU.subtract))
            link(V.tensor_tensor(rank_j, rank_j, fits, ALU.mult))
            link(V.scalar_tensor_tensor(row_f, idx8f[:, :, 0:TOPE], float(CAP), rank_j, ALU.mult, ALU.add))
            V.tensor_copy(row_of[:, :], row_f.rearrange("p b j -> p (b j)")).then_inc(s_rows, 1)
            for b in range(TB):
                step(V.tensor_tensor(prod4[:, b], oh4[:, b],
                                     gate_over[:, b, :].rearrange("p (j o) -> p j o", o=1).to_broadcast((P, TOPE, NE)), ALU.mult))
            sync()
            link(V.tensor_reduce(g_over, prod.rearrange("p (b j) e -> p b e j", b=TB), AX.X, ALU.add))

            dve.wait_ge(s_ssl, 1)
            dve.wait_ge(s_turn, T_SH + 2)
            V.tensor_tensor(hid_s.rearrange("p f t -> p (f t)"), silu_s.rearrange("p f t -> p (f t)"), banks((T_SH + 1) % 2),
                            ALU.mult).then_inc(s_sh, 1)
            dve.wait_ge(s_sh, 1)
            dve.sem_inc(s_free[(T_SH + 1) % 2], 1)
            for n in range(4):
                t = T_SH + 2 + n
                b, half = n // 2, n % 2
                dve.wait_ge(s_turn, t + 1)
                V.scalar_tensor_tensor(acc[:, b, half * 512:(half + 1) * 512], h[:, b, half * 512:(half + 1) * 512], ALPHA,
                                       banks(t % 2), ALU.mult, ALU.add).then_inc(s_acc, 1)
                dve.wait_ge(s_acc, n + 1)
                dve.sem_inc(s_free[t % 2], 1)

            def pair(i, qq):
                p = i * 2 + qq
                dve.wait_ge(s_sl, p + 1)
                V.tensor_tensor(hid[qq], silu_e[qq], banks(2 + qq).rearrange("p (e g f s) -> p e g f s", e=2, g=2, f=2)[:, :, 1],
                                ALU.mult).then_inc(s_hid[qq], 1)
                dve.wait_ge(s_dn, p + 1)
                after_first(dve, s_st[qq], i * 16, i)
                V.tensor_copy(yo[qq], banks(4 + 2 * qq, 2)).then_inc(s_yo[qq], 1)

            pair(0, 0)
            pair(0, 1)
            with dve.Fori(1, NPAIR // 2) as i:
                pair(i, 0)
                pair(i, 1)
            with dve.If(over(dve)):
                with dve.Fori(0, NE) as e:
                    dve.wait_ge(o_sl, e + 1)
                    V.tensor_tensor(hid_s.rearrange("p f t -> p (f t)"), silu_s.rearrange("p f t -> p (f t)"), banks(1),
                                    ALU.mult).then_inc(o_h, 1)
                    dve.wait_ge(o_dn, e + 1)
                    for b in range(TB):
                        V.scalar_tensor_tensor(acc[:, b, :], banks(4 + 2 * b, 2), g_over[:, b, bass.ds(e, 1)], acc[:, b, :],
                                               ALU.mult, ALU.add).then_inc(o_acc, 1)
                    dve.wait_ge(o_acc, e * 2 + 2)
            for n in range(TB * TOPE):
                b, j = n // TOPE, n % TOPE
                dve.wait_ge(s_G[n % 4], 16 * (n // 4 + 1))
                a = acc[:, b, :] if j < TOPE - 1 else h[:, b, :]
                V.scalar_tensor_tensor(a, G[n % 4], gate_main[:, b, j:j + 1], acc[:, b, :], ALU.mult, ALU.add).then_inc(s_Gu, 1)
                dve.wait_ge(s_Gu, n + 1)
                if n == TOPE - 1:
                    dve.wait_ge(s_gb3, 32)
                if j == TOPE - 1:
                    layer_norm(h[:, b, :], b, s_y)

        @block.tensor
        def _(pe):
            T = nc.tensor
            turns_on = [0, 0]

            def start_turn(t):
                if turns_on[t % 2]:
                    pe.wait_ge(s_free[t % 2], turns_on[t % 2])
                turns_on[t % 2] += 1

            def transpose_h(ready, done):
                for bank in range(4):
                    for kk in range(2):
                        for b in range(TB):
                            if bank == 0 and kk == 0:
                                pe.wait_ge(ready, b + 1)
                            ins = T.transpose(banks(2 + bank)[:, kk * SEQ + b * P:kk * SEQ + (b + 1) * P],
                                              h[:, b, (2 * bank + kk) * P:(2 * bank + kk + 1) * P], ident)
                    ins.then_inc(done, 1)

            def feat(dst, w, c0, m=P, src=hT, nk=KD):
                for k in range(nk):
                    ins = T.matmul(dst, w[:, k, c0:c0 + m], src[:, k, :], start=(k == 0), stop=(k == nk - 1))
                return ins

            def tokm(dst, w, c0, n, b, src=hT, nk=KD):
                for k in range(nk):
                    ins = T.matmul(dst, src[:, k, b * P:(b + 1) * P], w[:, k, c0:c0 + n], start=(k == 0), stop=(k == nk - 1))
                return ins

            pe.wait_ge(s_par, 16 * 17)
            pe.wait_ge(s_con, 32)
            T.transpose(banks(6)[:, 0:79], prow[0:79, :], consts[0:79, 0, 0:79])
            for c in range(4):
                T.transpose(banks(7)[:, c * TAPS:(c + 1) * TAPS], dw_rows[0:TAPS, c * P:(c + 1) * P], consts[0:TAPS, 0, 0:TAPS])
            T.matmul(banks(6)[0:NH_A, 128:512], relb[0:NBUCKET, :], buckets[0:NBUCKET, :], start=True, stop=True).then_inc(s_prT, 1)
            transpose_h(s_h, s_hTp)
            pe.wait_ge(s_hT, 4)

            arrived(pe, 0)
            wI = slot(0, KD, N_IDX_COLS)
            start_turn(0)
            for b in range(TB):
                tokm(banks(0)[:, 256 * b:256 * b + 128], wI, 0, 128, b)
                ins = tokm(banks(0)[:, 256 * b + 128:256 * b + 132], wI, 448, 4, b)
            ins.then_inc(s_turn, 1)
            start_turn(1)
            feat(banks(1)[:, 0:SEQ], wI, 128)
            feat(banks(1)[:, SEQ:2 * SEQ], wI, 256).then_inc(s_turn, 1)
            start_turn(2)
            feat(banks(0)[0:64, 0:SEQ], wI, 384, m=64)
            feat(banks(0)[64:128, 0:SEQ], wI, 384, m=64).then_inc(s_turn, 1)
            arrived(pe, 1)
            arrived(pe, 2)
            for c in range(4):
                t = 3 + c
                start_turn(t)
                feat(banks(t % 2)[:, 0:SEQ], slot(1, KD, 512), c * P)
                feat(banks(t % 2)[:, SEQ:2 * SEQ], slot(2, KD, 512), c * P).then_inc(s_turn, 1)
                if c == 0:
                    pe.wait_ge(s_cr, 2)
                    for b in range(TB):
                        ins = T.transpose(banks(5)[:, b * P:(b + 1) * P], c_tok_major[:, b, :], ident)
                    ins.then_inc(s_cTp, 1)
                if c == 1:
                    pe.wait_ge(s_qk, 3)
                    pe.wait_ge(s_cT, 1)
                    for b in range(TB):
                        w = (b + 1) * P
                        for hh in range(NH_I):
                            lo = 64 * (hh % 2)
                            ins = T.matmul(banks(2 + 2 * b + hh % 2)[:, hh // 2 * w:(hh // 2 + 1) * w],
                                           qiT[lo:lo + 64, hh // 2, b * P:(b + 1) * P], kiT[lo:lo + 64, 0:w],
                                           start=True, stop=True)
                        ins.then_inc(s_sc, 1)

            def two_blocks(t, item, c0):
                arrived(pe, item)
                start_turn(t)
                w = slot(item, KD, 512)
                feat(banks(t % 2)[:, 0:SEQ], w, c0)
                feat(banks(t % 2)[:, SEQ:2 * SEQ], w, c0 + P).then_inc(s_turn, 1)

            for i in range(4):
                two_blocks(7 + i, 3 + i // 2, 256 * (i % 2))
            for i in range(2):
                two_blocks(11 + i, 5, 256 * i)
            pe.wait_ge(s_aq, 8)
            pe.wait_ge(s_cT, 1)
            pe.wait_ge(s_relu, 2)
            for b, bk in ((0, 2), (1, 4)):
                w = (b + 1) * P
                for hh in range(NH_A):
                    ins = T.matmul(banks(bk, 2 * (b + 1))[:, hh * w:(hh + 1) * w], aqT[:, hh, b * P:(b + 1) * P], cT[:, 0:w],
                                   start=True, stop=True)
                ins.then_inc(s_lg, 1)
            for i in range(2):
                two_blocks(13 + i, 6, 256 * i)

            def probs_T(n, b, sblk, bk):
                lg = logits0 if b == 0 else logits1
                pe.wait_ge(s_pn, b + 1)
                if n == 2:
                    pe.wait_ge(s_pT, 1)
                for hh in range(NH_A):
                    ins = T.transpose(banks(bk, 2)[:, hh * P:(hh + 1) * P], lg[:, hh, sblk * P:(sblk + 1) * P], ident)
                ins.then_inc(s_pTp, 1)

            for b in range(TB):
                t = 15 + b
                arrived(pe, 7)
                start_turn(t)
                tokm(banks(t % 2), slot(7, KD, 512), 0, 512, b).then_inc(s_turn, 1)
                if b == 0:
                    probs_T(0, 0, 0, 2)
                    probs_T(1, 1, 0, 6)
            probs_T(2, 1, 1, 2)
            two_blocks(17, 8, 0)
            for b in range(TB):
                pe.wait_ge(s_pT, 1 if b == 0 else 3)
                if b == 1:
                    pe.wait_ge(s_oT, 1)
                for half in range(2):
                    for s_ in range(b + 1):
                        ins = T.matmul(banks(4 + half), c_tok_major[:, s_, :],
                                       probsT[:, b + s_, 4 * half:4 * half + 4, :].rearrange("p h t -> p (h t)"),
                                       start=(s_ == 0), stop=(s_ == b))
                ins.then_inc(s_oTp, 1)
            two_blocks(18, 8, 256)
            pe.wait_ge(s_oT, 2)
            pe.wait_ge(s_uvl, 16)
            for hh in range(NH_A):
                lo = 64 * (hh % 2)
                ins = T.matmul(banks(6, 2)[lo:lo + 64, (hh // 2) * SEQ:(hh // 2 + 1) * SEQ], wuv[:, hh, :], oT_att[:, hh, :],
                               start=True, stop=True)
            ins.then_inc(s_uvp, 1)

            def level(n):
                bk = 2 + 2 * (n % 2)
                if n >= 2:
                    pe.wait_ge(s_pc, n - 1)
                if n == 0:
                    pe.wait_ge(s_rq, 4)
                    pe.wait_ge(s_ha, 2)
                    X, Y = qT, kT
                else:
                    pe.wait_ge(s_xy, n)
                    X, Y = Xl[(n - 1) % 2], Yl[(n - 1) % 2]
                if n < 8:
                    for m in range(8):
                        ins = T.matmul(banks(bk, 2)[:, m * P:(m + 1) * P], Y[:, m * P:(m + 1) * P], X[:, m * P:(m + 1) * P],
                                       start=True, stop=True)
                else:
                    for m in range(NH_R):
                        ins = T.matmul(banks(bk)[:, m * P:(m + 1) * P], Y[:, 2 * m * P:(2 * m + 1) * P],
                                       X[:, (2 * m + 1) * P:(2 * m + 2) * P], start=True, stop=True)
                ins.then_inc(s_pl, 1)

            def branch(br, m, src):
                t = T_BR[br] + m
                item = I_BR[br]
                if m == 0:
                    arrived(pe, item)
                if m % 4 == 0:
                    arrived(pe, item + 1 + m // 4)
                start_turn(t)
                feat(banks(t % 2)[:, 0:SEQ], slot(item + 1 + m // 4, KD, 512), (m % 4) * P)
                feat(banks(t % 2)[:, SEQ:2 * SEQ], slot(item, 4, D), m * P, src=src, nk=4).then_inc(s_turn, 1)

            pe.wait_ge(s_aT, 1)
            pe.wait_ge(s_oT, 2)
            level(0)
            for m in range(KD):
                branch(0, m, aT)
                if m == 0:
                    pe.wait_ge(s_conv, 1)
                    for c in range(4):
                        ins = T.matmul(banks(7)[:, 0:SEQ], mean_w, conv[:, c, :], start=(c == 0), stop=(c == 3))
                    ins.then_inc(s_mean, 1)
                level(m + 1)
                if m == 3:
                    pe.wait_ge(s_sqr, 1)
                    for c in range(4):
                        ins = T.matmul(banks(7)[:, SEQ:2 * SEQ], mean_w, conv_sq[:, c, :], start=(c == 0), stop=(c == 3))
                    ins.then_inc(s_var, 1)
            pe.wait_ge(s_pc, 9)
            pe.wait_ge(s_rv, 2)
            pe.wait_ge(s_cn, 1)
            for hh in range(NH_R):
                o = banks(6, 2)[:, hh * SEQ:(hh + 1) * SEQ]
                T.matmul(o[:, 0:P], v_tok[:, 0, hh * P:(hh + 1) * P], inner[:, hh, 0, :], start=True, stop=True)
                T.matmul(o[:, P:SEQ], v_tok[:, 0, hh * P:(hh + 1) * P], inter[:, hh, :], start=True, stop=False)
                ins = T.matmul(o[:, P:SEQ], v_tok[:, 1, hh * P:(hh + 1) * P], inner[:, hh, 1, :], start=False, stop=True)
            ins.then_inc(s_on, 1)
            pe.wait_ge(s_cT2, 1)
            for m in range(KD):
                branch(1, m, conv)
                if m == 3:
                    pe.wait_ge(s_osq, 1)
                    for z in range(2):
                        ins = T.matmul(banks(2 + z), mean_o, fz[:, 512 * z:512 * z + 512], start=True, stop=True)
                    ins.then_inc(s_ms, 1)
            pe.wait_ge(s_ot, 1)
            for m in range(KD):
                branch(2, m, oT_rnn)
            pe.wait_ge(s_mg, 24)
            for half in range(2):
                arrived(pe, I_OUT + half)
                for b in range(TB):
                    t = T_OUT + 2 * half + b
                    start_turn(t)
                    tokm(banks(t % 2), slot(I_OUT + half, KD, 512), 0, 512, b, src=merged).then_inc(s_turn, 1)

            transpose_h(s_h2, s_h2Tp)
            pe.wait_ge(s_h2T, 4)
            pe.wait_ge(s_ro, 32)
            for b in range(TB):
                ins = tokm(banks(6)[:, b * NE:(b + 1) * NE], rw, 0, NE, b)
            ins.then_inc(s_rl, 1)
            arrived(pe, I_SGU)
            for g in range(2):
                t = T_SH + g
                start_turn(t)
                feat(banks(t % 2)[:, 0:SEQ], slot(I_SGU, KD, 512), 2 * g * P)
                feat(banks(t % 2)[:, SEQ:2 * SEQ], slot(I_SGU, KD, 512), (2 * g + 1) * P).then_inc(s_turn, 1)
            pe.wait_ge(s_sel, 1)
            T.matmul(banks(7)[:, 0:NE], before, sel[:, 0, :], start=True, stop=True)
            T.matmul(banks(7)[:, NE:2 * NE], ones, sel[:, 0, :], start=True, stop=False)
            T.matmul(banks(7)[:, NE:2 * NE], before, sel[:, 1, :], start=False, stop=True)
            for b in range(TB):
                ins = T.matmul(banks(7)[:, 64:64 + NE], ones, sel[:, b, :], start=(b == 0), stop=(b == 1))
            ins.then_inc(s_rk, 1)
            pe.wait_ge(s_so, 2)
            pe.wait_ge(s_tok, 1)
            for p in range(NPAIR):
                for b in range(TB):
                    ins = T.matmul(banks(6)[:, 128 + p:129 + p], slot_of[:, b, 2 * p:2 * p + 2, :].rearrange("p e c -> p (e c)"),
                                   tok_id[:, b:b + 1], start=(b == 0), stop=(b == 1))
            ins.then_inc(s_idp, 1)
            arrived(pe, I_SDN)
            pe.wait_ge(s_sh, 1)
            for n in range(4):
                t = T_SH + 2 + n
                b, half = n // 2, n % 2
                start_turn(t)
                tokm(banks(t % 2), slot(I_SDN, 2, D), half * 512, 512, b, src=hid_s, nk=2).then_inc(s_turn, 1)

            def tokens_T(i, qq):
                p = i * 2 + qq
                pe.wait_ge(s_xg[qq], i * 16 + 16)
                if not (isinstance(p, int) and p == 0):
                    pe.wait_ge(s_xc, p)
                for k in range(KD):
                    ins = T.transpose(banks(0, 2)[:, k * P:(k + 1) * P], xg[qq][:, k * P:(k + 1) * P], ident)
                ins.then_inc(s_xp, 1)

            def pair(i, qq, last=False):
                p = i * 2 + qq
                pe.wait_ge(s_xc, p + 1)
                after_first(pe, s_hid[qq], i, i)
                up = banks(2 + qq).rearrange("p (e f s) -> p e f s", e=2, f=4)
                for e in range(2):
                    s, v = pair_item(i, qq, e)
                    pe.wait_ge(s_w[s], v)
                    w = ring[:, s, :].rearrange("p (k n) -> p k n", k=KD)
                    for f in range(4):
                        for k in range(KD):
                            ins = T.matmul(up[:, e, f, :], w[:, k, f * P:(f + 1) * P], xT[:, k, e * CAP:(e + 1) * CAP],
                                           start=(k == 0), stop=(k == KD - 1))
                ins.then_inc(s_gu, 1)
                if not last:
                    tokens_T(*((i, 1) if qq == 0 else (i + 1, 0)))
                s, v = pair_item(i, qq, 2)
                pe.wait_ge(s_w[s], v)
                pe.wait_ge(s_hid[qq], i + 1)
                after_first(pe, s_yo[qq], i, i)
                w = ring[:, s, :].rearrange("p (e f n) -> p e f n", e=2, f=2)
                for e in range(2):
                    for half in range(2):
                        for f in range(2):
                            ins = T.matmul(banks(4 + 2 * qq + half)[e * CAP:(e + 1) * CAP, :], hid[qq][:, e, f, :],
                                           w[:, e, f, half * 512:(half + 1) * 512], start=(f == 0), stop=(f == 1))
                ins.then_inc(s_dn, 1)

            pe.wait_ge(s_acc, 4)
            tokens_T(0, 0)
            pair(0, 0)
            pair(0, 1)
            with pe.Fori(1, NPAIR // 2 - 1) as i:
                pair(i, 0)
                pair(i, 1)
            pair(NPAIR // 2 - 1, 0)
            pair(NPAIR // 2 - 1, 1, last=True)
            with pe.If(over(pe)):
                pe.wait_ge(s_xc, NPAIR)
                for qq in range(2):
                    pe.wait_ge(s_yo[qq], NPAIR // 2)
                wg = ring[:, 0, :].rearrange("p (k n) -> p k n", k=KD)
                wd = ring[:, 1, 0:2 * D].rearrange("p (f n) -> p f n", f=2)

                def over_expert(e):
                    pe.wait_ge(o_w, e * 32 + 32)
                    after_first(pe, o_h, e, e)
                    for f in range(4):
                        ins = feat(banks(f // 2)[:, (f % 2) * SEQ:(f % 2 + 1) * SEQ], wg, f * P)
                    ins.then_inc(o_up, 1)
                    pe.wait_ge(o_h, e + 1)
                    after_first(pe, o_acc, e * 2, e)
                    for b in range(TB):
                        for half in range(2):
                            ins = tokm(banks(4 + 2 * b + half), wd, half * 512, 512, b, src=hid_s, nk=2)
                    ins.then_inc(o_dn, 1)

                over_expert(0)
                with pe.Fori(1, NE) as e:
                    over_expert(e)


_INS = ["x", "ln_in_g", "ln_in_b", "w_in", "b_in", "conv_dw", "conv_b", "conv_ln_g", "conv_ln_b", "w_conv_proj",
        "hgrn_gamma", "hgrn_norm_g", "w_rnn_proj", "kv_norm_g", "w_uv", "w_att_proj", "rel_bias", "w_out",
        "ln_mix_g", "ln_mix_b", "router_w", "router_b", "w_expert_gu", "w_expert_dn", "w_shared_gu",
        "w_shared_dn", "ln_ffn_g", "ln_ffn_b"]


def shape_constants():
    import numpy as np
    a, b = np.arange(P)[:, None], np.arange(P)[None, :]
    tables = np.stack([a == b, np.ones((P, P)), a < b, np.where(b <= a, 3.0e38, BANNED), np.where(b <= a, 0.0, OFF),
                       np.full((P, P), 1 / D_CONV), np.full((P, P), 1 / P)], axis=1).astype(np.float32)
    level = [a == b] + [(a // (2 * hf) == b // (2 * hf)) & (a % (2 * hf) < hf) & (b % (2 * hf) >= hf) for hf in HALVES]
    dist = np.maximum(np.arange(NDIST) - (P - 1), 0)
    exact = NBUCKET // 2
    large = exact + (np.log(np.maximum(dist, 1).astype(np.float32) / exact) / math.log(128 / exact)
                     * (NBUCKET - exact)).astype(np.int32)
    bucket = np.where(dist < exact, dist, np.minimum(large, NBUCKET - 1))
    onehot = (bucket[None, :] == np.arange(NBUCKET)[:, None]).astype(np.float32)
    return {"c_f32": tables, "c_level": np.stack(level, axis=1).astype(np.float32), "c_onehot": onehot}


def kernel(**inputs):
    import numpy as np
    import concourse.bacc as bacc
    from concourse.bass_utils import run_bass_kernel_spmd

    nc = bacc.Bacc("TRN2", target_bir_lowering=False, num_devices=1)
    arrays, args = {}, {}
    for name, a in [(n, np.ascontiguousarray(inputs[n])) for n in _INS] + list(shape_constants().items()):
        arrays[f"in_{name}"] = a
        args[name] = nc.dram_tensor(f"in_{name}", a.shape, mybir.dt.from_np(a.dtype), kind="ExternalInput").ap()
    args["out"] = nc.dram_tensor("out_0", (1, SEQ, D), F32, kind="ExternalOutput").ap()
    build(nc, **args)
    r = run_bass_kernel_spmd(nc, [arrays], core_ids=[0])
    return r.results[0]["out_0"]
```

```python
import math
from contextlib import ExitStack

import concourse.bass as bass
from concourse import mybir

F32 = mybir.dt.float32
I32 = mybir.dt.int32
U8 = mybir.dt.uint8
ALU = mybir.AluOpType
ACT = mybir.ActivationFunctionType
AX = mybir.AxisListType

P = 128
D = 1024
SEQ = 256
TB = SEQ // P
KD = D // P
D_CONV = 512
TAPS = 31
TAPS_FIRST, TAPS_SECOND = 19, 23
NH_R = 4
NH_A = 8
NH_I = 4
D_IDX = 64
TOPK = 64
NBUCKET = 32
NDIST = 384
NE = 32
TOPE = 4
F_E = 256
ROUTE_SCALE = 2.5
ALPHA = 2.0 ** 0.25
EPS = 1e-5
CAP = 64
NPAIR = NE // 2
COL_RQ, COL_RF, COL_RI, COL_RG = 1024, 1536, 2048, 2560
COL_AQ, COL_IDX, COL_GATE = 3072, 4096, 4548
N_IDX_COLS = COL_GATE - COL_IDX
WSLOTS = 6
SLOT = 4096
BANNED = -3.0e38
TAKEN = -3.4e38
OFF = -1.0e30
TINY = 2.0 ** -60
POOL_F = 22912
HALVES = [1, 2, 4, 8, 16, 32, 64]


def build(nc, x, ln_in_g, ln_in_b, w_in, b_in, conv_dw, conv_b, conv_ln_g, conv_ln_b, w_conv_proj,
          hgrn_gamma, hgrn_norm_g, w_rnn_proj, kv_norm_g, w_uv, w_att_proj, rel_bias, w_out,
          ln_mix_g, ln_mix_b, router_w, router_b, w_expert_gu, w_expert_dn, w_shared_gu,
          w_shared_dn, ln_ffn_g, ln_ffn_b, c_f32, c_level, c_onehot, out):
    bias_by_dist = nc.dram_tensor("bias_by_dist", (NH_A, NDIST), F32, kind="Internal")
    bias_ap = bias_by_dist.ap()

    ctx = ExitStack()
    with ctx:
        def sb(name, shape, dt=F32):
            return ctx.enter_context(nc.sbuf_tensor(name, shape, dt))

        def sem(name):
            return ctx.enter_context(nc.semaphore(name))

        ring = sb("ring", [P, WSLOTS * SLOT])
        h = sb("h", [P, TB, D])
        hT = sb("hT", [P, KD, SEQ])
        consts = sb("consts", [P, 7, P])
        level_mask = sb("level_mask", [P, 8, P], U8)
        params = sb("params", [P, P])
        stats = sb("stats", [P, 4, 6])
        mv = sb("mv", [P, 4, 2])
        rstd = sb("rstd", [P, 4])
        small = sb("small", [P, 72])
        ident, ones, before, can, never, mean_w, mean_o = (consts[:, i, :] for i in range(7))

        pool = sb("pool", [P, POOL_F])
        used = [0]

        def part(n):
            used[0] += n
            assert used[0] <= POOL_F, used
            return pool[:, used[0] - n:used[0]]

        gb_conv = part(2 * D + 160)
        gb = gb_conv[:, 0:2 * D].rearrange("p (a d) -> p a d", a=2)
        UW = SEQ + TAPS - 1
        u_pad = gb_conv[:, 0:4 * UW].rearrange("p (c t) -> p c t", c=4)
        conv = gb_conv[:, 4 * UW:4 * UW + 1024].rearrange("p (c t) -> p c t", c=4)
        cvs = gb_conv[:, 0:1024]
        conv_sq = cvs.rearrange("p (c t) -> p c t", c=4)
        aq_merged = part(2048)
        aqT = aq_merged.rearrange("p (h t) -> p h t", h=NH_A)
        merged = aq_merged.rearrange("p (m t) -> p m t", m=KD)
        c_tok_major = part(256).rearrange("p (b c) -> p b c", b=TB)
        cT = part(256)
        qi_wuv = part(512)
        qiT = qi_wuv.rearrange("p (a t) -> p a t", a=2)
        wuv = qi_wuv.rearrange("p (h v) -> p h v", h=NH_A)
        kiT = part(256)
        sel_add = part(512).rearrange("p (b s) -> p b s", b=TB)
        r1 = part(6144)
        logits1 = r1[:, 0:2048].rearrange("p (h s) -> p h s", h=NH_A)
        relu_i = r1[:, 0:1024].rearrange("p (h s) -> p h s", h=NH_I)
        oT_att = r1[:, 0:2048].rearrange("p (h t) -> p h t", h=NH_A)
        logits0 = r1[:, 2048:3072].rearrange("p (h s) -> p h s", h=NH_A)
        score = r1[:, 2048:2304]
        probsT = r1[:, 3072:6144].rearrange("p (b h t) -> p b h t", b=3, h=NH_A)
        Xl = [r1[:, 2048 * i:2048 * i + 1024] for i in range(2)]
        Yl = [r1[:, 2048 * i + 1024:2048 * i + 2048] for i in range(2)]
        inter = r1[:, 4096:4608].rearrange("p (h t) -> p h t", h=NH_R)
        aT = r1[:, 5120:6144].rearrange("p (c t) -> p c t", c=4)
        t_region = part(2048)
        dist_bias = t_region.rearrange("p (h s) -> p h s", h=NH_A)
        inner = t_region[:, 0:1024].rearrange("p (h c t) -> p h c t", h=NH_R, c=2)
        oT_rnn = t_region[:, 1024:2048].rearrange("p (h t) -> p h t", h=NH_R)
        fz, cum, ls, kT, qT, sgT = (part(1024) for _ in range(6))
        v_tok = part(1024).rearrange("p (b n) -> p b n", b=TB)
        gate_tmp = part(512).rearrange("p (a t) -> p a t", a=2)
        ri_bias = part(512)
        row_bias = part(132)
        kvg = part(128)
        wi = part(8).rearrange("p (b h) -> p b h", b=TB)
        dw = part(4 * TAPS).rearrange("p (c k) -> p c k", c=4)

        def hd(t, i):
            return t[:, i * SEQ:(i + 1) * SEQ]

        EXTRA = 6048
        extra_slots = [pool[:, EXTRA + SLOT * i:EXTRA + SLOT * (i + 1)] for i in range(3)]
        regions = {"late": [2208, EXTRA], "early": [EXTRA + 3 * SLOT, 21408], "biases": [21920, POOL_F]}

        def mpart(region, *shape):
            n = math.prod(shape)
            at, end = regions[region]
            assert at + n <= end, (region, at, n, end)
            regions[region][0] += n
            v = pool[:, at:at + n]
            if len(shape) == 2:
                return v.rearrange("p (a b) -> p a b", a=shape[0])
            if len(shape) == 3:
                return v.rearrange("p (a b c) -> p a b c", a=shape[0], b=shape[1])
            return v
        xT = mpart("late", KD, 2 * CAP)
        yo = mpart("late", D)
        hid_s = mpart("late", 2, SEQ)
        silu_s = mpart("late", 2, SEQ)
        rw = mpart("early", KD, NE)
        slot_of = [mpart("early", TB, 2 * CAP) for _ in range(3)]
        slot_gate = [mpart("early", TB, 2 * CAP) for _ in range(3)]
        hid = mpart("early", F_E)
        silu_e = mpart("early", F_E)
        hg = [mpart(region, 2 * F_E) for region in ("late", "early", "biases")]
        scores = mpart("biases", TB, NE)
        biased = mpart("biases", TB, NE)
        sel = mpart("biases", TB, NE)
        gate = mpart("biases", TB, NE)
        rank_in = mpart("biases", TB, NE)
        top8 = mpart("biases", TB, 8)
        wsum = mpart("biases", TB)
        rb = mpart("biases", NE)
        cmax = mpart("biases", 1)
        iota_c = mpart("late", CAP)
        g_over = mpart("early", TB, NE)
        count = sb("count", [1, 1], I32)

        ps = ctx.enter_context(nc.psum_tensor("ps", [P, 8, 512], F32))

        def banks(a, n=1):
            return ps[:, a:a + n, :].rearrange("p b n -> p (b n)")

        s_x = sem("x_loaded"); s_gb = sem("ln_in_params_loaded"); s_par = sem("param_rows_loaded"); s_rp = sem("other_small_params_loaded")
        s_con = sem("consts_loaded"); s_lm = sem("level_masks_loaded")
        s_w = [sem(f"weights_in_slot{i}") for i in range(WSLOTS + 3)]
        s_h = sem("h_ready"); s_hTp = sem("hT_in_psum"); s_hT = sem("hT_ready")
        s_prT = sem("params_in_psum"); s_pr = sem("params_ready")
        s_pin = sem("power_base_ready"); s_pout = sem("power_ready")
        s_bd = sem("bias_by_dist_ready"); s_bdd = sem("bias_by_dist_in_dram"); s_T = sem("dist_bias_loaded"); s_uvl = sem("value_weights_loaded")
        s_turn = sem("turn_done")
        s_free = [sem("bank0_free"), sem("bank1_free")]
        s_sig = sem("sigmoid_ready")
        s_cr = sem("c_ready"); s_cTp = sem("cT_in_psum"); s_cT = sem("cT_ready")
        s_qk = sem("indexer_qk_ready"); s_sc = sem("indexer_products_ready"); s_relu = sem("relu_ready")
        s_reluf = sem("relu_used")
        s_upad = sem("u_pad_ready"); s_u = sem("conv_input_ready")
        s_conv = sem("conv_ready"); s_mean = sem("conv_mean_ready"); s_sqr = sem("conv_squares_ready")
        s_cdg = sem("conv_rstd_diagonal"); s_csp = sem("conv_rstd_spread")
        s_cen = sem("conv_centred"); s_var = sem("conv_var_ready"); s_cn = sem("conv_normed")
        s_cT2 = sem("conv_silu_ready")
        s_aq = sem("att_q_ready"); s_lg = sem("logits_ready"); s_la = sem("logits_biased")
        s_ex = sem("exp_ready"); s_pn = sem("probs_ready"); s_pTp = sem("probsT_in_psum")
        s_pT = sem("probsT_ready"); s_oTp = sem("att_oT_in_psum"); s_oT = sem("att_oT_ready")
        s_uvp = sem("att_values_in_psum"); s_aT = sem("att_values_ready")
        s_rf = sem("forget_ready"); s_hp = sem("hgrn_prep_vector"); s_ha = sem("hgrn_prep_scalar")
        s_lbv = sem("lower_bound_vector"); s_lba = sem("lower_bound_scalar")
        s_rq = sem("rnn_q_ready"); s_rv = sem("rnn_v_ready"); s_rg = sem("rnn_gate_ready")
        s_dl = sem("level_diff_ready"); s_el = sem("level_decay_ready"); s_xy = sem("level_xy_ready")
        s_pl = sem("level_products_ready"); s_pc = sem("level_products_taken")
        s_on = sem("rnn_o_in_psum"); s_osq = sem("rnn_o_squares_ready"); s_ms = sem("rnn_ms_ready")
        s_rdg = sem("rnn_rstd_diagonal"); s_rsp = sem("rnn_rstd_spread")
        s_ot = sem("rnn_oT_ready")
        s_mg = sem("merged_ready"); s_rs = sem("mix_residual_ready")
        s_gb2 = sem("ln_mix_params_loaded"); s_gb3 = sem("ln_ffn_params_loaded")
        s_h2 = sem("h2_ready"); s_h2Tp = sem("h2T_in_psum"); s_h2T = sem("h2T_ready")
        s_ro = sem("router_loaded"); s_rl = sem("router_logits_ready"); s_rsg = sem("router_scores_ready")
        s_sel = sem("selection_ready"); s_rk = sem("ranks_ready"); s_cnt = sem("count_ready")
        s_ssl = sem("shared_silu_ready"); s_sh = sem("shared_hidden_ready"); s_sdn = sem("shared_down_ready")
        s_S = sem("slots_ready"); s_xp = sem("xT_in_psum"); s_xc = sem("xT_ready"); s_gu = sem("expert_up_ready")
        s_sl = sem("expert_silu_ready"); s_hid = sem("expert_hidden_ready"); s_htp = sem("hidden_and_gates_in_psum")
        s_hg = sem("hidden_and_gates_ready"); s_dn = sem("expert_down_ready"); s_yo = sem("expert_out_ready")
        s_add = sem("expert_out_added"); s_Sf = sem("slots_found"); s_acc = sem("residual_ready")
        o_w = sem("over_weights_loaded"); o_up = sem("over_up_ready"); o_sl = sem("over_silu_ready")
        o_h = sem("over_hidden_ready"); o_dn = sem("over_down_ready"); o_acc = sem("over_added")
        s_y = sem("out_ready"); s_out = sem("out_stored")
        q_v = sem("vector_order"); q_a = sem("scalar_order"); q_g = sem("gpsimd_order")

        def strip(w, c0, n=512):
            return w[:, c0:c0 + n].rearrange("(k p) n -> p k n", p=P)

        w_in2 = w_in[0]
        stream = [(strip(w_in2, COL_IDX, N_IDX_COLS), KD, N_IDX_COLS)]
        free_at = [3]
        for c0, last in ((0, 7), (512, 7), (COL_AQ, 9), (COL_AQ + 512, 11), (COL_RF, 13), (COL_RQ, 15),
                         (COL_RI, 17), (COL_RG, 19)):
            stream.append((strip(w_in2, c0), KD, 512))
            free_at.append(last)
        BRANCH = [(2, w_att_proj), (0, w_conv_proj), (1, w_rnn_proj)]
        T_BR = [19, 27, 35]
        for (g, w), t0 in zip(BRANCH, T_BR):
            stream.append((w[0].rearrange("(k p) n -> p k n", p=P), 4, D))
            free_at.append(t0 + 8)
            for half in range(2):
                stream.append((strip(w_in2, COL_GATE + g * D + half * 512), KD, 512))
                free_at.append(t0 + 4 * half + 4)
        I_BR = [9, 12, 15]
        I_OUT = 18
        T_OUT = 43
        for half in range(2):
            stream.append((strip(w_out[0], half * 512), KD, 512))
            free_at.append(T_OUT + 3 + half)
        I_SGU, I_SDN = 20, 21
        stream.append((strip(w_shared_gu[0], 0), KD, 512))
        stream.append((w_shared_dn[0].rearrange("(k p) n -> p k n", p=P), 2, D))
        T_SH = T_OUT + 4
        free_at += [T_SH + 2, None]
        assert len(stream) == 22

        def slot(n, k, w):
            s = n % WSLOTS
            return ring[:, s * SLOT:s * SLOT + k * w].rearrange("p (k n) -> p k n", k=k)

        def arrived(eng, n):
            eng.wait_ge(s_w[n % WSLOTS], 16 * (n // WSLOTS + 1))

        PAIR_SLOTS = [(6, 7, 8), (4, 5, 0), (1, 2, 3)]

        def wslot(s):
            return ring[:, s * SLOT:(s + 1) * SLOT] if s < WSLOTS else extra_slots[s - WSLOTS]

        def pair_item(i, q, j):
            s = PAIR_SLOTS[q][j]
            before_it = len([n for n in range(len(stream)) if n % WSLOTS == s])
            return s, (i + before_it + 1) * 16

        gu_d = w_expert_gu[0].rearrange("e (k p) n -> e p k n", p=P)
        dn_d = w_expert_dn[0].rearrange("e (f p) n -> e p f n", p=P)
        COUNT_MAX = SEQ

        def over(eng):
            eng.wait_ge(s_cnt, 1)
            return eng.value_load(count[0:1, 0:1], min_val=0, max_val=COUNT_MAX) > CAP

        prow = fz[:, 0:P]
        dw_rows = fz[:, P:P + 512]
        bdist = ls[:, 0:NDIST]
        buckets = ls[:, NDIST:2 * NDIST]
        relb = ls[:, 2 * NDIST:2 * NDIST + NH_A]
        B_RQ, B_RF, B_RG, B_AQ = COL_RQ // P, COL_RF // P, COL_RG // P, COL_AQ // P
        B_GATE, B_CB, B_CG, B_CLB, B_GAM, B_NG, B_QI, B_KI = 32, 56, 60, 64, 68, 72, 76, 78

        def col(i):
            return params[:, i:i + 1]

        lb_a, lb_ln = small[:, 0:4], small[:, 4:8]
        lb = small[:, 8:12]
        minus_half = small[:, 56:57]
        ssq, crs = small[:, 12:14], small[:, 14:16]
        rrs = small[:, 64:72]
        m8 = small[:, 16:24]
        nmax = small[:, 24:40]
        esum = small[:, 40:56]

        def after_first(eng, s, value, i):
            if not (isinstance(i, int) and i == 0):
                eng.wait_ge(s, value)

        block = ctx.enter_context(nc.Block())

        @block.sync
        def _(sp):
            for b in range(TB):
                sp.dma_start(h[:, b, :], x[0, b * P:(b + 1) * P, :]).then_inc(s_x, 16)
            sp.dma_start(prow[0:32, :], b_in[0, 0:4096].rearrange("(m p) -> m p", p=P)).then_inc(s_par, 16)
            sp.dma_start(prow[32:56, :], b_in[0, COL_GATE:COL_GATE + 3072].rearrange("(m p) -> m p", p=P)).then_inc(s_par, 16)
            for r, a in ((56, conv_b), (60, conv_ln_g), (64, conv_ln_b), (68, hgrn_gamma), (72, hgrn_norm_g)):
                sp.dma_start(prow[r:r + 4, :], a[0].rearrange("(m p) -> m p", p=P)).then_inc(s_par, 16)
            sp.dma_start(prow[76:78, :], b_in[0, COL_IDX + 128:COL_IDX + 384].rearrange("(m p) -> m p", p=P)).then_inc(s_par, 16)
            for z in range(2):
                sp.dma_start(prow[78:79, 64 * z:64 * z + 64],
                             b_in[0, COL_IDX + 384:COL_IDX + 448].rearrange("(m p) -> m p", p=64)).then_inc(s_par, 16)
            def load_item(i, q, j):
                s, _ = pair_item(0, q, j)
                if j < 2:
                    sp.dma_start(wslot(s).rearrange("p (k n) -> p k n", k=KD),
                                 gu_d[i * 6 + (2 * q + j)]).then_inc(s_w[s], 16)
                else:
                    sp.dma_start(wslot(s).rearrange("p (e f n) -> p e f n", e=2, f=2),
                                 dn_d[bass.ds(i * 6 + 2 * q, 2)].rearrange("e p f n -> p e f n")).then_inc(s_w[s], 16)

            def load_pair(i, q):
                for j in range(3):
                    sp.wait_ge(s_dn if j == 2 else s_gu, i * 3 + (q - 2))
                    load_item(i, q, j)

            for n, (src, k, w) in enumerate(stream):
                if n == 16:
                    sp.wait_ge(s_on, 1)
                    load_item(0, 0, 0)
                if n == 18:
                    sp.wait_ge(s_ot, 1)
                    load_item(0, 0, 2)
                if n >= WSLOTS:
                    sp.wait_ge(s_turn, free_at[n - WSLOTS])
                sp.dma_start(slot(n, k, w), src).then_inc(s_w[n % WSLOTS], 16)
            sp.wait_ge(s_turn, T_OUT)
            load_item(0, 0, 1)
            for q in range(1, 3):
                for j in range(3):
                    n = 16 + 3 * (q - 1) + j
                    if n < 21:
                        sp.wait_ge(s_turn, free_at[n])
                    else:
                        sp.wait_ge(s_sdn, 1)
                    load_item(0, q, j)
            with sp.Fori(1, NPAIR // 3) as i:
                for q in range(3):
                    load_pair(i, q)
            load_pair(NPAIR // 3, 0)
            with sp.If(over(sp)):
                sp.wait_ge(s_dn, NPAIR)

                def load(e):
                    after_first(sp, o_dn, e, e)
                    sp.dma_start(wslot(0).rearrange("p (k n) -> p k n", k=KD), gu_d[e]).then_inc(o_w, 16)
                    sp.dma_start(wslot(1)[:, 0:2 * D].rearrange("p (f n) -> p f n", f=2), dn_d[e]).then_inc(o_w, 16)

                load(0)
                with sp.Fori(1, NE) as e:
                    load(e)
            for b in range(TB):
                sp.wait_ge(s_y, b + 1)
                sp.dma_start(out[0, b * P:(b + 1) * P, :], h[:, b, :]).then_inc(s_out, 16)
            sp.wait_ge(s_out, 16 * TB)

        @block.gpsimd
        def _(pool_e):
            def rows(ap, n):
                return ap.rearrange("(a n) -> a n", a=1).to_broadcast((P, n))

            powers = [0]

            def power(t):
                powers[0] += 1
                pool_e.wait_ge(s_pin, powers[0])
                pool_e.tensor_tensor(t, t, minus_half.to_broadcast((P, t.shape[1])), ALU.pow).then_inc(s_pout, 1)

            pool_e.dma_start(dw_rows[0:TAPS, :], conv_dw[0]).then_inc(s_rp, 16)
            pool_e.dma_start(relb[0:NBUCKET, :], rel_bias).then_inc(s_rp, 16)
            pool_e.dma_start(buckets[0:NBUCKET, :], c_onehot).then_inc(s_rp, 16)
            pool_e.dma_start(row_bias[:, 0:128], rows(b_in[0, COL_IDX:COL_IDX + 128], 128)).then_inc(s_rp, 16)
            pool_e.dma_start(row_bias[:, 128:132], rows(b_in[0, COL_GATE - 4:COL_GATE], 4)).then_inc(s_rp, 16)
            pool_e.dma_start(ri_bias, rows(b_in[0, COL_RI:COL_RI + 512], 512)).then_inc(s_rp, 16)
            pool_e.dma_start(kvg, rows(kv_norm_g[0], 128)).then_inc(s_rp, 16)
            pool_e.memset(minus_half, -0.5).then_inc(q_g, 1)
            pool_e.wait_ge(q_g, 1)
            for b in range(TB):
                power(rstd[:, b:b + 1])
            pool_e.wait_ge(s_bd, 1)
            pool_e.dma_start(bias_ap, bdist[0:NH_A, :]).then_inc(s_bdd, 16)
            pool_e.wait_ge(s_bdd, 16)
            pool_e.dma_start(dist_bias, bass.AP(bias_by_dist, 0, [[1, P], [NDIST, NH_A], [1, SEQ]])).then_inc(s_T, 16)

            power(crs)
            pool_e.dma_start(kT.rearrange("p (n t) -> p n t", n=8), c_level).then_inc(s_lm, 16)
            pool_e.wait_ge(s_lm, 16)
            pool_e.tensor_copy(level_mask[:, :, :].rearrange("p n t -> p (n t)"), kT).then_inc(q_g, 1)
            pool_e.wait_ge(s_relu, 2)
            pool_e.dma_start(wuv, w_uv[0].rearrange("h c v -> c h v")).then_inc(s_uvl, 16)
            power(crs)
            power(rrs)
            pool_e.wait_ge(s_ot, 1)
            pool_e.dma_start(rw, router_w[0].rearrange("(k p) e -> p k e", p=P)).then_inc(s_ro, 16)
            pool_e.dma_start(rb, rows(router_b[0], NE)).then_inc(s_ro, 16)
            pool_e.wait_ge(s_turn, T_BR[1] + KD)
            for i, a in enumerate((ln_mix_g, ln_mix_b)):
                pool_e.dma_start(gb[:, i, :], rows(a[0], D)).then_inc(s_gb2, 16)
            pool_e.wait_ge(s_mg, 8)
            pool_e.iota(iota_c, [[1, CAP]], base=0, channel_multiplier=0,
                        allow_small_or_imprecise_dtypes=True).then_inc(q_g, 1)

            for b in range(TB):
                power(rstd[:, b:b + 1])
            pool_e.wait_ge(s_h2, TB)
            for i, a in enumerate((ln_ffn_g, ln_ffn_b)):
                pool_e.dma_start(gb[:, i, :], rows(a[0], D)).then_inc(s_gb3, 16)
            for b in range(TB):
                power(rstd[:, b:b + 1])

        @block.scalar
        def _(act):
            q = [0]

            def link(ins):
                q[0] += 1
                ins.then_inc(q_a, 1)
                act.wait_ge(q_a, q[0])

            for i, a in enumerate((ln_in_g, ln_in_b)):
                act.dma_start(gb[:, i, :], a.rearrange("(a n) -> a n", a=1).to_broadcast((P, D))).then_inc(s_gb, 16)
            act.dma_start(consts[:, :, :], c_f32).then_inc(s_con, 16)

            for i in range(2):
                act.wait_ge(s_hTp, 2 * i + 1)
                nc.scalar.copy(hT[:, 4 * i:4 * i + 2, :].rearrange("p k t -> p (k t)"), banks(2 + 2 * i)).then_inc(s_hT, 1)
            act.wait_ge(s_prT, 1)
            nc.scalar.copy(params[:, 0:79], banks(6)[:, 0:79]).then_inc(s_pr, 1)
            nc.scalar.copy(dw.rearrange("p c k -> p (c k)"), banks(7)[:, 0:4 * TAPS]).then_inc(s_pr, 1)
            nc.scalar.copy(bdist[0:NH_A, :], banks(6)[0:NH_A, 128:512]).then_inc(s_bd, 1)
            act.wait_ge(s_pr, 2)
            act.wait_ge(s_lbv, 1)
            nc.scalar.activation(lb, lb, ACT.Exp).then_inc(s_lba, 1)
            act.wait_ge(s_lbv, 2)
            nc.scalar.activation(lb_a, lb_a, ACT.Ln)
            link(nc.scalar.activation(lb_ln, lb, ACT.Ln, bias=1.0, scale=-1.0))
            act.sem_inc(s_lba, 1)

            def evac(t, outs, sem_out):
                act.wait_ge(s_turn, t + 1)
                for n, (dst, bias) in enumerate(outs):
                    ins = nc.scalar.activation(dst, banks(t % 2)[:, n * SEQ:(n + 1) * SEQ], ACT.Identity, bias=bias)
                    ins.then_inc(sem_out, 1)
                done[sem_out] = done.get(sem_out, 0) + len(outs)
                act.wait_ge(sem_out, done[sem_out])
                act.sem_inc(s_free[t % 2], 1)

            done = {}

            evac(1, [(qiT[:, 0, :], col(B_QI)), (qiT[:, 1, :], col(B_QI + 1))], s_qk)
            evac(2, [(kiT, col(B_KI))], s_qk)
            def conv_gate(c):
                t = 3 + c
                act.wait_ge(s_turn, t + 1)
                if c >= 2:
                    act.wait_ge(s_u, c - 1)
                nc.scalar.activation(gate_tmp[:, c % 2, :], banks(t % 2)[:, SEQ:2 * SEQ], ACT.Sigmoid,
                                     bias=col(4 + c)).then_inc(s_sig, 1)

            conv_gate(0)
            act.wait_ge(s_cTp, 1)
            nc.scalar.copy(cT, banks(5)[:, 0:SEQ]).then_inc(s_cT, 1)
            conv_gate(1)
            act.wait_ge(s_sc, 1)
            nc.scalar.activation(relu_i[:, :, 0:P].rearrange("p (y z) s -> p y z s", y=2),
                                 ps[:, 2:4, 0:2 * P].rearrange("p y (z s) -> p y z s", z=2),
                                 ACT.Relu).then_inc(s_relu, 1)
            conv_gate(2)
            act.wait_ge(s_sc, 2)
            act.wait_ge(s_reluf, 1)
            nc.scalar.activation(relu_i, banks(4, 2).rearrange("p (h s) -> p h s", h=NH_I),
                                 ACT.Relu).then_inc(s_relu, 1)
            conv_gate(3)
            for i in range(4):
                evac(7 + i, [(aqT[:, 2 * i + z, :], col(B_AQ + 2 * i + z)) for z in range(2)], s_aq)
            act.wait_ge(s_bdd, 16)
            for i in range(2):
                evac(11 + i, [(hd(fz, 2 * i + z), col(B_RF + 2 * i + z)) for z in range(2)], s_rf)
            def exps(b):
                lg, w = (logits0, P) if b == 0 else (logits1, SEQ)
                act.wait_ge(s_la, b + 1)
                for hh in range(NH_A):
                    ins = nc.scalar.activation(lg[:, hh, :], lg[:, hh, :], ACT.Exp, bias=nmax[:, 8 * b + hh:8 * b + hh + 1],
                                               accum_out=esum[:, 8 * b + hh:8 * b + hh + 1])
                ins.then_inc(s_ex, 1)

            exps(0)
            exps(1)
            act.wait_ge(s_hp, 1)
            link(nc.scalar.activation(cum, cum, ACT.Exp))
            nc.scalar.activation(cum, cum, ACT.Ln, bias=1.0).then_inc(s_ha, 1)
            evac(13, [(hd(qT, z), col(B_RQ + z)) for z in range(2)], s_rq)
            act.wait_ge(s_hp, 2)
            act.wait_ge(q_g, 2)
            for i in range(4):
                ins = nc.scalar.activation(hd(kT, i), hd(cum, i), ACT.Exp, bias=lb_ln[:, i:i + 1])
            ins.then_inc(s_ha, 1)
            act.wait_ge(s_hp, 3)
            link(nc.scalar.activation(fz, fz, ACT.Exp))
            nc.scalar.activation(fz, fz, ACT.Ln, bias=1.0).then_inc(s_ha, 1)
            evac(14, [(hd(qT, 2 + z), col(B_RQ + 2 + z)) for z in range(2)], s_rq)

            for n, bk in enumerate((2, 6, 2)):
                act.wait_ge(s_pTp, n + 1)
                nc.scalar.copy(probsT[:, n].rearrange("p h t -> p (h t)"), banks(bk, 2)).then_inc(s_pT, 1)
            for b in range(TB):
                act.wait_ge(s_oTp, b + 1)
                for half in range(2):
                    ins = nc.scalar.copy(oT_att[:, 4 * half:4 * half + 4, b * P:(b + 1) * P],
                                         banks(4 + half).rearrange("p (h t) -> p h t", h=4))
                ins.then_inc(s_oT, 1)
            for i in range(2):
                t = 17 + i
                act.wait_ge(s_turn, t + 1)
                for z in range(2):
                    ins = nc.scalar.activation(hd(sgT, 2 * i + z), banks(t % 2)[:, z * SEQ:(z + 1) * SEQ], ACT.Sigmoid,
                                               bias=col(B_RG + 2 * i + z))
                    ins.then_inc(s_rg, 1)
                act.wait_ge(s_rg, 2 * i + 2)
                act.sem_inc(s_free[t % 2], 1)
            act.wait_ge(s_uvp, 1)
            nc.scalar.copy(aT.rearrange("p c t -> p (c t)"), banks(6, 2)).then_inc(s_aT, 1)

            def branch_gate(br, m):
                t = T_BR[br] + m
                n = 8 * br + m
                act.wait_ge(s_turn, t + 1)
                if n >= 2:
                    act.wait_ge(s_mg, n - 1)
                else:
                    act.wait_ge(s_u, 3 + n)
                nc.scalar.activation(gate_tmp[:, n % 2, :], banks(t % 2)[:, 0:SEQ], ACT.Tanh, scale=0.5,
                                     bias=col(B_GATE + 8 * BRANCH[br][0] + m)).then_inc(s_sig, 1)

            def decay(lv):
                act.wait_ge(s_dl, lv + 1)
                e = (fz, ls)[lv % 2]
                nc.scalar.activation(e, e, ACT.Exp).then_inc(s_el, 1)

            decay(0)
            for m in range(KD):
                if m < 7:
                    decay(m + 1)
                branch_gate(0, m)
                if m == 6:
                    act.wait_ge(s_cn, 1)
                    for c in range(4):
                        ins = nc.scalar.activation(conv[:, c, :], conv[:, c, :], ACT.Silu, bias=col(B_CLB + c), scale=col(B_CG + c))
                    ins.then_inc(s_cT2, 1)
            for m in range(KD):
                branch_gate(1, m)
                if m == 0:
                    act.wait_ge(s_on, 1)
                    nc.scalar.activation(fz, banks(6, 2), ACT.Square).then_inc(s_osq, 1)
            for m in range(KD):
                branch_gate(2, m)

            act.wait_ge(s_h2Tp, 1)
            nc.scalar.copy(hT[:, :, 0:P], banks(2, 2).rearrange("p (k t) -> p k t", k=KD)).then_inc(s_h2T, 1)
            act.wait_ge(s_h2Tp, 2)
            nc.scalar.copy(hT[:, 0:4, P:SEQ], banks(4).rearrange("p (k t) -> p k t", k=4)).then_inc(s_h2T, 1)
            act.wait_ge(s_rl, 1)
            nc.scalar.activation(scores.rearrange("p b e -> p (b e)"), banks(2)[:, 0:2 * NE], ACT.Sigmoid).then_inc(s_rsg, 1)
            act.wait_ge(s_turn, T_SH + 1)
            nc.scalar.activation(silu_s.rearrange("p f t -> p (f t)"), banks(T_SH % 2), ACT.Silu).then_inc(s_ssl, 1)
            act.wait_ge(s_ssl, 1)
            act.sem_inc(s_free[T_SH % 2], 1)
            act.wait_ge(s_xp, 1)
            nc.scalar.copy(xT.rearrange("p k s -> p (k s)"), banks(0, 2)).then_inc(s_xc, 1)

            def pair(i, q, last=False):
                p = i * 3 + q
                act.wait_ge(s_gu, p + 1)
                if not (isinstance(p, int) and p == 0):
                    act.wait_ge(s_hid, p)
                nc.scalar.activation(silu_e, banks(2)[:, 0:F_E], ACT.Silu).then_inc(s_sl, 1)
                if not last:
                    act.wait_ge(s_xp, p + 2)
                    nc.scalar.copy(xT.rearrange("p k s -> p (k s)"), banks(0, 2)).then_inc(s_xc, 1)
                act.wait_ge(s_htp, p + 1)
                if not (isinstance(p, int) and p < 3):
                    act.wait_ge(s_add, p - 2)
                nc.scalar.copy(hg[q], banks(3)).then_inc(s_hg, 1)

            for q in range(3):
                pair(0, q)
            with act.Fori(1, NPAIR // 3) as i:
                for q in range(3):
                    pair(i, q)
            pair(NPAIR // 3, 0, last=True)
            with act.If(over(act)):

                def over_silu(e):
                    act.wait_ge(o_up, e + 1)
                    after_first(act, o_h, e, e)
                    nc.scalar.activation(silu_s.rearrange("p f t -> p (f t)"), banks(0), ACT.Silu).then_inc(o_sl, 1)

                over_silu(0)
                with act.Fori(1, NE) as e:
                    over_silu(e)

        @block.vector
        def _(dve):
            q = [0]
            V = nc.vector

            def step(ins):
                q[0] += 1
                ins.then_inc(q_v, 1)

            def sync():
                dve.wait_ge(q_v, q[0])

            def link(ins):
                step(ins)
                sync()

            def rsqrt(dst, src, scale=1.0, eps=EPS):
                rs[0] += 1
                V.tensor_scalar(dst, src, scale, eps, ALU.mult, ALU.add).then_inc(s_pin, 1)
                dve.wait_ge(s_pout, rs[0])

            rs = [0]

            def layer_norm(t, i, done, eps=EPS, stats_done=False):
                if not stats_done:
                    for half in range(2):
                        step(V.bn_stats(stats[:, 2 * i + half, :], t[:, half * 512:(half + 1) * 512]))
                sync()
                link(V.bn_aggr(mv[:, i, :], stats[:, 2 * i:2 * i + 2, :].rearrange("p a s -> p (a s)")))
                rsqrt(rstd[:, i:i + 1], mv[:, i, 1:2], eps=eps)
                link(V.tensor_scalar(t, t, mv[:, i, 0:1], rstd[:, i:i + 1], ALU.subtract, ALU.mult))
                link(V.tensor_tensor(t, t, gb[:, 0, :], ALU.mult))
                V.tensor_tensor(t, t, gb[:, 1, :], ALU.add).then_inc(done, 1)

            dve.wait_ge(s_gb, 32)
            dve.wait_ge(s_x, 32)
            for b in range(TB):
                layer_norm(h[:, b, :], b, s_h)
            dve.wait_ge(s_h, 2)
            step(V.memset(u_pad[:, :, 0:TAPS - 1], 0.0))
            for i in range(2):
                dve.wait_ge(s_hTp, 2 * i + 2)
                V.tensor_copy(hT[:, 4 * i + 2:4 * i + 4, :].rearrange("p k t -> p (k t)"), banks(3 + 2 * i)).then_inc(s_hT, 1)

            dve.wait_ge(s_pr, 1)
            link(V.tensor_scalar(params[:, B_GATE:B_GATE + 24], params[:, B_GATE:B_GATE + 24], 0.5, None, ALU.mult))
            link(V.tensor_tensor(lb, params[:, B_GAM:B_GAM + 4], params[:, B_GAM:B_GAM + 4], ALU.subtract))
            dve.sem_inc(s_lbv, 1)
            dve.wait_ge(s_lba, 1)
            link(V.reciprocal(lb_ln, lb))
            link(V.tensor_tensor(lb, lb, lb_ln, ALU.mult))
            link(V.tensor_tensor(lb, lb, lb, ALU.subtract))
            link(V.tensor_scalar(lb_a, lb, TINY, None, ALU.max))
            dve.sem_inc(s_lbv, 1)
            dve.wait_ge(s_lba, 2)
            link(V.tensor_scalar(lb, lb, TINY, OFF, ALU.is_lt, ALU.mult))
            link(V.tensor_tensor(lb_a, lb_a, lb, ALU.add))

            dve.wait_ge(s_turn, 1)
            dve.wait_ge(s_rp, 16 * 7)
            for b in range(TB):
                step(V.tensor_tensor(c_tok_major[:, b, :], banks(0)[:, 256 * b:256 * b + 128], row_bias[:, 0:128], ALU.add))
                step(V.tensor_tensor(wi[:, b, :], banks(0)[:, 256 * b + 128:256 * b + 132], row_bias[:, 128:132], ALU.add))
            sync()
            dve.sem_inc(s_free[0], 1)
            for b in range(TB):
                step(V.scalar_tensor_tensor(cum[:, 128 * b:128 * b + 128], c_tok_major[:, b, :], 1.0, c_tok_major[:, b, :],
                                            ALU.mult, ALU.mult))
            sync()
            link(V.tensor_reduce(ssq, cum[:, 0:256].rearrange("p (b c) -> p b c", b=TB), AX.X, ALU.add))
            rsqrt(crs, ssq, 1.0 / P)
            for b in range(TB):
                V.scalar_tensor_tensor(c_tok_major[:, b, :], c_tok_major[:, b, :], crs[:, b:b + 1], kvg,
                                       ALU.mult, ALU.mult).then_inc(s_cr, 1)

            def conv_in(c):
                t = 3 + c
                dve.wait_ge(s_sig, c + 1)
                V.scalar_tensor_tensor(u_pad[:, c, TAPS - 1:UW], banks(t % 2)[:, 0:SEQ], col(c),
                                       gate_tmp[:, c % 2, :], ALU.add, ALU.mult).then_inc(s_u, 1)
                dve.wait_ge(s_u, c + 1)
                dve.sem_inc(s_free[t % 2], 1)

            def top_keys(b):
                w = (b + 1) * P
                sc = score[:, 0:w]
                dve.wait_ge(s_relu, b + 1)
                link(V.tensor_scalar(sc, relu_i[:, 0, 0:w], wi[:, b, 0:1], None, ALU.mult))
                for hh in range(1, NH_I):
                    w_h = 2 * (hh % 2) + hh // 2
                    ins = V.scalar_tensor_tensor(sc, relu_i[:, hh, 0:w], wi[:, b, w_h:w_h + 1], sc, ALU.mult, ALU.add)
                    if hh < NH_I - 1:
                        link(ins)
                ins.then_inc(s_reluf, 1)
                dve.wait_ge(s_reluf, b + 1)
                link(V.tensor_tensor(score[:, b * P:w], score[:, b * P:w], can, ALU.min))
                for _ in range(TOPK // 8):
                    link(V.max(m8, sc))
                    link(V.match_replace(sc, m8, sc, TAKEN))
                link(V.tensor_scalar(sel_add[:, b, 0:w], sc, (BANNED + TAKEN) / 2, OFF, ALU.is_gt, ALU.mult))
                link(V.tensor_tensor(sel_add[:, b, b * P:w], sel_add[:, b, b * P:w], never, ALU.add))

            dve.wait_ge(s_con, 16)
            dve.wait_ge(s_pr, 2)
            conv_in(0)
            conv_in(1)
            top_keys(0)
            conv_in(2)
            conv_in(3)
            top_keys(1)
            def conv_taps(first, end):
                sync()
                since = q[0]
                for k in range(first, end):
                    for c in range(4):
                        src = u_pad[:, c, k:k + SEQ]
                        if k == 0:
                            ins = V.tensor_scalar(conv[:, c, :], src, dw[:, c, 0:1], col(B_CB + c), ALU.mult, ALU.add)
                        else:
                            if q[0] - 3 > since:
                                dve.wait_ge(q_v, q[0] - 3)
                            ins = V.scalar_tensor_tensor(conv[:, c, :], src, dw[:, c, k:k + 1], conv[:, c, :], ALU.mult, ALU.add)
                        if k == TAPS - 1 and c == 3:
                            ins.then_inc(s_conv, 1)
                        else:
                            step(ins)

            conv_taps(0, TAPS_FIRST)
            dve.wait_ge(s_T, 16)
            for b, (lg, w, bk) in enumerate(((logits0, P, 2), (logits1, SEQ, 4))):
                dve.wait_ge(s_lg, b + 1)
                nb = w // P
                src = banks(bk, 2 * nb).rearrange("p (h s) -> p h s", h=NH_A)
                tb_ = dist_bias[:, :, 0:w][:, :, ::-1]
                link(V.scalar_tensor_tensor(lg, src, float(P) ** -0.5, tb_, ALU.mult, ALU.add))
                link(V.tensor_tensor(lg, lg, sel_add[:, b:b + 1, 0:w].to_broadcast((P, NH_A, w)), ALU.add))
                V.tensor_reduce(nmax[:, 8 * b:8 * b + 8], lg, AX.X, ALU.max, negate=True).then_inc(s_la, 1)

            dve.wait_ge(s_rf, 4)
            V.scalar_tensor_tensor(cum, fz, -1.0, fz, ALU.mult, ALU.min).then_inc(s_hp, 1)
            for b, (lg, w) in enumerate(((logits0, P), (logits1, SEQ))):
                dve.wait_ge(s_ex, b + 1)
                link(V.reciprocal(esum[:, 8 * b:8 * b + 8], esum[:, 8 * b:8 * b + 8]))
                V.tensor_tensor(lg, lg, esum[:, 8 * b:8 * b + 8].rearrange("p (h o) -> p h o", o=1).to_broadcast((P, NH_A, w)),
                                ALU.mult).then_inc(s_pn, 1)
            dve.wait_ge(s_ha, 1)
            link(V.scalar_tensor_tensor(ls, fz, 0.0, cum, ALU.min, ALU.subtract))
            V.tensor_tensor(cum, ls, fz, ALU.subtract).then_inc(s_hp, 1)
            dve.wait_ge(s_hp, 2)
            for i in range(4):
                step(V.tensor_scalar(hd(ls, i), hd(ls, i), lb_ln[:, i:i + 1], None, ALU.add))
            sync()
            for i in range(4):
                step(V.tensor_scalar(hd(fz, i), hd(ls, i), lb_a[:, i:i + 1], None, ALU.subtract))
            sync()
            V.scalar_tensor_tensor(fz, fz, -1.0, fz, ALU.mult, ALU.min).then_inc(s_hp, 1)
            dve.wait_ge(s_ha, 3)
            for i in range(4):
                step(V.scalar_tensor_tensor(hd(ls, i), hd(ls, i), lb_a[:, i:i + 1], hd(fz, i), ALU.max, ALU.add))
            sync()
            for n in range(8):
                step(V.tensor_tensor_scan(cum[:, n * P:(n + 1) * P], ones, ls[:, n * P:(n + 1) * P], 0.0, ALU.mult, ALU.add))
            sync()
            for b in range(TB):
                t = 15 + b
                dve.wait_ge(s_turn, t + 1)
                V.tensor_tensor(v_tok[:, b, :], banks(t % 2), ri_bias, ALU.add).then_inc(s_rv, 1)
                dve.wait_ge(s_rv, b + 1)
                dve.sem_inc(s_free[t % 2], 1)
                if b == 0:
                    conv_taps(TAPS_FIRST, TAPS_SECOND)
            conv_taps(TAPS_SECOND, TAPS)

            def level_diff(lv):
                d = (fz, ls)[lv % 2]
                if lv < 7:
                    half = HALVES[lv]
                    a = cum.rearrange("p (n w) -> p n w", w=2 * half)
                    dd = d.rearrange("p (n w) -> p n w", w=2 * half)
                    mid = a[:, :, half - 1:half].to_broadcast((P, SEQ * 4 // (2 * half), 2 * half))
                    link(V.tensor_tensor(dd, a, mid, ALU.subtract))
                    V.scalar_tensor_tensor(d, d, -1.0, d, ALU.mult, ALU.min).then_inc(s_dl, 1)
                else:
                    a = cum.rearrange("p (h t) -> p h t", h=NH_R)
                    dd = d.rearrange("p (h t) -> p h t", h=NH_R)
                    mid = a[:, :, P - 1:P].to_broadcast((P, NH_R, P))
                    step(V.tensor_tensor(dd[:, :, 0:P], a[:, :, 0:P], mid, ALU.subtract))
                    step(V.tensor_copy(dd[:, :, P:SEQ], a[:, :, P:SEQ]))
                    sync()
                    V.scalar_tensor_tensor(d, d, -1.0, d, ALU.mult, ALU.min).then_inc(s_dl, 1)

            def level_xy(lv):
                e = (fz, ls)[lv % 2]
                dve.wait_ge(s_el, lv + 1)
                if lv >= 2:
                    dve.wait_ge(s_pl, lv - 1 + 1)
                step(V.tensor_tensor(Xl[lv % 2], e, qT, ALU.mult))
                V.tensor_tensor(Yl[lv % 2], e, kT, ALU.mult).then_inc(s_xy, 1)

            inner_f = inner.rearrange("p h c t -> p (h c) t")

            def take(n):
                bk = 2 + 2 * (n % 2)
                dve.wait_ge(s_pl, n + 1)
                m = level_mask[:, n:n + 1, :].to_broadcast((P, 8, P))
                V.copy_predicated(inner_f, m, banks(bk, 2).rearrange("p (n t) -> p n t", n=8)).then_inc(s_pc, 1)

            def merge(br, m):
                n = 8 * br + m
                t = T_BR[br] + m
                dve.wait_ge(s_sig, 4 + n + 1)
                y = banks(t % 2)[:, SEQ:2 * SEQ]
                if br == 0:
                    V.scalar_tensor_tensor(merged[:, m, :], gate_tmp[:, n % 2, :], 1.0, y, ALU.add, ALU.mult).then_inc(s_mg, 1)
                    dve.wait_ge(s_mg, n + 1)
                    dve.sem_inc(s_free[t % 2], 1)
                else:
                    link(V.scalar_tensor_tensor(gate_tmp[:, n % 2, :], gate_tmp[:, n % 2, :], 1.0, y, ALU.add, ALU.mult))
                    dve.sem_inc(s_free[t % 2], 1)
                    V.tensor_tensor(merged[:, m, :], merged[:, m, :], gate_tmp[:, n % 2, :], ALU.add).then_inc(s_mg, 1)

            def diagonals(dst, cols, n):
                return V.tensor_tensor(dst.rearrange("p (n t) -> p n t", n=n), consts[:, 0:1, :].to_broadcast((P, n, P)),
                                       cols.rearrange("p (n o) -> p n o", o=1).to_broadcast((P, n, P)), ALU.mult)

            def over_blocks(row):
                return row.rearrange("p (o t) -> p o t", o=1).to_broadcast((P, 4, SEQ))

            dve.wait_ge(s_uvp, 1)
            link(V.memset(t_region[:, 0:1024], 0.0))
            dve.wait_ge(s_rq, 4)
            dve.wait_ge(s_ha, 3)
            level_diff(0)
            dve.wait_ge(s_dl, 1)
            for m in range(KD):
                level_xy(m)
                if m < 7:
                    level_diff(m + 1)
                take(m)
                merge(0, m)
                if m == 1:
                    dve.wait_ge(s_mean, 1)
                    V.tensor_tensor(conv, conv, over_blocks(banks(7)[:, 0:SEQ]), ALU.subtract).then_inc(s_cen, 1)
                    dve.wait_ge(s_cen, 1)
                    V.tensor_tensor(conv_sq, conv, conv, ALU.mult).then_inc(s_sqr, 1)
                if m == 3:
                    dve.wait_ge(s_var, 1)
                    rsqrt(crs, banks(7)[:, SEQ:SEQ + TB])
                    diagonals(cvs[:, 0:SEQ], crs, TB).then_inc(s_cdg, 1)
                if m == 5:
                    dve.wait_ge(s_csp, 1)
                    V.tensor_tensor(conv, conv, over_blocks(banks(7)[:, SEQ:2 * SEQ]), ALU.mult).then_inc(s_cn, 1)
            dve.wait_ge(s_pl, 9)
            V.tensor_copy(inter.rearrange("p h t -> p (h t)"), banks(2)).then_inc(s_pc, 1)
            for m in range(KD):
                merge(1, m)
                if m == 2:
                    dve.wait_ge(s_ms, 1)
                    rsqrt(rrs, banks(2)[:, 0:8])
                    diagonals(ls, rrs, 8).then_inc(s_rdg, 1)
                if m == 4:
                    dve.wait_ge(s_rsp, 1)
                    link(V.tensor_tensor(ls, banks(4, 2), sgT, ALU.mult))
                    for i in range(4):
                        ins = V.scalar_tensor_tensor(oT_rnn[:, i, :], banks(6, 2)[:, i * SEQ:(i + 1) * SEQ],
                                                     col(B_NG + i), hd(ls, i), ALU.mult, ALU.mult)
                        if i < 3:
                            step(ins)
                    ins.then_inc(s_ot, 1)
            for m in range(KD):
                merge(2, m)

            for b in range(TB):
                for half in range(2):
                    n = 2 * b + half
                    t = T_OUT + n
                    dve.wait_ge(s_turn, t + 1)
                    hh = h[:, b, half * 512:(half + 1) * 512]
                    V.scalar_tensor_tensor(hh, hh, 2 * ALPHA, banks(t % 2), ALU.mult, ALU.add).then_inc(s_rs, 1)
                    dve.wait_ge(s_rs, n + 1)
                    dve.sem_inc(s_free[t % 2], 1)
                    step(V.bn_stats(stats[:, 2 * b + half, :], hh))
                if b == 0:
                    dve.wait_ge(s_gb2, 32)
                layer_norm(h[:, b, :], b, s_h2, eps=4 * EPS, stats_done=True)
            dve.wait_ge(s_h2Tp, 2)
            V.tensor_copy(hT[:, 4:8, P:SEQ], banks(5).rearrange("p (k t) -> p k t", k=4)).then_inc(s_h2T, 1)

            dve.wait_ge(s_rsg, 1)
            dve.wait_ge(s_ro, 32)
            dve.wait_ge(q_g, 3)
            link(V.tensor_tensor(biased, scores, rb.rearrange("p (o e) -> p o e", o=1).to_broadcast((P, TB, NE)), ALU.add))
            for b in range(TB):
                step(V.max(top8[:, b, :], biased[:, b, :]))
            sync()
            link(V.memset(top8[:, :, TOPE:8], -BANNED))
            for b in range(TB):
                step(V.match_replace(biased[:, b, :], top8[:, b, :], biased[:, b, :], TAKEN))
            sync()
            V.tensor_scalar(sel, biased, (BANNED + TAKEN) / 2, None, ALU.is_lt).then_inc(s_sel, 1)
            dve.wait_ge(s_sel, 1)
            link(V.tensor_tensor(gate, scores, sel, ALU.mult))
            link(V.tensor_reduce(wsum, gate, AX.X, ALU.add))
            link(V.reciprocal(wsum, wsum))
            link(V.scalar_tensor_tensor(gate, gate, ROUTE_SCALE, wsum.rearrange("p (b o) -> p b o", o=1).to_broadcast((P, TB, NE)),
                                        ALU.mult, ALU.mult))
            link(V.tensor_scalar(rank_in, sel, -1000.0, 1000.0, ALU.mult, ALU.add))
            dve.wait_ge(s_rk, 1)
            link(V.tensor_tensor(rank_in, rank_in, banks(3)[:, 0:2 * NE].rearrange("p (b e) -> p b e", b=TB), ALU.add))

            def find_slots(n, e0, q_n):
                full = (P, 2, CAP)
                experts = slice(e0, e0 + 2) if isinstance(e0, int) else bass.ds(e0, 2)
                so = slot_of[q_n].rearrange("p b (e c) -> p b e c", e=2)
                sg = slot_gate[q_n].rearrange("p b (e c) -> p b e c", e=2)
                for b in range(TB):
                    V.tensor_tensor(so[:, b], rank_in[:, b, experts].rearrange("p (e o) -> p e o", o=1).to_broadcast(full),
                                    iota_c.rearrange("p (o c) -> p o c", o=1).to_broadcast(full), ALU.is_equal).then_inc(s_Sf, 1)
                dve.wait_ge(s_Sf, n * 2 + 2)
                for b in range(TB):
                    V.tensor_tensor(sg[:, b], so[:, b], gate[:, b, experts].rearrange("p (e o) -> p e o", o=1).to_broadcast(full),
                                    ALU.mult).then_inc(s_S, 1)

            find_slots(0, 0, 0)
            link(V.tensor_reduce(cmax[0:1, :], banks(3)[0:1, 64:64 + NE], AX.X, ALU.max))
            V.tensor_copy(count[:, :], cmax[0:1, :]).then_inc(s_cnt, 1)

            dve.wait_ge(s_ssl, 1)
            dve.wait_ge(s_turn, T_SH + 2)
            V.tensor_tensor(hid_s.rearrange("p f t -> p (f t)"), silu_s.rearrange("p f t -> p (f t)"), banks((T_SH + 1) % 2),
                            ALU.mult).then_inc(s_sh, 1)
            link(V.tensor_scalar(g_over, rank_in, float(CAP), None, ALU.is_ge))
            link(V.tensor_tensor(g_over, g_over, gate, ALU.mult))

            def pair(i, q_, last=False):
                p = i * 3 + q_
                if not last:
                    if not (isinstance(p, int) and p < 2):
                        dve.wait_ge(s_htp, p - 1)
                    find_slots(p + 1, i * 6 + (2 * q_ + 2), (q_ + 1) % 3)
                dve.wait_ge(s_sl, p + 1)
                if not (isinstance(p, int) and p == 0):
                    dve.wait_ge(s_htp, p)
                V.tensor_tensor(hid, silu_e, banks(2)[:, F_E:2 * F_E], ALU.mult).then_inc(s_hid, 1)
                dve.wait_ge(s_dn, p + 1)
                if not (isinstance(p, int) and p == 0):
                    dve.wait_ge(s_add, p)
                V.tensor_copy(yo, banks(0, 2)).then_inc(s_yo, 1)

            for q_ in range(3):
                pair(0, q_)
            with dve.Fori(1, NPAIR // 3) as i:
                for q_ in range(3):
                    pair(i, q_)
            pair(NPAIR // 3, 0, last=True)
            for b in range(TB):
                dve.wait_ge(s_add, NPAIR + b)
                V.scalar_tensor_tensor(h[:, b, :], h[:, b, :], ALPHA, banks(4 + 2 * b, 2), ALU.mult, ALU.add).then_inc(s_acc, 1)
            with dve.If(over(dve)):
                dve.wait_ge(s_acc, TB)
                with dve.Fori(0, NE) as e:
                    dve.wait_ge(o_sl, e + 1)
                    V.tensor_tensor(hid_s.rearrange("p f t -> p (f t)"), silu_s.rearrange("p f t -> p (f t)"), banks(1),
                                    ALU.mult).then_inc(o_h, 1)
                    dve.wait_ge(o_dn, e + 1)
                    for b in range(TB):
                        V.scalar_tensor_tensor(h[:, b, :], banks(4 + 2 * b, 2), g_over[:, b, bass.ds(e, 1)], h[:, b, :],
                                               ALU.mult, ALU.add).then_inc(o_acc, 1)
                    dve.wait_ge(o_acc, e * 2 + 2)
            dve.wait_ge(s_acc, TB)
            dve.wait_ge(s_gb3, 32)
            for b in range(TB):
                layer_norm(h[:, b, :], b, s_y)

        @block.tensor
        def _(pe):
            T = nc.tensor
            turns_on = [0, 0]

            def start_turn(t):
                if turns_on[t % 2]:
                    pe.wait_ge(s_free[t % 2], turns_on[t % 2])
                turns_on[t % 2] += 1

            def transpose_h(ready, done):
                for bank in range(4):
                    for kk in range(2):
                        for b in range(TB):
                            if bank == 0 and kk == 0:
                                pe.wait_ge(ready, b + 1)
                            ins = T.transpose(banks(2 + bank)[:, kk * SEQ + b * P:kk * SEQ + (b + 1) * P],
                                              h[:, b, (2 * bank + kk) * P:(2 * bank + kk + 1) * P], ident)
                    ins.then_inc(done, 1)

            def feat(dst, w, c0, m=P, src=hT, nk=KD):
                for k in range(nk):
                    ins = T.matmul(dst, w[:, k, c0:c0 + m], src[:, k, :], start=(k == 0), stop=(k == nk - 1))
                return ins

            def tokm(dst, w, c0, n, b, src=hT, nk=KD):
                for k in range(nk):
                    ins = T.matmul(dst, src[:, k, b * P:(b + 1) * P], w[:, k, c0:c0 + n], start=(k == 0), stop=(k == nk - 1))
                return ins

            pe.wait_ge(s_par, 16 * 10)
            pe.wait_ge(s_rp, 16 * 7)
            pe.wait_ge(s_con, 16)
            T.transpose(banks(6)[:, 0:79], prow[0:79, :], consts[0:79, 0, 0:79])
            for c in range(4):
                T.transpose(banks(7)[:, c * TAPS:(c + 1) * TAPS], dw_rows[0:TAPS, c * P:(c + 1) * P], consts[0:TAPS, 0, 0:TAPS])
            T.matmul(banks(6)[0:NH_A, 128:512], relb[0:NBUCKET, :], buckets[0:NBUCKET, :], start=True, stop=True).then_inc(s_prT, 1)
            transpose_h(s_h, s_hTp)
            pe.wait_ge(s_hT, 4)

            arrived(pe, 0)
            wI = slot(0, KD, N_IDX_COLS)
            start_turn(0)
            for b in range(TB):
                tokm(banks(0)[:, 256 * b:256 * b + 128], wI, 0, 128, b)
                ins = tokm(banks(0)[:, 256 * b + 128:256 * b + 132], wI, 448, 4, b)
            ins.then_inc(s_turn, 1)
            start_turn(1)
            feat(banks(1)[:, 0:SEQ], wI, 128)
            feat(banks(1)[:, SEQ:2 * SEQ], wI, 256).then_inc(s_turn, 1)
            start_turn(2)
            feat(banks(0)[0:64, 0:SEQ], wI, 384, m=64)
            feat(banks(0)[64:128, 0:SEQ], wI, 384, m=64).then_inc(s_turn, 1)
            arrived(pe, 1)
            arrived(pe, 2)
            for c in range(4):
                t = 3 + c
                start_turn(t)
                feat(banks(t % 2)[:, 0:SEQ], slot(1, KD, 512), c * P)
                feat(banks(t % 2)[:, SEQ:2 * SEQ], slot(2, KD, 512), c * P).then_inc(s_turn, 1)
                if c == 0:
                    pe.wait_ge(s_cr, 2)
                    for b in range(TB):
                        ins = T.transpose(banks(5)[:, b * P:(b + 1) * P], c_tok_major[:, b, :], ident)
                    ins.then_inc(s_cTp, 1)
                if c == 1:
                    pe.wait_ge(s_qk, 3)
                    pe.wait_ge(s_cT, 1)
                    for b in range(TB):
                        w = (b + 1) * P
                        for hh in range(NH_I):
                            lo = 64 * (hh % 2)
                            ins = T.matmul(banks(2 + 2 * b + hh % 2)[:, hh // 2 * w:(hh // 2 + 1) * w],
                                           qiT[lo:lo + 64, hh // 2, b * P:(b + 1) * P], kiT[lo:lo + 64, 0:w],
                                           start=True, stop=True)
                        ins.then_inc(s_sc, 1)

            def two_blocks(t, item, c0):
                arrived(pe, item)
                start_turn(t)
                w = slot(item, KD, 512)
                feat(banks(t % 2)[:, 0:SEQ], w, c0)
                feat(banks(t % 2)[:, SEQ:2 * SEQ], w, c0 + P).then_inc(s_turn, 1)

            for i in range(4):
                two_blocks(7 + i, 3 + i // 2, 256 * (i % 2))
            for i in range(2):
                two_blocks(11 + i, 5, 256 * i)
            pe.wait_ge(s_aq, 8)
            pe.wait_ge(s_cT, 1)
            pe.wait_ge(s_relu, 2)
            for b, bk in ((0, 2), (1, 4)):
                w = (b + 1) * P
                for hh in range(NH_A):
                    ins = T.matmul(banks(bk, 2 * (b + 1))[:, hh * w:(hh + 1) * w], aqT[:, hh, b * P:(b + 1) * P], cT[:, 0:w],
                                   start=True, stop=True)
                ins.then_inc(s_lg, 1)
            for i in range(2):
                two_blocks(13 + i, 6, 256 * i)

            def probs_T(n, b, sblk, bk):
                lg = logits0 if b == 0 else logits1
                pe.wait_ge(s_pn, b + 1)
                if n == 2:
                    pe.wait_ge(s_pT, 1)
                for hh in range(NH_A):
                    ins = T.transpose(banks(bk, 2)[:, hh * P:(hh + 1) * P], lg[:, hh, sblk * P:(sblk + 1) * P], ident)
                ins.then_inc(s_pTp, 1)

            for b in range(TB):
                t = 15 + b
                arrived(pe, 7)
                start_turn(t)
                tokm(banks(t % 2), slot(7, KD, 512), 0, 512, b).then_inc(s_turn, 1)
                if b == 0:
                    probs_T(0, 0, 0, 2)
                    probs_T(1, 1, 0, 6)
            probs_T(2, 1, 1, 2)
            two_blocks(17, 8, 0)
            for b in range(TB):
                pe.wait_ge(s_pT, 1 if b == 0 else 3)
                if b == 1:
                    pe.wait_ge(s_oT, 1)
                for half in range(2):
                    for s_ in range(b + 1):
                        ins = T.matmul(banks(4 + half), c_tok_major[:, s_, :],
                                       probsT[:, b + s_, 4 * half:4 * half + 4, :].rearrange("p h t -> p (h t)"),
                                       start=(s_ == 0), stop=(s_ == b))
                ins.then_inc(s_oTp, 1)
            two_blocks(18, 8, 256)
            pe.wait_ge(s_oT, 2)
            pe.wait_ge(s_uvl, 16)
            for hh in range(NH_A):
                lo = 64 * (hh % 2)
                ins = T.matmul(banks(6, 2)[lo:lo + 64, (hh // 2) * SEQ:(hh // 2 + 1) * SEQ], wuv[:, hh, :], oT_att[:, hh, :],
                               start=True, stop=True)
            ins.then_inc(s_uvp, 1)

            def level(n):
                bk = 2 + 2 * (n % 2)
                if n >= 2:
                    pe.wait_ge(s_pc, n - 1)
                if n == 0:
                    pe.wait_ge(s_rq, 4)
                    pe.wait_ge(s_ha, 2)
                    X, Y = qT, kT
                else:
                    pe.wait_ge(s_xy, n)
                    X, Y = Xl[(n - 1) % 2], Yl[(n - 1) % 2]
                if n < 8:
                    for m in range(8):
                        ins = T.matmul(banks(bk, 2)[:, m * P:(m + 1) * P], Y[:, m * P:(m + 1) * P], X[:, m * P:(m + 1) * P],
                                       start=True, stop=True)
                else:
                    for m in range(NH_R):
                        ins = T.matmul(banks(bk)[:, m * P:(m + 1) * P], Y[:, 2 * m * P:(2 * m + 1) * P],
                                       X[:, (2 * m + 1) * P:(2 * m + 2) * P], start=True, stop=True)
                ins.then_inc(s_pl, 1)

            def branch(br, m, src):
                t = T_BR[br] + m
                item = I_BR[br]
                if m == 0:
                    arrived(pe, item)
                if m % 4 == 0:
                    arrived(pe, item + 1 + m // 4)
                start_turn(t)
                feat(banks(t % 2)[:, 0:SEQ], slot(item + 1 + m // 4, KD, 512), (m % 4) * P)
                feat(banks(t % 2)[:, SEQ:2 * SEQ], slot(item, 4, D), m * P, src=src, nk=4).then_inc(s_turn, 1)

            pe.wait_ge(s_aT, 1)
            pe.wait_ge(s_oT, 2)
            level(0)
            for m in range(KD):
                branch(0, m, aT)
                if m == 0:
                    pe.wait_ge(s_conv, 1)
                    for c in range(4):
                        ins = T.matmul(banks(7)[:, 0:SEQ], mean_w, conv[:, c, :], start=(c == 0), stop=(c == 3))
                    ins.then_inc(s_mean, 1)
                level(m + 1)
                if m == 2:
                    pe.wait_ge(s_sqr, 1)
                    for b in range(TB):
                        for c in range(4):
                            ins = T.matmul(banks(7)[:, SEQ + b:SEQ + b + 1], conv_sq[:, c, b * P:(b + 1) * P], mean_w[:, 0:1],
                                           start=(c == 0), stop=(c == 3))
                    ins.then_inc(s_var, 1)
                if m == 4:
                    pe.wait_ge(s_cdg, 1)
                    T.matmul(banks(7)[:, SEQ:2 * SEQ], ones, cvs[:, 0:SEQ], start=True, stop=True).then_inc(s_csp, 1)
            pe.wait_ge(s_pc, 9)
            pe.wait_ge(s_rv, 2)
            pe.wait_ge(s_cn, 1)
            for hh in range(NH_R):
                o = banks(6, 2)[:, hh * SEQ:(hh + 1) * SEQ]
                T.matmul(o[:, 0:P], v_tok[:, 0, hh * P:(hh + 1) * P], inner[:, hh, 0, :], start=True, stop=True)
                T.matmul(o[:, P:SEQ], v_tok[:, 0, hh * P:(hh + 1) * P], inter[:, hh, :], start=True, stop=False)
                ins = T.matmul(o[:, P:SEQ], v_tok[:, 1, hh * P:(hh + 1) * P], inner[:, hh, 1, :], start=False, stop=True)
            ins.then_inc(s_on, 1)
            pe.wait_ge(s_cT2, 1)
            for m in range(KD):
                branch(1, m, conv)
                if m == 1:
                    pe.wait_ge(s_osq, 1)
                    for n in range(8):
                        ins = T.matmul(banks(2)[:, n:n + 1], fz[:, n * P:(n + 1) * P], mean_o[:, 0:1], start=True, stop=True)
                    ins.then_inc(s_ms, 1)
                if m == 3:
                    pe.wait_ge(s_rdg, 1)
                    for z in range(2):
                        ins = T.matmul(banks(4 + z), ones, ls[:, 512 * z:512 * z + 512], start=True, stop=True)
                    ins.then_inc(s_rsp, 1)
            pe.wait_ge(s_ot, 1)
            for m in range(KD):
                branch(2, m, oT_rnn)
            pe.wait_ge(s_mg, 24)
            for b in range(TB):
                for half in range(2):
                    t = T_OUT + 2 * b + half
                    arrived(pe, I_OUT + half)
                    start_turn(t)
                    tokm(banks(t % 2), slot(I_OUT + half, KD, 512), 0, 512, b, src=merged).then_inc(s_turn, 1)

            for b in range(TB):
                pe.wait_ge(s_h2, b + 1)
                for k in range(KD):
                    ins = T.transpose(banks(2 + 2 * b, 2)[:, k * P:(k + 1) * P], h[:, b, k * P:(k + 1) * P], ident)
                ins.then_inc(s_h2Tp, 1)
            pe.wait_ge(s_ro, 32)
            pe.wait_ge(s_h2T, 3)
            for b in range(TB):
                ins = tokm(banks(2)[:, b * NE:(b + 1) * NE], rw, 0, NE, b)
            ins.then_inc(s_rl, 1)
            arrived(pe, I_SGU)

            def shared_up(g):
                t = T_SH + g
                start_turn(t)
                feat(banks(t % 2)[:, 0:SEQ], slot(I_SGU, KD, 512), 2 * g * P)
                feat(banks(t % 2)[:, SEQ:2 * SEQ], slot(I_SGU, KD, 512), (2 * g + 1) * P).then_inc(s_turn, 1)

            shared_up(0)
            pe.wait_ge(s_sel, 1)
            T.matmul(banks(3)[:, 0:NE], before, sel[:, 0, :], start=True, stop=True)
            T.matmul(banks(3)[:, NE:2 * NE], ones, sel[:, 0, :], start=True, stop=False)
            T.matmul(banks(3)[:, NE:2 * NE], before, sel[:, 1, :], start=False, stop=True)
            for b in range(TB):
                ins = T.matmul(banks(3)[:, 64:64 + NE], ones, sel[:, b, :], start=(b == 0), stop=(b == 1))
            ins.then_inc(s_rk, 1)
            shared_up(1)

            def gather(q):
                for k in range(KD):
                    for b in range(TB):
                        ins = T.matmul(banks(0, 2)[:, k * P:(k + 1) * P], h[:, b, k * P:(k + 1) * P], slot_of[q][:, b, :],
                                       start=(b == 0), stop=(b == 1))
                ins.then_inc(s_xp, 1)

            def add_out(q, last=False):
                for b in range(TB):
                    for half in range(2):
                        ins = T.matmul(banks(4 + 2 * b + half), hg[q][:, F_E + b * P:F_E + (b + 1) * P],
                                       yo[:, half * 512:(half + 1) * 512], start=False, stop=last)
                    if last:
                        ins.then_inc(s_add, 1)
                if not last:
                    ins.then_inc(s_add, 1)

            def pair(i, q, last=False):
                p = i * 3 + q
                first = isinstance(p, int) and p == 0
                for e in range(2):
                    s, v = pair_item(i, q, e)
                    pe.wait_ge(s_w[s], v)
                pe.wait_ge(s_xc, p + 1)
                if not first:
                    pe.wait_ge(s_hid, p)
                for k in range(KD):
                    for e in range(2):
                        w = wslot(PAIR_SLOTS[q][e]).rearrange("p (k n) -> p k n", k=KD)
                        ins = T.matmul(banks(2)[e * CAP:(e + 1) * CAP, :], xT[:, k, e * CAP:(e + 1) * CAP], w[:, k, :],
                                       start=(k == 0), stop=(k == KD - 1))
                ins.then_inc(s_gu, 1)
                if not last:
                    pe.wait_ge(s_S, p * 2 + 4)
                    if not first:
                        pe.wait_ge(s_yo, p)
                    gather((q + 1) % 3)
                pe.wait_ge(s_hid, p + 1)
                if not first:
                    pe.wait_ge(s_hg, p)
                for f in range(2):
                    T.transpose(banks(3)[:, f * P:(f + 1) * P], hid[:, f * P:(f + 1) * P], ident)
                for b in range(TB):
                    ins = T.transpose(banks(3)[:, F_E + b * P:F_E + (b + 1) * P], slot_gate[q][:, b, :], ident)
                ins.then_inc(s_htp, 1)
                if not first:
                    pe.wait_ge(s_yo, p)
                    add_out((q + 2) % 3)
                s, v = pair_item(i, q, 2)
                pe.wait_ge(s_w[s], v)
                pe.wait_ge(s_hg, p + 1)
                if last:
                    pe.wait_ge(s_yo, p)
                else:
                    pe.wait_ge(s_xc, p + 2)
                w = wslot(s).rearrange("p (e f n) -> p e f n", e=2, f=2)
                for half in range(2):
                    for f in range(2):
                        for e in range(2):
                            ins = T.matmul(banks(half)[e * CAP:(e + 1) * CAP, :], hg[q][:, f * P + e * CAP:f * P + (e + 1) * CAP],
                                           w[:, e, f, half * 512:(half + 1) * 512], start=(f == 0), stop=(f == 1))
                ins.then_inc(s_dn, 1)

            pe.wait_ge(s_S, 2)
            pe.wait_ge(s_sh, 1)
            gather(0)
            arrived(pe, I_SDN)
            w_sdn = slot(I_SDN, 2, D)
            for b in range(TB):
                for half in range(2):
                    for f in range(2):
                        ins = T.matmul(banks(4 + 2 * b + half), hid_s[:, f, b * P:(b + 1) * P],
                                       w_sdn[:, f, half * 512:(half + 1) * 512], start=(f == 0), stop=False)
            ins.then_inc(s_sdn, 1)
            for q in range(3):
                pair(0, q)
            with pe.Fori(1, NPAIR // 3) as i:
                for q in range(3):
                    pair(i, q)
            pair(NPAIR // 3, 0, last=True)
            pe.wait_ge(s_yo, NPAIR)
            add_out(0, last=True)
            with pe.If(over(pe)):
                pe.wait_ge(s_acc, TB)
                wg = wslot(0).rearrange("p (k n) -> p k n", k=KD)
                wd = wslot(1)[:, 0:2 * D].rearrange("p (f n) -> p f n", f=2)

                def over_expert(e):
                    pe.wait_ge(o_w, e * 32 + 32)
                    after_first(pe, o_h, e, e)
                    for f in range(4):
                        ins = feat(banks(f // 2)[:, (f % 2) * SEQ:(f % 2 + 1) * SEQ], wg, f * P)
                    ins.then_inc(o_up, 1)
                    pe.wait_ge(o_h, e + 1)
                    after_first(pe, o_acc, e * 2, e)
                    for b in range(TB):
                        for half in range(2):
                            ins = tokm(banks(4 + 2 * b + half), wd, half * 512, 512, b, src=hid_s, nk=2)
                    ins.then_inc(o_dn, 1)

                over_expert(0)
                with pe.Fori(1, NE) as e:
                    over_expert(e)


_INS = ["x", "ln_in_g", "ln_in_b", "w_in", "b_in", "conv_dw", "conv_b", "conv_ln_g", "conv_ln_b", "w_conv_proj",
        "hgrn_gamma", "hgrn_norm_g", "w_rnn_proj", "kv_norm_g", "w_uv", "w_att_proj", "rel_bias", "w_out",
        "ln_mix_g", "ln_mix_b", "router_w", "router_b", "w_expert_gu", "w_expert_dn", "w_shared_gu",
        "w_shared_dn", "ln_ffn_g", "ln_ffn_b"]


def shape_constants():
    import numpy as np
    a, b = np.arange(P)[:, None], np.arange(P)[None, :]
    tables = np.stack([a == b, np.ones((P, P)), a < b, np.where(b <= a, 3.0e38, BANNED), np.where(b <= a, 0.0, OFF),
                       np.full((P, P), 1 / D_CONV), np.full((P, P), 1 / P)], axis=1).astype(np.float32)
    level = [a == b] + [(a // (2 * hf) == b // (2 * hf)) & (a % (2 * hf) < hf) & (b % (2 * hf) >= hf) for hf in HALVES]
    dist = np.maximum(np.arange(NDIST) - (P - 1), 0)
    exact = NBUCKET // 2
    large = exact + (np.log(np.maximum(dist, 1).astype(np.float32) / exact) / math.log(128 / exact)
                     * (NBUCKET - exact)).astype(np.int32)
    bucket = np.where(dist < exact, dist, np.minimum(large, NBUCKET - 1))
    onehot = (bucket[None, :] == np.arange(NBUCKET)[:, None]).astype(np.float32)
    return {"c_f32": tables, "c_level": np.stack(level, axis=1).astype(np.float32), "c_onehot": onehot}


def kernel(**inputs):
    import numpy as np
    import concourse.bacc as bacc
    from concourse.bass_utils import run_bass_kernel_spmd

    nc = bacc.Bacc("TRN2", target_bir_lowering=False, num_devices=1)
    arrays, args = {}, {}
    for name, a in [(n, np.ascontiguousarray(inputs[n])) for n in _INS] + list(shape_constants().items()):
        arrays[f"in_{name}"] = a
        args[name] = nc.dram_tensor(f"in_{name}", a.shape, mybir.dt.from_np(a.dtype), kind="ExternalInput").ap()
    args["out"] = nc.dram_tensor("out_0", (1, SEQ, D), F32, kind="ExternalOutput").ap()
    build(nc, **args)
    r = run_bass_kernel_spmd(nc, [arrays], core_ids=[0])
    return r.results[0]["out_0"]
```

```python
import math
from contextlib import ExitStack

import concourse.bass as bass
from concourse import mybir

F32 = mybir.dt.float32
BF16 = mybir.dt.bfloat16
I32 = mybir.dt.int32
U8 = mybir.dt.uint8
ALU = mybir.AluOpType
ACT = mybir.ActivationFunctionType
AX = mybir.AxisListType

P = 128
D = 1024
SEQ = 256
TB = SEQ // P
KD = D // P
D_CONV = 512
TAPS = 31
TAPS_FIRST, TAPS_SECOND = 19, 23
NH_R = 4
NH_A = 8
NH_I = 4
TOPK = 64
NBUCKET = 32
NDIST = 384
NE = 32
TOPE = 4
F_E = 256
ROUTE_SCALE = 2.5
ALPHA = 2.0 ** 0.25
EPS = 1e-5
CAP = 64
NPAIR = NE // 2
COL_RQ, COL_RF, COL_RI, COL_RG = 1024, 1536, 2048, 2560
COL_AQ, COL_IDX, COL_GATE = 3072, 4096, 4548
N_IDX_COLS = COL_GATE - COL_IDX
WSLOTS = 6
SLOT = 4096
BANNED = -3.0e38
TAKEN = -3.4e38
OFF = -1.0e30
TINY = 2.0 ** -60
POOL_F = 22912
HALVES = [1, 2, 4, 8, 16, 32, 64]


def build(nc, x, ln_in_g, ln_in_b, w_in, b_in, conv_dw, conv_b, conv_ln_g, conv_ln_b, w_conv_proj,
          hgrn_gamma, hgrn_norm_g, w_rnn_proj, kv_norm_g, w_uv, w_att_proj, rel_bias, w_out,
          ln_mix_g, ln_mix_b, router_w, router_b, w_expert_gu, w_expert_dn, w_shared_gu,
          w_shared_dn, ln_ffn_g, ln_ffn_b, c_f32, c_level, c_onehot, out):
    bias_by_dist = nc.dram_tensor("bias_by_dist", (NH_A, NDIST), F32, kind="Internal")
    bias_ap = bias_by_dist.ap()

    ctx = ExitStack()
    with ctx:
        def sb(name, shape, dt=F32):
            return ctx.enter_context(nc.sbuf_tensor(name, shape, dt))

        def sem(name):
            return ctx.enter_context(nc.semaphore(name))

        ring = sb("ring", [P, WSLOTS * SLOT])
        h = sb("h", [P, TB, D])
        hT = sb("hT", [P, KD, SEQ])
        consts = sb("consts", [P, 7, P])
        level_mask = sb("level_mask", [P, 8, P], U8)
        params = sb("params", [P, P])
        stats = sb("stats", [P, 4, 6])
        mv = sb("mv", [P, 4, 2])
        rstd = sb("rstd", [P, 4])
        small = sb("small", [P, 75])
        ident, ones, before, can, never, mean_w, mean_o = (consts[:, i, :] for i in range(7))

        pool = sb("pool", [P, POOL_F])
        used = [0]

        def part(n):
            used[0] += n
            assert used[0] <= POOL_F, used
            return pool[:, used[0] - n:used[0]]

        gb_conv = part(2 * D + 160)
        gb = gb_conv[:, 0:2 * D].rearrange("p (a d) -> p a d", a=2)
        UW = SEQ + TAPS - 1
        u_pad = gb_conv[:, 0:4 * UW].rearrange("p (c t) -> p c t", c=4)
        conv = gb_conv[:, 4 * UW:4 * UW + 1024].rearrange("p (c t) -> p c t", c=4)
        cvs = gb_conv[:, 0:1024]
        conv_sq = cvs.rearrange("p (c t) -> p c t", c=4)
        aq_merged = part(2048)
        aqT = aq_merged.rearrange("p (h t) -> p h t", h=NH_A)
        merged = aq_merged.rearrange("p (m t) -> p m t", m=KD)
        c_tok_major = part(256).rearrange("p (b c) -> p b c", b=TB)
        cT = part(256)
        qi_wuv = part(512)
        qiT = qi_wuv.rearrange("p (a t) -> p a t", a=2)
        wuv = qi_wuv.rearrange("p (h v) -> p h v", h=NH_A)
        kiT = part(256)
        sel_add = part(512).rearrange("p (b s) -> p b s", b=TB)
        r1 = part(6144)
        logits1 = r1[:, 0:2048].rearrange("p (h s) -> p h s", h=NH_A)
        relu_i = r1[:, 0:1024].rearrange("p (h s) -> p h s", h=NH_I)
        oT_att = r1[:, 0:2048].rearrange("p (h t) -> p h t", h=NH_A)
        logits0 = r1[:, 2048:3072].rearrange("p (h s) -> p h s", h=NH_A)
        score = r1[:, 2048:2304]
        probsT = r1[:, 3072:6144].rearrange("p (b h t) -> p b h t", b=3, h=NH_A)
        Xl = [r1[:, 2048 * i:2048 * i + 1024] for i in range(2)]
        Yl = [r1[:, 2048 * i + 1024:2048 * i + 2048] for i in range(2)]
        inter = r1[:, 4096:4608].rearrange("p (h t) -> p h t", h=NH_R)
        aT = r1[:, 5120:6144].rearrange("p (c t) -> p c t", c=4)
        t_region = part(2048)
        dist_bias = t_region.rearrange("p (h s) -> p h s", h=NH_A)
        inner = t_region[:, 0:1024].rearrange("p (h c t) -> p h c t", h=NH_R, c=2)
        oT_rnn = t_region[:, 1024:2048].rearrange("p (h t) -> p h t", h=NH_R)
        fz, cum, ls, kT, qT, sgT = (part(1024) for _ in range(6))
        v_tok = part(1024).rearrange("p (b n) -> p b n", b=TB)
        gate_tmp = part(512).rearrange("p (a t) -> p a t", a=2)
        ri_bias = part(512)
        row_bias = part(132)
        kvg = part(128)
        wi = part(8).rearrange("p (b h) -> p b h", b=TB)
        dw = part(4 * TAPS).rearrange("p (c k) -> p c k", c=4)

        def hd(t, i):
            return t[:, i * SEQ:(i + 1) * SEQ]

        EXTRA = 6048
        extra_slots = [pool[:, EXTRA + SLOT * i:EXTRA + SLOT * (i + 1)] for i in range(3)]
        regions = {"merged": [2208, 4256], "attention": [4256, EXTRA], "early": [EXTRA + 3 * SLOT, 21408],
                   "biases": [21920, POOL_F], "gain_bias": [0, 2208]}

        def mpart(region, *shape):
            n = math.prod(shape)
            at, end = regions[region]
            assert at + n <= end, (region, at, n, end)
            regions[region][0] += n
            v = pool[:, at:at + n]
            if len(shape) == 2:
                return v.rearrange("p (a b) -> p a b", a=shape[0])
            if len(shape) == 3:
                return v.rearrange("p (a b c) -> p a b c", a=shape[0], b=shape[1])
            return v
        xT = mpart("merged", KD, 2 * CAP)
        split = xT.rearrange("p k s -> p (k s)")
        yo = mpart("merged", D)
        silu_s = yo[:, 0:2 * SEQ].rearrange("p (f t) -> p f t", f=2)
        hid_s = yo[:, 2 * SEQ:4 * SEQ].rearrange("p (f t) -> p f t", f=2)
        rw = mpart("early", KD, NE)
        slot_of = [mpart("early", TB, CAP).rearrange("p b c -> p (b c)").bitcast(BF16).rearrange("p (b s) -> p b s", b=TB)
                   for _ in range(3)]
        slot_gate = [mpart("early", TB, 2 * CAP) for _ in range(3)]
        hid = mpart("early", F_E)
        silu_e = mpart("early", F_E)
        hidT = [mpart(region, F_E) for region in ("attention", "early", "biases")]
        token_of = [mpart(region, P).bitcast(BF16) for region in ("attention", "early", "biases")]
        ffn_bias = mpart("attention", D)
        h_terms = [[t.bitcast(BF16) for t in (ffn_bias[:, 0:D // 2], ffn_bias[:, D // 2:D], mpart("early", D // 2))],
                   [mpart("gain_bias", D // 2).bitcast(BF16) for _ in range(3)]]
        yo_terms = [[t.bitcast(BF16) for t in halves] for halves in (
            (mpart("gain_bias", D // 4), mpart("gain_bias", D // 4)),
            (mpart("attention", D // 4), level_mask[:, :, :].rearrange("p n t -> p (n t)")),
            (consts[:, 2:4, :].rearrange("p a t -> p (a t)"), consts[:, 4:6, :].rearrange("p a t -> p (a t)")))]
        scores = mpart("biases", TB, NE)
        scores_T = silu_e
        biased = mpart("biases", TB, NE)
        sel = mpart("biases", TB, NE)
        gate = mpart("biases", TB, NE)
        rank_in = mpart("biases", TB, NE)
        top8 = mpart("biases", TB, 8)
        wsum = mpart("biases", TB)
        rb = mpart("biases", NE)
        cmax = mpart("biases", 1)
        iota_c = mpart("biases", CAP)
        ident_b = mpart("biases", P // 2).bitcast(BF16)
        slot_g = small[:, 72:75]
        g_over = mpart("early", TB, NE)
        count = sb("count", [1, 1], I32)

        ps = ctx.enter_context(nc.psum_tensor("ps", [P, 8, 512], F32))

        def banks(a, n=1):
            return ps[:, a:a + n, :].rearrange("p b n -> p (b n)")

        s_x = [sem("x_block0_loaded"), sem("x_block1_loaded")]; s_gb = [sem("ln_in_gain_loaded"), sem("ln_in_bias_loaded")]; s_par = sem("param_rows_loaded"); s_rp = sem("other_small_params_loaded"); s_rb = sem("bias_rows_loaded")
        s_con = sem("consts_loaded"); s_lm = sem("level_masks_loaded")
        s_w = [sem(f"weights_in_slot{i}") for i in range(WSLOTS + 3)]
        s_h = sem("h_ready"); s_hTp = sem("hT_in_psum"); s_hT = [sem("hT_block0_ready"), sem("hT_block1_ready")]
        s_prT = sem("params_in_psum"); s_pr = sem("params_ready")
        s_pin = sem("power_base_ready"); s_pout = sem("power_ready")
        s_bd = sem("bias_by_dist_ready"); s_bdd = sem("bias_by_dist_in_dram"); s_T = sem("dist_bias_loaded"); s_uvl = sem("value_weights_loaded")
        s_turn = sem("turn_done")
        s_free = [sem("bank0_free"), sem("bank1_free")]
        s_sig = sem("sigmoid_ready")
        s_cr = sem("c_ready"); s_cTp = sem("cT_in_psum"); s_cT = sem("cT_ready")
        s_qk = sem("indexer_qk_ready"); s_sc = sem("indexer_products_ready"); s_relu = sem("relu_ready")
        s_reluf = sem("relu_used")
        s_u = sem("conv_input_ready")
        s_conv = sem("conv_ready"); s_mean = sem("conv_mean_ready"); s_sqr = sem("conv_squares_ready")
        s_cdg = sem("conv_rstd_diagonal"); s_csp = sem("conv_rstd_spread")
        s_cen = sem("conv_centred"); s_var = sem("conv_var_ready"); s_cn = sem("conv_normed")
        s_cT2 = sem("conv_silu_ready")
        s_aq = sem("att_q_ready"); s_lg = sem("logits_ready"); s_la = sem("logits_biased")
        s_ex = sem("exp_ready"); s_pn = sem("probs_ready"); s_pTp = sem("probsT_in_psum")
        s_pT = sem("probsT_ready"); s_oTp = sem("att_oT_in_psum"); s_oT = sem("att_oT_ready")
        s_uvp = sem("att_values_in_psum"); s_aT = sem("att_values_ready")
        s_rf = sem("forget_ready"); s_hp = sem("hgrn_prep_vector"); s_ha = sem("hgrn_prep_scalar")
        s_lbv = sem("lower_bound_vector"); s_lba = sem("lower_bound_scalar")
        s_rq = sem("rnn_q_ready"); s_rv = sem("rnn_v_ready"); s_rg = sem("rnn_gate_ready")
        s_dl = sem("level_diff_ready"); s_el = sem("level_decay_ready"); s_xy = sem("level_xy_ready")
        s_pl = sem("level_products_ready"); s_pc = sem("level_products_taken")
        s_on = sem("rnn_o_in_psum"); s_osq = sem("rnn_o_squares_ready"); s_ms = sem("rnn_ms_ready")
        s_rdg = sem("rnn_rstd_diagonal"); s_rsp = sem("rnn_rstd_spread")
        s_ot = sem("rnn_oT_ready")
        s_mg = sem("merged_ready"); s_rs = sem("mix_residual_ready")
        s_gb2 = sem("ln_mix_params_loaded"); s_gb3 = sem("ln_ffn_params_loaded")
        s_h2 = sem("h2_ready"); s_h2Tp = sem("h2T_in_psum"); s_h2T = [sem("h2T_block0_ready"), sem("h2T_block1_ready")]
        s_ro = sem("router_loaded"); s_rl = sem("router_logits_ready"); s_rsg = sem("router_scores_ready"); s_rst = sem("router_scores_token_major")
        s_sel = sem("selection_ready"); s_rk = sem("ranks_ready"); s_cnt = sem("count_ready")
        s_h2c = sem("h2_first_terms_ready"); s_h2r = sem("h2_rest_ready"); s_h2m = sem("h2_second_terms_ready")
        s_h3 = sem("h2_terms_ready")
        s_ssl = sem("shared_silu_ready"); s_sh = sem("shared_hidden_ready"); s_sdn = sem("shared_down_ready")
        s_S = sem("slots_ready"); s_xp = sem("xT_in_psum"); s_xc = sem("xT_ready"); s_gu = sem("expert_up_ready")
        s_sl = sem("expert_silu_ready"); s_hid = sem("expert_hidden_ready"); s_htp = sem("hidden_and_gates_in_psum")
        s_hg = sem("hiddenT_ready"); s_tk = sem("token_of_ready"); s_sg = sem("slot_gates_ready"); s_dn = sem("expert_down_ready"); s_yo = sem("expert_out_ready")
        s_add = sem("expert_out_added"); s_y1 = sem("out_first_term_ready"); s_y2 = sem("out_rest_ready")
        s_y3 = sem("out_second_term_ready"); s_Sf = sem("slots_found"); s_acc = sem("residual_ready")
        o_w = sem("over_weights_loaded"); o_up = sem("over_up_ready"); o_sl = sem("over_silu_ready")
        o_h = sem("over_hidden_ready"); o_dn = sem("over_down_ready"); o_acc = sem("over_added"); o_st = sem("over_stats_ready")
        s_y = sem("out_ready"); s_out = sem("out_stored")
        q_v = sem("vector_order"); q_a = sem("scalar_order"); q_g = sem("gpsimd_order")

        def strip(w, c0, n=512):
            return w[:, c0:c0 + n].rearrange("(k p) n -> p k n", p=P)

        w_in2 = w_in[0]
        stream = [(strip(w_in2, COL_IDX, N_IDX_COLS - NH_I), KD, N_IDX_COLS)]
        free_at = [3]
        for c0, last in ((0, 7), (512, 7), (COL_AQ, 9), (COL_AQ + 512, 11), (COL_RF, 13), (COL_RQ, 15),
                         (COL_RI, 17), (COL_RG, 19)):
            stream.append((strip(w_in2, c0), KD, 512))
            free_at.append(last)
        BRANCH = [(2, w_att_proj), (0, w_conv_proj), (1, w_rnn_proj)]
        T_BR = [19, 27, 35]
        for (g, w), t0 in zip(BRANCH, T_BR):
            stream.append((w[0].rearrange("(k p) n -> p k n", p=P), 4, D))
            free_at.append(t0 + 8)
            for half in range(2):
                stream.append((strip(w_in2, COL_GATE + g * D + half * 512), KD, 512))
                free_at.append(t0 + 4 * half + 4)
        I_BR = [9, 12, 15]
        I_OUT = 18
        T_OUT = 43
        for half in range(2):
            stream.append((strip(w_out[0], half * 512), KD, 512))
            free_at.append(T_OUT + 3 + half)
        I_SGU, I_SDN = 20, 21
        stream.append((strip(w_shared_gu[0], 0), KD, 512))
        stream.append((w_shared_dn[0].rearrange("(k p) n -> p k n", p=P), 2, D))
        T_SH = T_OUT + 4
        free_at += [T_SH + 2, None]
        assert len(stream) == 22

        def slot(n, k, w):
            s = n % WSLOTS
            return ring[:, s * SLOT:s * SLOT + k * w].rearrange("p (k n) -> p k n", k=k)

        def arrived(eng, n):
            eng.wait_ge(s_w[n % WSLOTS], 16 * (n // WSLOTS + 1))

        PAIR_SLOTS = [(6, 7, 8), (4, 5, 0), (1, 2, 3)]

        def wslot(s):
            return ring[:, s * SLOT:(s + 1) * SLOT] if s < WSLOTS else extra_slots[s - WSLOTS]

        def pair_item(i, q, j):
            s = PAIR_SLOTS[q][j]
            before_it = len([n for n in range(len(stream)) if n % WSLOTS == s])
            return s, (i + before_it + 1) * 16

        gu_d = w_expert_gu[0].rearrange("e (k p) n -> e p k n", p=P)
        dn_d = w_expert_dn[0].rearrange("e (f p) n -> e p f n", p=P)
        COUNT_MAX = SEQ

        def over(eng):
            eng.wait_ge(s_cnt, 1)
            return eng.value_load(count[0:1, 0:1], min_val=0, max_val=COUNT_MAX) > CAP

        prow = fz[:, 0:P]
        dw_rows = fz[:, P:P + 512]
        bdist = ls[:, 0:NDIST]
        buckets = ls[:, NDIST:2 * NDIST]
        relb = ls[:, 2 * NDIST:2 * NDIST + NH_A]
        B_RQ, B_RF, B_RG, B_AQ = COL_RQ // P, COL_RF // P, COL_RG // P, COL_AQ // P
        B_GATE, B_CB, B_CG, B_CLB, B_GAM, B_NG, B_QI, B_KI = 32, 56, 60, 64, 68, 72, 76, 78

        def col(i):
            return params[:, i:i + 1]

        lb_a, lb_ln = small[:, 0:4], small[:, 4:8]
        lb = small[:, 8:12]
        minus_half = small[:, 56:57]
        ssq, crs = small[:, 12:14], small[:, 14:16]
        rrs = small[:, 64:72]
        m8 = small[:, 16:24]
        nmax = small[:, 24:40]
        esum = small[:, 40:56]

        def after_first(eng, s, value, i):
            if not (isinstance(i, int) and i == 0):
                eng.wait_ge(s, value)

        block = ctx.enter_context(nc.Block())

        @block.sync
        def _(sp):
            sp.dma_start(h[:, 0, :], x[0, 0:P, :]).then_inc(s_x[0], 16)
            sp.dma_start(prow[0:32, :], b_in[0, 0:4096].rearrange("(m p) -> m p", p=P)).then_inc(s_par, 16)
            sp.dma_start(prow[32:56, :], b_in[0, COL_GATE:COL_GATE + 3072].rearrange("(m p) -> m p", p=P)).then_inc(s_par, 16)
            for r, a in ((56, conv_b), (60, conv_ln_g), (64, conv_ln_b), (68, hgrn_gamma), (72, hgrn_norm_g)):
                sp.dma_start(prow[r:r + 4, :], a[0].rearrange("(m p) -> m p", p=P)).then_inc(s_par, 16)
            sp.dma_start(prow[76:78, :], b_in[0, COL_IDX + 128:COL_IDX + 384].rearrange("(m p) -> m p", p=P)).then_inc(s_par, 16)
            for z in range(2):
                sp.dma_start(prow[78:79, 64 * z:64 * z + 64],
                             b_in[0, COL_IDX + 384:COL_IDX + 448].rearrange("(m p) -> m p", p=64)).then_inc(s_par, 16)
            def load_item(i, q, j):
                s, _ = pair_item(0, q, j)
                if j < 2:
                    sp.dma_start(wslot(s).rearrange("p (k n) -> p k n", k=KD),
                                 gu_d[i * 6 + (2 * q + j)]).then_inc(s_w[s], 16)
                else:
                    sp.dma_start(wslot(s).rearrange("p (e f n) -> p e f n", e=2, f=2),
                                 dn_d[bass.ds(i * 6 + 2 * q, 2)].rearrange("e p f n -> p e f n")).then_inc(s_w[s], 16)

            def load_pair(i, q):
                for j in range(3):
                    if j < 2:
                        sp.wait_ge(s_gu, i * 3 + (q - 2))
                    else:
                        sp.wait_ge(s_dn, i * 6 + 2 * (q - 2))
                    load_item(i, q, j)

            for n, (src, k, w) in enumerate(stream):
                if n == 1:
                    sp.wait_ge(s_rb, 16 * 4)
                if n == 16:
                    sp.wait_ge(s_on, 1)
                    load_item(0, 0, 0)
                if n == 18:
                    sp.wait_ge(s_ot, 1)
                    load_item(0, 0, 2)
                if n >= WSLOTS:
                    sp.wait_ge(s_turn, free_at[n - WSLOTS])
                dst = slot(n, k, w)
                if n == 0:
                    dst = dst[:, :, NH_I:N_IDX_COLS]
                sp.dma_start(dst, src).then_inc(s_w[n % WSLOTS], 16)
            sp.wait_ge(s_turn, T_OUT)
            load_item(0, 0, 1)
            for q in range(1, 3):
                for j in range(3):
                    n = 16 + 3 * (q - 1) + j
                    if n < 21:
                        sp.wait_ge(s_turn, free_at[n])
                    else:
                        sp.wait_ge(s_sdn, 1)
                    load_item(0, q, j)
            with sp.Fori(1, NPAIR // 3) as i:
                for q in range(3):
                    load_pair(i, q)
            load_pair(NPAIR // 3, 0)
            with sp.If(over(sp)):
                sp.wait_ge(s_dn, 2 * NPAIR)

                def load(e):
                    after_first(sp, o_dn, e, e)
                    sp.dma_start(wslot(0).rearrange("p (k n) -> p k n", k=KD), gu_d[e]).then_inc(o_w, 16)
                    sp.dma_start(wslot(1)[:, 0:2 * D].rearrange("p (f n) -> p f n", f=2), dn_d[e]).then_inc(o_w, 16)

                load(0)
                with sp.Fori(1, NE) as e:
                    load(e)
            for b in range(TB):
                sp.wait_ge(s_y, b + 1)
                sp.dma_start(out[0, b * P:(b + 1) * P, :], h[:, b, :]).then_inc(s_out, 16)
            sp.wait_ge(s_out, 16 * TB)

        @block.gpsimd
        def _(pool_e):
            def rows(ap, n):
                return ap.rearrange("(a n) -> a n", a=1).to_broadcast((P, n))

            powers = [0]

            def power(t):
                powers[0] += 1
                pool_e.wait_ge(s_pin, powers[0])
                pool_e.tensor_tensor(t, t, minus_half.to_broadcast((P, t.shape[1])), ALU.pow).then_inc(s_pout, 1)

            pool_e.dma_start(dw_rows[0:TAPS, :], conv_dw[0]).then_inc(s_rp, 16)
            pool_e.dma_start(slot(0, KD, N_IDX_COLS)[:, :, 0:NH_I],
                             strip(w_in2, COL_IDX + N_IDX_COLS - NH_I, NH_I)).then_inc(s_rp, 16)
            pool_e.dma_start(relb[0:NBUCKET, :], rel_bias).then_inc(s_rp, 16)
            pool_e.dma_start(buckets[0:NBUCKET, :], c_onehot).then_inc(s_rp, 16)
            pool_e.dma_start(row_bias[:, 0:128], rows(b_in[0, COL_IDX:COL_IDX + 128], 128)).then_inc(s_rb, 16)
            pool_e.dma_start(row_bias[:, 128:132], rows(b_in[0, COL_GATE - 4:COL_GATE], 4)).then_inc(s_rb, 16)
            pool_e.dma_start(ri_bias, rows(b_in[0, COL_RI:COL_RI + 512], 512)).then_inc(s_rb, 16)
            pool_e.dma_start(kvg, rows(kv_norm_g[0], 128)).then_inc(s_rb, 16)
            pool_e.memset(minus_half, -0.5).then_inc(q_g, 1)
            pool_e.wait_ge(q_g, 1)
            for b in range(TB):
                power(rstd[:, b:b + 1])
            power(crs)
            pool_e.wait_ge(s_bd, 1)
            pool_e.dma_start(bias_ap, bdist[0:NH_A, :]).then_inc(s_bdd, 16)
            pool_e.wait_ge(s_bdd, 16)
            pool_e.dma_start(dist_bias, bass.AP(bias_by_dist, 0, [[1, P], [NDIST, NH_A], [1, SEQ]])).then_inc(s_T, 16)

            pool_e.dma_start(kT.rearrange("p (n t) -> p n t", n=8), c_level).then_inc(s_lm, 16)
            pool_e.wait_ge(s_lm, 16)
            pool_e.tensor_copy(level_mask[:, :, :].rearrange("p n t -> p (n t)"), kT).then_inc(q_g, 1)
            pool_e.wait_ge(s_relu, 2)
            pool_e.dma_start(wuv, w_uv[0].rearrange("h c v -> c h v")).then_inc(s_uvl, 16)
            power(crs)
            power(rrs)
            pool_e.wait_ge(s_ot, 1)
            pool_e.dma_start(rw, router_w[0].rearrange("(k p) e -> p k e", p=P)).then_inc(s_ro, 16)
            pool_e.dma_start(rb, rows(router_b[0], NE)).then_inc(s_ro, 16)
            pool_e.wait_ge(s_turn, T_BR[1] + KD)
            for i, a in enumerate((ln_mix_g, ln_mix_b)):
                pool_e.dma_start(gb[:, i, :], rows(a[0], D)).then_inc(s_gb2, 16)
            pool_e.wait_ge(s_mg, 8)
            pool_e.iota(iota_c, [[1, CAP]], base=0, channel_multiplier=0,
                        allow_small_or_imprecise_dtypes=True).then_inc(q_g, 1)

            for b in range(TB):
                power(rstd[:, b:b + 1])
            pool_e.wait_ge(s_xp, NPAIR)
            for dst, a in ((gb[:, 0, :], ln_ffn_g), (ffn_bias, ln_ffn_b)):
                pool_e.dma_start(dst, rows(a[0], D)).then_inc(s_gb3, 16)
            for b in range(TB):
                power(rstd[:, b:b + 1])

        @block.scalar
        def _(act):
            q = [0]

            def link(ins):
                q[0] += 1
                ins.then_inc(q_a, 1)
                act.wait_ge(q_a, q[0])

            def hT_out(ready, done, b):
                act.wait_ge(ready, b + 1)
                if b == 0:
                    nc.scalar.copy(hT[:, :, 0:P], banks(2, 2).rearrange("p (k t) -> p k t", k=KD)).then_inc(done[0], 1)
                else:
                    nc.scalar.copy(hT[:, 0:4, P:SEQ], banks(4).rearrange("p (k t) -> p k t", k=4)).then_inc(done[1], 1)

            for i, a in enumerate((ln_in_g, ln_in_b)):
                act.dma_start(gb[:, i, :], a.rearrange("(a n) -> a n", a=1).to_broadcast((P, D))).then_inc(s_gb[i], 16)
            act.dma_start(h[:, 1, :], x[0, P:SEQ, :]).then_inc(s_x[1], 16)
            act.dma_start(consts[:, :, :], c_f32).then_inc(s_con, 16)

            act.wait_ge(s_prT, 1)
            nc.scalar.copy(params[:, 0:79], banks(6)[:, 0:79]).then_inc(s_pr, 1)
            nc.scalar.copy(dw.rearrange("p c k -> p (c k)"), banks(7)[:, 0:4 * TAPS]).then_inc(s_pr, 1)
            nc.scalar.copy(bdist[0:NH_A, :], banks(6)[0:NH_A, 128:512]).then_inc(s_bd, 1)
            for b in range(TB):
                hT_out(s_hTp, s_hT, b)
            act.wait_ge(s_pr, 2)
            act.wait_ge(s_lbv, 1)
            nc.scalar.activation(lb, lb, ACT.Exp).then_inc(s_lba, 1)
            act.wait_ge(s_lbv, 2)
            nc.scalar.activation(lb_a, lb_a, ACT.Ln)
            link(nc.scalar.activation(lb_ln, lb, ACT.Ln, bias=1.0, scale=-1.0))
            act.sem_inc(s_lba, 1)

            def evac(t, outs, sem_out):
                act.wait_ge(s_turn, t + 1)
                for n, (dst, bias) in enumerate(outs):
                    ins = nc.scalar.activation(dst, banks(t % 2)[:, n * SEQ:(n + 1) * SEQ], ACT.Identity, bias=bias)
                    ins.then_inc(sem_out, 1)
                done[sem_out] = done.get(sem_out, 0) + len(outs)
                act.wait_ge(sem_out, done[sem_out])
                act.sem_inc(s_free[t % 2], 1)

            done = {}

            evac(1, [(qiT[:, 0, :], col(B_QI)), (qiT[:, 1, :], col(B_QI + 1))], s_qk)
            evac(2, [(kiT, col(B_KI))], s_qk)
            def conv_gate(c):
                t = 3 + c
                act.wait_ge(s_turn, t + 1)
                if c >= 2:
                    act.wait_ge(s_u, c - 1)
                nc.scalar.activation(gate_tmp[:, c % 2, :], banks(t % 2)[:, SEQ:2 * SEQ], ACT.Sigmoid,
                                     bias=col(4 + c)).then_inc(s_sig, 1)

            conv_gate(0)
            act.wait_ge(s_cTp, 1)
            nc.scalar.copy(cT, banks(5)[:, 0:SEQ]).then_inc(s_cT, 1)
            conv_gate(1)
            act.wait_ge(s_sc, 1)
            nc.scalar.activation(relu_i[:, :, 0:P].rearrange("p (y z) s -> p y z s", y=2),
                                 ps[:, 2:4, 0:2 * P].rearrange("p y (z s) -> p y z s", z=2),
                                 ACT.Relu).then_inc(s_relu, 1)
            conv_gate(2)
            act.wait_ge(s_sc, 2)
            act.wait_ge(s_reluf, 1)
            nc.scalar.activation(relu_i, banks(4, 2).rearrange("p (h s) -> p h s", h=NH_I),
                                 ACT.Relu).then_inc(s_relu, 1)
            conv_gate(3)
            for i in range(4):
                evac(7 + i, [(aqT[:, 2 * i + z, :], col(B_AQ + 2 * i + z)) for z in range(2)], s_aq)
            act.wait_ge(s_bdd, 16)
            for i in range(2):
                evac(11 + i, [(hd(fz, 2 * i + z), col(B_RF + 2 * i + z)) for z in range(2)], s_rf)
            def exps(b):
                lg, w = (logits0, P) if b == 0 else (logits1, SEQ)
                act.wait_ge(s_la, b + 1)
                for hh in range(NH_A):
                    ins = nc.scalar.activation(lg[:, hh, :], lg[:, hh, :], ACT.Exp, bias=nmax[:, 8 * b + hh:8 * b + hh + 1],
                                               accum_out=esum[:, 8 * b + hh:8 * b + hh + 1])
                ins.then_inc(s_ex, 1)

            exps(0)
            exps(1)
            evac(13, [(hd(qT, z), col(B_RQ + z)) for z in range(2)], s_rq)
            act.wait_ge(s_hp, 1)
            link(nc.scalar.activation(cum, cum, ACT.Exp))
            nc.scalar.activation(cum, cum, ACT.Ln, bias=1.0).then_inc(s_ha, 1)
            evac(14, [(hd(qT, 2 + z), col(B_RQ + 2 + z)) for z in range(2)], s_rq)
            act.wait_ge(s_hp, 2)
            act.wait_ge(q_g, 2)
            for i in range(4):
                ins = nc.scalar.activation(hd(kT, i), hd(cum, i), ACT.Exp, bias=lb_ln[:, i:i + 1])
            ins.then_inc(s_ha, 1)
            act.wait_ge(s_hp, 3)
            link(nc.scalar.activation(fz, fz, ACT.Exp))
            nc.scalar.activation(fz, fz, ACT.Ln, bias=1.0).then_inc(s_ha, 1)

            for n, bk in enumerate((2, 6, 2)):
                act.wait_ge(s_pTp, n + 1)
                nc.scalar.copy(probsT[:, n].rearrange("p h t -> p (h t)"), banks(bk, 2)).then_inc(s_pT, 1)
            for b in range(TB):
                act.wait_ge(s_oTp, b + 1)
                for half in range(2):
                    ins = nc.scalar.copy(oT_att[:, 4 * half:4 * half + 4, b * P:(b + 1) * P],
                                         banks(4 + half).rearrange("p (h t) -> p h t", h=4))
                ins.then_inc(s_oT, 1)
            for i in range(2):
                t = 17 + i
                act.wait_ge(s_turn, t + 1)
                for z in range(2):
                    ins = nc.scalar.activation(hd(sgT, 2 * i + z), banks(t % 2)[:, z * SEQ:(z + 1) * SEQ], ACT.Sigmoid,
                                               bias=col(B_RG + 2 * i + z))
                    ins.then_inc(s_rg, 1)
                act.wait_ge(s_rg, 2 * i + 2)
                act.sem_inc(s_free[t % 2], 1)
            act.wait_ge(s_uvp, 1)
            nc.scalar.copy(aT.rearrange("p c t -> p (c t)"), banks(6, 2)).then_inc(s_aT, 1)

            def branch_gate(br, m):
                t = T_BR[br] + m
                n = 8 * br + m
                act.wait_ge(s_turn, t + 1)
                if n >= 2:
                    act.wait_ge(s_mg, n - 1)
                else:
                    act.wait_ge(s_u, 3 + n)
                nc.scalar.activation(gate_tmp[:, n % 2, :], banks(t % 2)[:, 0:SEQ], ACT.Tanh, scale=0.5,
                                     bias=col(B_GATE + 8 * BRANCH[br][0] + m)).then_inc(s_sig, 1)

            def decay(lv):
                act.wait_ge(s_dl, lv + 1)
                e = (fz, ls)[lv % 2]
                nc.scalar.activation(e, e, ACT.Exp).then_inc(s_el, 1)

            decay(0)
            for m in range(KD):
                if m < 7:
                    decay(m + 1)
                branch_gate(0, m)
                if m == 6:
                    act.wait_ge(s_cn, 1)
                    for c in range(4):
                        ins = nc.scalar.activation(conv[:, c, :], conv[:, c, :], ACT.Silu, bias=col(B_CLB + c), scale=col(B_CG + c))
                    ins.then_inc(s_cT2, 1)
            for m in range(KD):
                branch_gate(1, m)
                if m == 0:
                    act.wait_ge(s_on, 1)
                    nc.scalar.activation(fz, banks(6, 2), ACT.Square).then_inc(s_osq, 1)
            for m in range(KD):
                branch_gate(2, m)

            for b in range(TB):
                hT_out(s_h2Tp, s_h2T, b)
                nc.scalar.copy(h_terms[b][0], h[:, b, :]).then_inc(s_h2c, 1)
            for b in range(TB):
                act.wait_ge(s_h2r, b + 1)
                nc.scalar.copy(h_terms[b][1], split).then_inc(s_h2m, 1)
            act.wait_ge(s_rl, 1)
            nc.scalar.activation(scores_T[0:NE, :], banks(2)[0:NE, 0:SEQ], ACT.Sigmoid).then_inc(s_rsg, 1)
            act.wait_ge(s_turn, T_SH + 1)
            nc.scalar.activation(silu_s.rearrange("p f t -> p (f t)"), banks(T_SH % 2), ACT.Silu).then_inc(s_ssl, 1)
            act.wait_ge(s_ssl, 1)
            act.sem_inc(s_free[T_SH % 2], 1)
            act.wait_ge(s_xp, 1)
            nc.scalar.copy(xT.rearrange("p k s -> p (k s)"), banks(0, 2)).then_inc(s_xc, 1)

            def pair(i, q, last=False):
                p = i * 3 + q
                act.wait_ge(s_gu, p + 1)
                if not (isinstance(p, int) and p == 0):
                    act.wait_ge(s_hid, p)
                nc.scalar.activation(silu_e, banks(2)[:, 0:F_E], ACT.Silu).then_inc(s_sl, 1)
                if not last:
                    act.wait_ge(s_xp, p + 2)
                    nc.scalar.copy(xT.rearrange("p k s -> p (k s)"), banks(0, 2)).then_inc(s_xc, 1)
                act.wait_ge(s_htp, p + 1)
                if not (isinstance(p, int) and p < 3):
                    act.wait_ge(s_add, p - 2)
                nc.scalar.copy(hidT[q], banks(3)[:, 0:F_E]).then_inc(s_hg, 1)
                nc.scalar.copy(token_of[q], banks(3)[:, F_E:2 * F_E]).then_inc(s_tk, 1)
                if not (isinstance(p, int) and p == 0):
                    act.wait_ge(s_add, p)
                act.wait_ge(s_sg, p + 1)
                for half in range(2):
                    act.wait_ge(s_dn, p * 2 + (half + 1))
                    nc.scalar.activation(yo_terms[0][half], banks(half), ACT.Copy, scale=slot_g[:, q:q + 1]).then_inc(s_y1, 1)
                for half in range(2):
                    act.wait_ge(s_y2, p * 2 + (half + 1))
                    nc.scalar.copy(yo_terms[1][half], yo[:, half * 512:(half + 1) * 512]).then_inc(s_y3, 1)

            for q in range(3):
                pair(0, q)
            with act.Fori(1, NPAIR // 3) as i:
                for q in range(3):
                    pair(i, q)
            pair(NPAIR // 3, 0, last=True)
            with act.If(over(act)):

                def over_silu(e):
                    act.wait_ge(o_up, e + 1)
                    after_first(act, o_h, e, e)
                    nc.scalar.activation(silu_s.rearrange("p f t -> p (f t)"), banks(0), ACT.Silu).then_inc(o_sl, 1)

                over_silu(0)
                with act.Fori(1, NE) as e:
                    over_silu(e)

        @block.vector
        def _(dve):
            q = [0]
            V = nc.vector

            def step(ins):
                q[0] += 1
                ins.then_inc(q_v, 1)

            def sync():
                dve.wait_ge(q_v, q[0])

            def link(ins):
                step(ins)
                sync()

            def ask_rsqrt(dst, src, scale=1.0, eps=EPS):
                rs[0] += 1
                V.tensor_scalar(dst, src, scale, eps, ALU.mult, ALU.add).then_inc(s_pin, 1)

            def rsqrt(dst, src, scale=1.0):
                ask_rsqrt(dst, src, scale)
                dve.wait_ge(s_pout, rs[0])

            rs = [0]

            def layer_norm(t, i, done, eps=EPS, stats_done=False, gb_ready=None, bias=gb[:, 1, :]):
                if not stats_done:
                    for half in range(2):
                        step(V.bn_stats(stats[:, 2 * i + half, :], t[:, half * 512:(half + 1) * 512]))
                sync()
                link(V.bn_aggr(mv[:, i, :], stats[:, 2 * i:2 * i + 2, :].rearrange("p a s -> p (a s)")))
                ask_rsqrt(rstd[:, i:i + 1], mv[:, i, 1:2], eps=eps)
                if gb_ready:
                    dve.wait_ge(*gb_ready[0])
                link(V.scalar_tensor_tensor(t, t, mv[:, i, 0:1], gb[:, 0, :], ALU.subtract, ALU.mult))
                dve.wait_ge(s_pout, rs[0])
                if gb_ready:
                    dve.wait_ge(*gb_ready[1])
                V.scalar_tensor_tensor(t, t, rstd[:, i:i + 1], bias, ALU.mult, ALU.add).then_inc(done, 1)

            for b in range(TB):
                dve.wait_ge(s_x[b], 16)
                layer_norm(h[:, b, :], b, s_h, gb_ready=((s_gb[0], 16), (s_gb[1], 16)))
            dve.wait_ge(s_h, 2)
            step(V.memset(u_pad[:, :, 0:TAPS - 1], 0.0))
            dve.wait_ge(s_hTp, 2)
            V.tensor_copy(hT[:, 4:8, P:SEQ], banks(5).rearrange("p (k t) -> p k t", k=4)).then_inc(s_hT[1], 1)

            dve.wait_ge(s_pr, 1)
            link(V.tensor_scalar(params[:, B_GATE:B_GATE + 24], params[:, B_GATE:B_GATE + 24], 0.5, None, ALU.mult))
            link(V.tensor_tensor(lb, params[:, B_GAM:B_GAM + 4], params[:, B_GAM:B_GAM + 4], ALU.subtract))
            dve.sem_inc(s_lbv, 1)
            dve.wait_ge(s_lba, 1)
            link(V.reciprocal(lb_ln, lb))
            link(V.tensor_tensor(lb, lb, lb_ln, ALU.mult))
            link(V.tensor_tensor(lb, lb, lb, ALU.subtract))
            link(V.tensor_scalar(lb_a, lb, TINY, None, ALU.max))
            dve.sem_inc(s_lbv, 1)
            dve.wait_ge(s_lba, 2)
            link(V.tensor_scalar(lb, lb, TINY, OFF, ALU.is_lt, ALU.mult))
            link(V.tensor_tensor(lb_a, lb_a, lb, ALU.add))

            dve.wait_ge(s_turn, 1)
            dve.wait_ge(s_rb, 16 * 4)
            for b in range(TB):
                step(V.tensor_tensor(c_tok_major[:, b, :], banks(0)[:, 256 * b + NH_I:256 * b + NH_I + P], row_bias[:, 0:128], ALU.add))
                step(V.tensor_tensor(wi[:, b, :], banks(0)[:, 256 * b:256 * b + NH_I], row_bias[:, 128:132], ALU.add))
            sync()
            dve.sem_inc(s_free[0], 1)
            for b in range(TB):
                step(V.scalar_tensor_tensor(cum[:, 128 * b:128 * b + 128], c_tok_major[:, b, :], 1.0, c_tok_major[:, b, :],
                                            ALU.mult, ALU.mult))
            sync()
            link(V.tensor_reduce(ssq, cum[:, 0:256].rearrange("p (b c) -> p b c", b=TB), AX.X, ALU.add))
            rsqrt(crs, ssq, 1.0 / P)
            for b in range(TB):
                V.scalar_tensor_tensor(c_tok_major[:, b, :], c_tok_major[:, b, :], crs[:, b:b + 1], kvg,
                                       ALU.mult, ALU.mult).then_inc(s_cr, 1)

            def conv_in(c):
                t = 3 + c
                dve.wait_ge(s_sig, c + 1)
                V.scalar_tensor_tensor(u_pad[:, c, TAPS - 1:UW], banks(t % 2)[:, 0:SEQ], col(c),
                                       gate_tmp[:, c % 2, :], ALU.add, ALU.mult).then_inc(s_u, 1)
                dve.wait_ge(s_u, c + 1)
                dve.sem_inc(s_free[t % 2], 1)

            def top_keys(b):
                w = (b + 1) * P
                sc = score[:, 0:w]
                dve.wait_ge(s_relu, b + 1)
                link(V.tensor_scalar(sc, relu_i[:, 0, 0:w], wi[:, b, 0:1], None, ALU.mult))
                for hh in range(1, NH_I):
                    w_h = 2 * (hh % 2) + hh // 2
                    ins = V.scalar_tensor_tensor(sc, relu_i[:, hh, 0:w], wi[:, b, w_h:w_h + 1], sc, ALU.mult, ALU.add)
                    if hh < NH_I - 1:
                        link(ins)
                ins.then_inc(s_reluf, 1)
                dve.wait_ge(s_reluf, b + 1)
                link(V.tensor_tensor(score[:, b * P:w], score[:, b * P:w], can, ALU.min))
                for _ in range(TOPK // 8):
                    link(V.max(m8, sc))
                    link(V.match_replace(sc, m8, sc, TAKEN))
                link(V.tensor_scalar(sel_add[:, b, 0:w], sc, (BANNED + TAKEN) / 2, OFF, ALU.is_gt, ALU.mult))
                link(V.tensor_tensor(sel_add[:, b, b * P:w], sel_add[:, b, b * P:w], never, ALU.add))

            dve.wait_ge(s_con, 16)
            dve.wait_ge(s_pr, 2)
            conv_in(0)
            conv_in(1)
            top_keys(0)
            conv_in(2)
            conv_in(3)
            top_keys(1)
            def conv_taps(first, end):
                sync()
                since = q[0]
                for k in range(first, end):
                    for c in range(4):
                        src = u_pad[:, c, k:k + SEQ]
                        if k == 0:
                            ins = V.tensor_scalar(conv[:, c, :], src, dw[:, c, 0:1], col(B_CB + c), ALU.mult, ALU.add)
                        else:
                            if q[0] - 3 > since:
                                dve.wait_ge(q_v, q[0] - 3)
                            ins = V.scalar_tensor_tensor(conv[:, c, :], src, dw[:, c, k:k + 1], conv[:, c, :], ALU.mult, ALU.add)
                        if k == TAPS - 1 and c == 3:
                            ins.then_inc(s_conv, 1)
                        else:
                            step(ins)

            conv_taps(0, TAPS_FIRST)
            dve.wait_ge(s_T, 16)
            for b, (lg, w, bk) in enumerate(((logits0, P, 2), (logits1, SEQ, 4))):
                dve.wait_ge(s_lg, b + 1)
                nb = w // P
                src = banks(bk, 2 * nb).rearrange("p (h s) -> p h s", h=NH_A)
                tb_ = dist_bias[:, :, 0:w][:, :, ::-1]
                link(V.scalar_tensor_tensor(lg, src, float(P) ** -0.5, tb_, ALU.mult, ALU.add))
                link(V.tensor_tensor(lg, lg, sel_add[:, b:b + 1, 0:w].to_broadcast((P, NH_A, w)), ALU.add))
                V.tensor_reduce(nmax[:, 8 * b:8 * b + 8], lg, AX.X, ALU.max, negate=True).then_inc(s_la, 1)

            dve.wait_ge(s_rf, 4)
            V.scalar_tensor_tensor(cum, fz, -1.0, fz, ALU.mult, ALU.min).then_inc(s_hp, 1)
            for b, (lg, w) in enumerate(((logits0, P), (logits1, SEQ))):
                dve.wait_ge(s_ex, b + 1)
                link(V.reciprocal(esum[:, 8 * b:8 * b + 8], esum[:, 8 * b:8 * b + 8]))
                V.tensor_tensor(lg, lg, esum[:, 8 * b:8 * b + 8].rearrange("p (h o) -> p h o", o=1).to_broadcast((P, NH_A, w)),
                                ALU.mult).then_inc(s_pn, 1)
            dve.wait_ge(s_ha, 1)
            link(V.scalar_tensor_tensor(ls, fz, 0.0, cum, ALU.min, ALU.subtract))
            V.tensor_tensor(cum, ls, fz, ALU.subtract).then_inc(s_hp, 1)
            dve.wait_ge(s_hp, 2)
            for i in range(4):
                step(V.tensor_scalar(hd(ls, i), hd(ls, i), lb_ln[:, i:i + 1], None, ALU.add))
            sync()
            for i in range(4):
                step(V.tensor_scalar(hd(fz, i), hd(ls, i), lb_a[:, i:i + 1], None, ALU.subtract))
            sync()
            V.scalar_tensor_tensor(fz, fz, -1.0, fz, ALU.mult, ALU.min).then_inc(s_hp, 1)
            dve.wait_ge(s_ha, 3)
            for i in range(4):
                step(V.scalar_tensor_tensor(hd(ls, i), hd(ls, i), lb_a[:, i:i + 1], hd(fz, i), ALU.max, ALU.add))
            sync()
            for n in range(8):
                step(V.tensor_tensor_scan(cum[:, n * P:(n + 1) * P], ones, ls[:, n * P:(n + 1) * P], 0.0, ALU.mult, ALU.add))
            sync()
            for b in range(TB):
                t = 15 + b
                dve.wait_ge(s_turn, t + 1)
                V.tensor_tensor(v_tok[:, b, :], banks(t % 2), ri_bias, ALU.add).then_inc(s_rv, 1)
                dve.wait_ge(s_rv, b + 1)
                dve.sem_inc(s_free[t % 2], 1)
                if b == 0:
                    conv_taps(TAPS_FIRST, TAPS_SECOND)
            conv_taps(TAPS_SECOND, TAPS)

            def level_diff(lv):
                d = (fz, ls)[lv % 2]
                if lv < 7:
                    half = HALVES[lv]
                    a = cum.rearrange("p (n w) -> p n w", w=2 * half)
                    dd = d.rearrange("p (n w) -> p n w", w=2 * half)
                    mid = a[:, :, half - 1:half].to_broadcast((P, SEQ * 4 // (2 * half), 2 * half))
                    link(V.tensor_tensor(dd, a, mid, ALU.subtract))
                    V.scalar_tensor_tensor(d, d, -1.0, d, ALU.mult, ALU.min).then_inc(s_dl, 1)
                else:
                    a = cum.rearrange("p (h t) -> p h t", h=NH_R)
                    dd = d.rearrange("p (h t) -> p h t", h=NH_R)
                    mid = a[:, :, P - 1:P].to_broadcast((P, NH_R, P))
                    step(V.tensor_tensor(dd[:, :, 0:P], a[:, :, 0:P], mid, ALU.subtract))
                    step(V.tensor_copy(dd[:, :, P:SEQ], a[:, :, P:SEQ]))
                    sync()
                    V.scalar_tensor_tensor(d, d, -1.0, d, ALU.mult, ALU.min).then_inc(s_dl, 1)

            def level_xy(lv):
                e = (fz, ls)[lv % 2]
                dve.wait_ge(s_el, lv + 1)
                if lv >= 2:
                    dve.wait_ge(s_pl, lv - 1 + 1)
                step(V.tensor_tensor(Xl[lv % 2], e, qT, ALU.mult))
                V.tensor_tensor(Yl[lv % 2], e, kT, ALU.mult).then_inc(s_xy, 1)

            inner_f = inner.rearrange("p h c t -> p (h c) t")

            def take(n):
                bk = 2 + 2 * (n % 2)
                dve.wait_ge(s_pl, n + 1)
                m = level_mask[:, n:n + 1, :].to_broadcast((P, 8, P))
                V.copy_predicated(inner_f, m, banks(bk, 2).rearrange("p (n t) -> p n t", n=8)).then_inc(s_pc, 1)

            def merge(br, m):
                n = 8 * br + m
                t = T_BR[br] + m
                dve.wait_ge(s_sig, 4 + n + 1)
                y = banks(t % 2)[:, SEQ:2 * SEQ]
                if br == 0:
                    V.scalar_tensor_tensor(merged[:, m, :], gate_tmp[:, n % 2, :], 1.0, y, ALU.add, ALU.mult).then_inc(s_mg, 1)
                    dve.wait_ge(s_mg, n + 1)
                    dve.sem_inc(s_free[t % 2], 1)
                else:
                    link(V.scalar_tensor_tensor(gate_tmp[:, n % 2, :], gate_tmp[:, n % 2, :], 1.0, y, ALU.add, ALU.mult))
                    dve.sem_inc(s_free[t % 2], 1)
                    V.tensor_tensor(merged[:, m, :], merged[:, m, :], gate_tmp[:, n % 2, :], ALU.add).then_inc(s_mg, 1)

            def diagonals(dst, cols, n):
                return V.tensor_tensor(dst.rearrange("p (n t) -> p n t", n=n), consts[:, 0:1, :].to_broadcast((P, n, P)),
                                       cols.rearrange("p (n o) -> p n o", o=1).to_broadcast((P, n, P)), ALU.mult)

            def over_blocks(row):
                return row.rearrange("p (o t) -> p o t", o=1).to_broadcast((P, 4, SEQ))

            dve.wait_ge(s_uvp, 1)
            link(V.memset(t_region[:, 0:1024], 0.0))
            dve.wait_ge(s_rq, 4)
            dve.wait_ge(s_ha, 3)
            level_diff(0)
            dve.wait_ge(s_dl, 1)
            for m in range(KD):
                level_xy(m)
                if m < 7:
                    level_diff(m + 1)
                take(m)
                merge(0, m)
                if m == 1:
                    dve.wait_ge(s_mean, 1)
                    V.tensor_tensor(conv, conv, over_blocks(banks(7)[:, 0:SEQ]), ALU.subtract).then_inc(s_cen, 1)
                    dve.wait_ge(s_cen, 1)
                    V.tensor_tensor(conv_sq, conv, conv, ALU.mult).then_inc(s_sqr, 1)
                if m == 3:
                    dve.wait_ge(s_var, 1)
                    rsqrt(crs, banks(7)[:, SEQ:SEQ + TB])
                    diagonals(cvs[:, 0:SEQ], crs, TB).then_inc(s_cdg, 1)
                if m == 5:
                    dve.wait_ge(s_csp, 1)
                    V.tensor_tensor(conv, conv, over_blocks(banks(7)[:, SEQ:2 * SEQ]), ALU.mult).then_inc(s_cn, 1)
            dve.wait_ge(s_pl, 9)
            V.tensor_copy(inter.rearrange("p h t -> p (h t)"), banks(2)).then_inc(s_pc, 1)
            for m in range(KD):
                merge(1, m)
                if m == 2:
                    dve.wait_ge(s_ms, 1)
                    rsqrt(rrs, banks(2)[:, 0:8])
                    diagonals(ls, rrs, 8).then_inc(s_rdg, 1)
                if m == 4:
                    dve.wait_ge(s_rsp, 1)
                    link(V.tensor_tensor(ls, banks(4, 2), sgT, ALU.mult))
                    for i in range(4):
                        ins = V.scalar_tensor_tensor(oT_rnn[:, i, :], banks(6, 2)[:, i * SEQ:(i + 1) * SEQ],
                                                     col(B_NG + i), hd(ls, i), ALU.mult, ALU.mult)
                        if i < 3:
                            step(ins)
                    ins.then_inc(s_ot, 1)
            for m in range(KD):
                merge(2, m)

            for b in range(TB):
                for half in range(2):
                    n = 2 * b + half
                    t = T_OUT + n
                    dve.wait_ge(s_turn, t + 1)
                    hh = h[:, b, half * 512:(half + 1) * 512]
                    V.scalar_tensor_tensor(hh, hh, 2 * ALPHA, banks(t % 2), ALU.mult, ALU.add).then_inc(s_rs, 1)
                    dve.wait_ge(s_rs, n + 1)
                    dve.sem_inc(s_free[t % 2], 1)
                    step(V.bn_stats(stats[:, 2 * b + half, :], hh))
                layer_norm(h[:, b, :], b, s_h2, eps=4 * EPS, stats_done=True, gb_ready=((s_gb2, 32), (s_gb2, 32)))
            dve.wait_ge(s_h2Tp, 2)
            V.tensor_copy(hT[:, 4:8, P:SEQ], banks(5).rearrange("p (k t) -> p k t", k=4)).then_inc(s_h2T[1], 1)

            for b in range(TB):
                dve.wait_ge(s_h2c, b + 1)
                V.tensor_tensor(split, h[:, b, :], h_terms[b][0], ALU.subtract).then_inc(s_h2r, 1)
                dve.wait_ge(s_h2m, b + 1)
                V.tensor_tensor(h_terms[b][2], split, h_terms[b][1], ALU.subtract).then_inc(s_h3, 1)
                dve.wait_ge(s_h3, b + 1)
            step(V.tensor_copy(ident_b, ident))

            dve.wait_ge(s_rst, 1)
            dve.wait_ge(s_ro, 32)
            dve.wait_ge(q_g, 3)
            link(V.tensor_copy(scores.rearrange("p b e -> p (b e)"), banks(4)[:, 0:2 * NE]))
            link(V.tensor_tensor(biased, scores, rb.rearrange("p (o e) -> p o e", o=1).to_broadcast((P, TB, NE)), ALU.add))
            for b in range(TB):
                step(V.max(top8[:, b, :], biased[:, b, :]))
            sync()
            link(V.memset(top8[:, :, TOPE:8], -BANNED))
            for b in range(TB):
                step(V.match_replace(biased[:, b, :], top8[:, b, :], biased[:, b, :], TAKEN))
            sync()
            V.tensor_scalar(sel, biased, (BANNED + TAKEN) / 2, None, ALU.is_lt).then_inc(s_sel, 1)
            dve.wait_ge(s_sel, 1)
            link(V.tensor_tensor(gate, scores, sel, ALU.mult))
            link(V.tensor_reduce(wsum, gate, AX.X, ALU.add))
            link(V.reciprocal(wsum, wsum))
            link(V.scalar_tensor_tensor(gate, gate, ROUTE_SCALE, wsum.rearrange("p (b o) -> p b o", o=1).to_broadcast((P, TB, NE)),
                                        ALU.mult, ALU.mult))
            link(V.tensor_scalar(rank_in, sel, -1000.0, 1000.0, ALU.mult, ALU.add))
            dve.wait_ge(s_rk, 1)
            link(V.tensor_tensor(rank_in, rank_in, banks(3)[:, 0:2 * NE].rearrange("p (b e) -> p b e", b=TB), ALU.add))

            def find_slots(n, e0, q_n):
                full = (P, 2, CAP)
                experts = slice(e0, e0 + 2) if isinstance(e0, int) else bass.ds(e0, 2)
                so = slot_of[q_n].rearrange("p b (e c) -> p b e c", e=2)
                sg = slot_gate[q_n].rearrange("p b (e c) -> p b e c", e=2)
                for b in range(TB):
                    V.tensor_tensor(so[:, b], rank_in[:, b, experts].rearrange("p (e o) -> p e o", o=1).to_broadcast(full),
                                    iota_c.rearrange("p (o c) -> p o c", o=1).to_broadcast(full), ALU.is_equal).then_inc(s_Sf, 1)
                dve.wait_ge(s_Sf, n * 2 + 2)
                for b in range(TB):
                    V.tensor_tensor(sg[:, b], so[:, b], gate[:, b, experts].rearrange("p (e o) -> p e o", o=1).to_broadcast(full),
                                    ALU.mult).then_inc(s_S, 1)

            find_slots(0, 0, 0)
            link(V.tensor_reduce(cmax[0:1, :], banks(3)[0:1, 64:64 + NE], AX.X, ALU.max))
            V.tensor_copy(count[:, :], cmax[0:1, :]).then_inc(s_cnt, 1)

            dve.wait_ge(s_ssl, 1)
            dve.wait_ge(s_turn, T_SH + 2)
            V.tensor_tensor(hid_s.rearrange("p f t -> p (f t)"), silu_s.rearrange("p f t -> p (f t)"), banks((T_SH + 1) % 2),
                            ALU.mult).then_inc(s_sh, 1)
            link(V.tensor_scalar(g_over, rank_in, float(CAP), None, ALU.is_ge))
            link(V.tensor_tensor(g_over, g_over, gate, ALU.mult))

            def pair(i, q_, last=False):
                p = i * 3 + q_
                if not last:
                    if not (isinstance(p, int) and p < 2):
                        dve.wait_ge(s_htp, p - 1)
                    find_slots(p + 1, i * 6 + (2 * q_ + 2), (q_ + 1) % 3)
                dve.wait_ge(s_sl, p + 1)
                if not (isinstance(p, int) and p == 0):
                    dve.wait_ge(s_htp, p)
                V.tensor_tensor(hid, silu_e, banks(2)[:, F_E:2 * F_E], ALU.mult).then_inc(s_hid, 1)
                dve.wait_ge(s_hg, p + 1)
                dve.wait_ge(s_tk, p + 1)
                V.tensor_copy(slot_g[:, q_:q_ + 1], banks(2)[:, 0:1]).then_inc(s_sg, 1)
                dve.wait_ge(s_sg, p + 1)
                for half in range(2):
                    dve.wait_ge(s_y1, p * 2 + (half + 1))
                    V.scalar_tensor_tensor(yo[:, half * 512:(half + 1) * 512], banks(half), slot_g[:, q_:q_ + 1],
                                           yo_terms[0][half], ALU.mult, ALU.subtract).then_inc(s_y2, 1)
                for half in range(2):
                    dve.wait_ge(s_y3, p * 2 + (half + 1))
                    V.tensor_tensor(yo_terms[2][half], yo[:, half * 512:(half + 1) * 512], yo_terms[1][half],
                                    ALU.subtract).then_inc(s_yo, 1)

            for q_ in range(3):
                pair(0, q_)
            with dve.Fori(1, NPAIR // 3) as i:
                for q_ in range(3):
                    pair(i, q_)
            pair(NPAIR // 3, 0, last=True)
            for half in range(2):
                for b in range(TB):
                    dve.wait_ge(s_add, NPAIR + 2 * half + b)
                    hh = h[:, b, half * 512:(half + 1) * 512]
                    V.scalar_tensor_tensor(hh, hh, ALPHA, banks(4 + 2 * b + half), ALU.mult, ALU.add).then_inc(s_acc, 1)
                    dve.wait_ge(s_acc, 2 * half + b + 1)
                    step(V.bn_stats(stats[:, 2 * b + half, :], hh))
            with dve.If(over(dve)):
                dve.wait_ge(s_acc, 2 * TB)
                with dve.Fori(0, NE) as e:
                    dve.wait_ge(o_sl, e + 1)
                    V.tensor_tensor(hid_s.rearrange("p f t -> p (f t)"), silu_s.rearrange("p f t -> p (f t)"), banks(1),
                                    ALU.mult).then_inc(o_h, 1)
                    dve.wait_ge(o_dn, e + 1)
                    for b in range(TB):
                        V.scalar_tensor_tensor(h[:, b, :], banks(4 + 2 * b, 2), g_over[:, b, bass.ds(e, 1)], h[:, b, :],
                                               ALU.mult, ALU.add).then_inc(o_acc, 1)
                    dve.wait_ge(o_acc, e * 2 + 2)
                for b in range(TB):
                    for half in range(2):
                        V.bn_stats(stats[:, 2 * b + half, :], h[:, b, half * 512:(half + 1) * 512]).then_inc(o_st, 1)
                dve.wait_ge(o_st, 2 * TB)
            dve.wait_ge(s_acc, 2 * TB)
            dve.wait_ge(s_gb3, 32)
            for b in range(TB):
                layer_norm(h[:, b, :], b, s_y, stats_done=True, bias=ffn_bias)

        @block.tensor
        def _(pe):
            T = nc.tensor
            turns_on = [0, 0]

            def start_turn(t):
                if turns_on[t % 2]:
                    pe.wait_ge(s_free[t % 2], turns_on[t % 2])
                turns_on[t % 2] += 1

            def transpose_h(ready, done, b):
                pe.wait_ge(ready, b + 1)
                for k in range(KD):
                    ins = T.transpose(banks(2 + 2 * b, 2)[:, k * P:(k + 1) * P], h[:, b, k * P:(k + 1) * P], ident)
                ins.then_inc(done, 1)

            def feat(dst, w, c0, m=P, src=hT, nk=KD):
                for k in range(nk):
                    ins = T.matmul(dst, w[:, k, c0:c0 + m], src[:, k, :], start=(k == 0), stop=(k == nk - 1))
                return ins

            def tokm(dst, w, c0, n, b, src=hT, nk=KD, before_last=None):
                for k in range(nk):
                    if before_last and k == nk - 1:
                        pe.wait_ge(*before_last)
                    ins = T.matmul(dst, src[:, k, b * P:(b + 1) * P], w[:, k, c0:c0 + n], start=(k == 0), stop=(k == nk - 1))
                return ins

            pe.wait_ge(s_par, 16 * 10)
            pe.wait_ge(s_rp, 16 * 4)
            pe.wait_ge(s_con, 16)
            T.transpose(banks(6)[:, 0:79], prow[0:79, :], consts[0:79, 0, 0:79])
            for c in range(4):
                T.transpose(banks(7)[:, c * TAPS:(c + 1) * TAPS], dw_rows[0:TAPS, c * P:(c + 1) * P], consts[0:TAPS, 0, 0:TAPS])
            T.matmul(banks(6)[0:NH_A, 128:512], relb[0:NBUCKET, :], buckets[0:NBUCKET, :], start=True, stop=True).then_inc(s_prT, 1)
            for b in range(TB):
                transpose_h(s_h, s_hTp, b)

            arrived(pe, 0)
            wI = slot(0, KD, N_IDX_COLS)
            start_turn(0)
            for b in range(TB):
                pe.wait_ge(s_hT[b], 1 + b)
                ins = tokm(banks(0)[:, 256 * b:256 * b + NH_I + P], wI, 0, NH_I + P, b)
            ins.then_inc(s_turn, 1)
            start_turn(1)
            feat(banks(1)[:, 0:SEQ], wI, NH_I + P)
            feat(banks(1)[:, SEQ:2 * SEQ], wI, NH_I + 2 * P).then_inc(s_turn, 1)
            start_turn(2)
            for k in range(KD):
                for lo in (0, 64):
                    ins = T.matmul(banks(0)[lo:lo + 64, 0:SEQ], wI[:, k, NH_I + 3 * P:N_IDX_COLS], hT[:, k, :],
                                   start=(k == 0), stop=(k == KD - 1))
            ins.then_inc(s_turn, 1)
            arrived(pe, 1)
            arrived(pe, 2)
            for c in range(4):
                t = 3 + c
                start_turn(t)
                feat(banks(t % 2)[:, 0:SEQ], slot(1, KD, 512), c * P)
                feat(banks(t % 2)[:, SEQ:2 * SEQ], slot(2, KD, 512), c * P).then_inc(s_turn, 1)
                if c == 0:
                    pe.wait_ge(s_cr, 2)
                    for b in range(TB):
                        ins = T.transpose(banks(5)[:, b * P:(b + 1) * P], c_tok_major[:, b, :], ident)
                    ins.then_inc(s_cTp, 1)
                if c == 1:
                    pe.wait_ge(s_qk, 3)
                    pe.wait_ge(s_cT, 1)
                    for b in range(TB):
                        w = (b + 1) * P
                        for hh in range(NH_I):
                            lo = 64 * (hh % 2)
                            ins = T.matmul(banks(2 + 2 * b + hh % 2)[:, hh // 2 * w:(hh // 2 + 1) * w],
                                           qiT[lo:lo + 64, hh // 2, b * P:(b + 1) * P], kiT[lo:lo + 64, 0:w],
                                           start=True, stop=True)
                        ins.then_inc(s_sc, 1)

            def two_blocks(t, item, c0):
                arrived(pe, item)
                start_turn(t)
                w = slot(item, KD, 512)
                feat(banks(t % 2)[:, 0:SEQ], w, c0)
                feat(banks(t % 2)[:, SEQ:2 * SEQ], w, c0 + P).then_inc(s_turn, 1)

            for i in range(4):
                two_blocks(7 + i, 3 + i // 2, 256 * (i % 2))
            for i in range(2):
                two_blocks(11 + i, 5, 256 * i)
            pe.wait_ge(s_aq, 8)
            pe.wait_ge(s_cT, 1)
            pe.wait_ge(s_relu, 2)
            for b, bk in ((0, 2), (1, 4)):
                w = (b + 1) * P
                for hh in range(NH_A):
                    ins = T.matmul(banks(bk, 2 * (b + 1))[:, hh * w:(hh + 1) * w], aqT[:, hh, b * P:(b + 1) * P], cT[:, 0:w],
                                   start=True, stop=True)
                ins.then_inc(s_lg, 1)
            for i in range(2):
                two_blocks(13 + i, 6, 256 * i)

            def probs_T(n, b, sblk, bk):
                lg = logits0 if b == 0 else logits1
                pe.wait_ge(s_pn, b + 1)
                if n == 2:
                    pe.wait_ge(s_pT, 1)
                for hh in range(NH_A):
                    ins = T.transpose(banks(bk, 2)[:, hh * P:(hh + 1) * P], lg[:, hh, sblk * P:(sblk + 1) * P], ident)
                ins.then_inc(s_pTp, 1)

            for b in range(TB):
                t = 15 + b
                arrived(pe, 7)
                start_turn(t)
                tokm(banks(t % 2), slot(7, KD, 512), 0, 512, b).then_inc(s_turn, 1)
                if b == 0:
                    probs_T(0, 0, 0, 2)
                    probs_T(1, 1, 0, 6)
            probs_T(2, 1, 1, 2)
            two_blocks(17, 8, 0)
            for b in range(TB):
                pe.wait_ge(s_pT, 1 if b == 0 else 3)
                if b == 1:
                    pe.wait_ge(s_oT, 1)
                for half in range(2):
                    for s_ in range(b + 1):
                        ins = T.matmul(banks(4 + half), c_tok_major[:, s_, :],
                                       probsT[:, b + s_, 4 * half:4 * half + 4, :].rearrange("p h t -> p (h t)"),
                                       start=(s_ == 0), stop=(s_ == b))
                ins.then_inc(s_oTp, 1)
            two_blocks(18, 8, 256)
            pe.wait_ge(s_oT, 2)
            pe.wait_ge(s_uvl, 16)
            for hh in range(NH_A):
                lo = 64 * (hh % 2)
                ins = T.matmul(banks(6, 2)[lo:lo + 64, (hh // 2) * SEQ:(hh // 2 + 1) * SEQ], wuv[:, hh, :], oT_att[:, hh, :],
                               start=True, stop=True)
            ins.then_inc(s_uvp, 1)

            def level(n):
                bk = 2 + 2 * (n % 2)
                if n >= 2:
                    pe.wait_ge(s_pc, n - 1)
                if n == 0:
                    pe.wait_ge(s_rq, 4)
                    pe.wait_ge(s_ha, 2)
                    X, Y = qT, kT
                else:
                    pe.wait_ge(s_xy, n)
                    X, Y = Xl[(n - 1) % 2], Yl[(n - 1) % 2]
                if n < 8:
                    for m in range(8):
                        ins = T.matmul(banks(bk, 2)[:, m * P:(m + 1) * P], Y[:, m * P:(m + 1) * P], X[:, m * P:(m + 1) * P],
                                       start=True, stop=True)
                else:
                    for m in range(NH_R):
                        ins = T.matmul(banks(bk)[:, m * P:(m + 1) * P], Y[:, 2 * m * P:(2 * m + 1) * P],
                                       X[:, (2 * m + 1) * P:(2 * m + 2) * P], start=True, stop=True)
                ins.then_inc(s_pl, 1)

            def branch(br, m, src):
                t = T_BR[br] + m
                item = I_BR[br]
                if m == 0:
                    arrived(pe, item)
                if m % 4 == 0:
                    arrived(pe, item + 1 + m // 4)
                start_turn(t)
                feat(banks(t % 2)[:, 0:SEQ], slot(item + 1 + m // 4, KD, 512), (m % 4) * P)
                feat(banks(t % 2)[:, SEQ:2 * SEQ], slot(item, 4, D), m * P, src=src, nk=4).then_inc(s_turn, 1)

            pe.wait_ge(s_aT, 1)
            pe.wait_ge(s_oT, 2)
            level(0)
            for m in range(KD):
                branch(0, m, aT)
                if m == 0:
                    pe.wait_ge(s_conv, 1)
                    for c in range(4):
                        ins = T.matmul(banks(7)[:, 0:SEQ], mean_w, conv[:, c, :], start=(c == 0), stop=(c == 3))
                    ins.then_inc(s_mean, 1)
                level(m + 1)
                if m == 2:
                    pe.wait_ge(s_sqr, 1)
                    for b in range(TB):
                        for c in range(4):
                            ins = T.matmul(banks(7)[:, SEQ + b:SEQ + b + 1], conv_sq[:, c, b * P:(b + 1) * P], mean_w[:, 0:1],
                                           start=(c == 0), stop=(c == 3))
                    ins.then_inc(s_var, 1)
                if m == 4:
                    pe.wait_ge(s_cdg, 1)
                    T.matmul(banks(7)[:, SEQ:2 * SEQ], ones, cvs[:, 0:SEQ], start=True, stop=True).then_inc(s_csp, 1)
            pe.wait_ge(s_cT2, 1)
            for m in range(KD):
                branch(1, m, conv)
                if m == 0:
                    pe.wait_ge(s_pc, 9)
                    pe.wait_ge(s_rv, 2)
                    pe.wait_ge(s_cn, 1)
                    for hh in range(NH_R):
                        o = banks(6, 2)[:, hh * SEQ:(hh + 1) * SEQ]
                        T.matmul(o[:, 0:P], v_tok[:, 0, hh * P:(hh + 1) * P], inner[:, hh, 0, :], start=True, stop=True)
                        T.matmul(o[:, P:SEQ], v_tok[:, 0, hh * P:(hh + 1) * P], inter[:, hh, :], start=True, stop=False)
                        ins = T.matmul(o[:, P:SEQ], v_tok[:, 1, hh * P:(hh + 1) * P], inner[:, hh, 1, :], start=False, stop=True)
                    ins.then_inc(s_on, 1)
                if m == 1:
                    pe.wait_ge(s_osq, 1)
                    for n in range(8):
                        ins = T.matmul(banks(2)[:, n:n + 1], fz[:, n * P:(n + 1) * P], mean_o[:, 0:1], start=True, stop=True)
                    ins.then_inc(s_ms, 1)
                if m == 3:
                    pe.wait_ge(s_rdg, 1)
                    for z in range(2):
                        ins = T.matmul(banks(4 + z), ones, ls[:, 512 * z:512 * z + 512], start=True, stop=True)
                    ins.then_inc(s_rsp, 1)
            pe.wait_ge(s_ot, 1)
            for m in range(KD):
                branch(2, m, oT_rnn)
            pe.wait_ge(s_mg, 23)
            for b in range(TB):
                for half in range(2):
                    t = T_OUT + 2 * b + half
                    arrived(pe, I_OUT + half)
                    start_turn(t)
                    tokm(banks(t % 2), slot(I_OUT + half, KD, 512), 0, 512, b, src=merged,
                         before_last=(s_mg, 24)).then_inc(s_turn, 1)
                    if b == 1 and half == 0:
                        transpose_h(s_h2, s_h2Tp, 0)

            def shared_up(g, b):
                t = T_SH + g
                if b == 0:
                    start_turn(t)
                w = slot(I_SGU, KD, 512)
                for f in range(2):
                    for k in range(KD):
                        ins = T.matmul(banks(t % 2)[:, f * SEQ + b * P:f * SEQ + (b + 1) * P],
                                       w[:, k, (2 * g + f) * P:(2 * g + f + 1) * P], hT[:, k, b * P:(b + 1) * P],
                                       start=(k == 0), stop=(k == KD - 1))
                if b == 1:
                    ins.then_inc(s_turn, 1)

            arrived(pe, I_SGU)
            pe.wait_ge(s_h2T[0], 1)
            shared_up(0, 0)
            transpose_h(s_h2, s_h2Tp, 1)
            pe.wait_ge(s_ro, 32)
            pe.wait_ge(s_h2T[1], 2)
            feat(banks(2)[0:NE, 0:SEQ], rw, 0, m=NE).then_inc(s_rl, 1)
            shared_up(1, 0)
            pe.wait_ge(s_rsg, 1)
            for b in range(TB):
                ins = T.transpose(banks(4)[:, b * NE:(b + 1) * NE], scores_T[0:NE, b * P:(b + 1) * P], consts[0:NE, 0, 0:NE])
            ins.then_inc(s_rst, 1)
            shared_up(0, 1)
            pe.wait_ge(s_sel, 1)
            T.matmul(banks(3)[:, 0:NE], before, sel[:, 0, :], start=True, stop=True)
            T.matmul(banks(3)[:, NE:2 * NE], ones, sel[:, 0, :], start=True, stop=False)
            T.matmul(banks(3)[:, NE:2 * NE], before, sel[:, 1, :], start=False, stop=True)
            for b in range(TB):
                ins = T.matmul(banks(3)[:, 64:64 + NE], ones, sel[:, b, :], start=(b == 0), stop=(b == 1))
            ins.then_inc(s_rk, 1)
            shared_up(1, 1)

            def gather(q):
                for k in range(KD):
                    for b in range(TB):
                        for n in range(3):
                            ins = T.matmul(banks(0, 2)[:, k * P:(k + 1) * P], h_terms[b][n][:, k * P:(k + 1) * P],
                                           slot_of[q][:, b, :], start=(b == 0 and n == 0), stop=(b == 1 and n == 2))
                ins.then_inc(s_xp, 1)

            def add_out(q, last=False):
                for half in range(2):
                    if last:
                        pe.wait_ge(s_yo, 2 * NPAIR - 1 + half)
                    for b in range(TB):
                        for n in range(3):
                            ins = T.matmul(banks(4 + 2 * b + half), token_of[q][:, b * P:(b + 1) * P],
                                           yo_terms[n][half], start=False, stop=(last and n == 2))
                        if last:
                            ins.then_inc(s_add, 1)
                if not last:
                    ins.then_inc(s_add, 1)

            def pair(i, q, last=False):
                p = i * 3 + q
                first = isinstance(p, int) and p == 0
                for e in range(2):
                    s, v = pair_item(i, q, e)
                    pe.wait_ge(s_w[s], v)
                pe.wait_ge(s_xc, p + 1)
                if not first:
                    pe.wait_ge(s_sg, p)
                for k in range(KD):
                    for e in range(2):
                        w = wslot(PAIR_SLOTS[q][e]).rearrange("p (k n) -> p k n", k=KD)
                        ins = T.matmul(banks(2)[e * CAP:(e + 1) * CAP, :], xT[:, k, e * CAP:(e + 1) * CAP], w[:, k, :],
                                       start=(k == 0), stop=(k == KD - 1))
                ins.then_inc(s_gu, 1)
                if not last:
                    pe.wait_ge(s_S, p * 2 + 4)
                    if not first:
                        pe.wait_ge(s_y2, p * 2)
                    gather((q + 1) % 3)
                pe.wait_ge(s_hid, p + 1)
                if not first:
                    pe.wait_ge(s_hg, p)
                    pe.wait_ge(s_tk, p)
                for f in range(2):
                    T.transpose(banks(3)[:, f * P:(f + 1) * P], hid[:, f * P:(f + 1) * P], ident)
                for b in range(TB):
                    T.matmul(banks(3)[:, F_E + b * P:F_E + (b + 1) * P], slot_of[q][:, b, :], ident_b, start=True, stop=True)
                for b in range(TB):
                    ins = T.matmul(banks(2)[:, 0:1], slot_gate[q][:, b, :], ones[:, 0:1], start=(b == 0), stop=(b == 1))
                ins.then_inc(s_htp, 1)
                if not first:
                    pe.wait_ge(s_yo, p * 2)
                    add_out((q + 2) % 3)
                s, v = pair_item(i, q, 2)
                pe.wait_ge(s_w[s], v)
                pe.wait_ge(s_hg, p + 1)
                if not last:
                    pe.wait_ge(s_xc, p + 2)
                w = wslot(s).rearrange("p (e f n) -> p e f n", e=2, f=2)
                for half in range(2):
                    for f in range(2):
                        for e in range(2):
                            ins = T.matmul(banks(half)[e * CAP:(e + 1) * CAP, :], hidT[q][:, f * P + e * CAP:f * P + (e + 1) * CAP],
                                           w[:, e, f, half * 512:(half + 1) * 512], start=(f == 0), stop=(f == 1))
                    ins.then_inc(s_dn, 1)

            pe.wait_ge(s_S, 2)
            pe.wait_ge(s_sh, 1)
            pe.wait_ge(s_h3, TB)
            gather(0)
            arrived(pe, I_SDN)
            w_sdn = slot(I_SDN, 2, D)
            for b in range(TB):
                for half in range(2):
                    for f in range(2):
                        ins = T.matmul(banks(4 + 2 * b + half), hid_s[:, f, b * P:(b + 1) * P],
                                       w_sdn[:, f, half * 512:(half + 1) * 512], start=(f == 0), stop=False)
            ins.then_inc(s_sdn, 1)
            for q in range(3):
                pair(0, q)
            with pe.Fori(1, NPAIR // 3) as i:
                for q in range(3):
                    pair(i, q)
            pair(NPAIR // 3, 0, last=True)
            add_out(0, last=True)
            with pe.If(over(pe)):
                pe.wait_ge(s_acc, 2 * TB)
                wg = wslot(0).rearrange("p (k n) -> p k n", k=KD)
                wd = wslot(1)[:, 0:2 * D].rearrange("p (f n) -> p f n", f=2)

                def over_expert(e):
                    pe.wait_ge(o_w, e * 32 + 32)
                    after_first(pe, o_h, e, e)
                    for f in range(4):
                        ins = feat(banks(f // 2)[:, (f % 2) * SEQ:(f % 2 + 1) * SEQ], wg, f * P)
                    ins.then_inc(o_up, 1)
                    pe.wait_ge(o_h, e + 1)
                    after_first(pe, o_acc, e * 2, e)
                    for b in range(TB):
                        for half in range(2):
                            ins = tokm(banks(4 + 2 * b + half), wd, half * 512, 512, b, src=hid_s, nk=2)
                    ins.then_inc(o_dn, 1)

                over_expert(0)
                with pe.Fori(1, NE) as e:
                    over_expert(e)


_INS = ["x", "ln_in_g", "ln_in_b", "w_in", "b_in", "conv_dw", "conv_b", "conv_ln_g", "conv_ln_b", "w_conv_proj",
        "hgrn_gamma", "hgrn_norm_g", "w_rnn_proj", "kv_norm_g", "w_uv", "w_att_proj", "rel_bias", "w_out",
        "ln_mix_g", "ln_mix_b", "router_w", "router_b", "w_expert_gu", "w_expert_dn", "w_shared_gu",
        "w_shared_dn", "ln_ffn_g", "ln_ffn_b"]


def shape_constants():
    import numpy as np
    a, b = np.arange(P)[:, None], np.arange(P)[None, :]
    tables = np.stack([a == b, np.ones((P, P)), a < b, np.where(b <= a, 3.0e38, BANNED), np.where(b <= a, 0.0, OFF),
                       np.full((P, P), 1 / D_CONV), np.full((P, P), 1 / P)], axis=1).astype(np.float32)
    level = [a == b] + [(a // (2 * hf) == b // (2 * hf)) & (a % (2 * hf) < hf) & (b % (2 * hf) >= hf) for hf in HALVES]
    dist = np.maximum(np.arange(NDIST) - (P - 1), 0)
    exact = NBUCKET // 2
    large = exact + (np.log(np.maximum(dist, 1).astype(np.float32) / exact) / math.log(128 / exact)
                     * (NBUCKET - exact)).astype(np.int32)
    bucket = np.where(dist < exact, dist, np.minimum(large, NBUCKET - 1))
    onehot = (bucket[None, :] == np.arange(NBUCKET)[:, None]).astype(np.float32)
    return {"c_f32": tables, "c_level": np.stack(level, axis=1).astype(np.float32), "c_onehot": onehot}


def kernel(**inputs):
    import numpy as np
    import concourse.bacc as bacc
    from concourse.bass_utils import run_bass_kernel_spmd

    nc = bacc.Bacc("TRN2", target_bir_lowering=False, num_devices=1)
    arrays, args = {}, {}
    for name, a in [(n, np.ascontiguousarray(inputs[n])) for n in _INS] + list(shape_constants().items()):
        arrays[f"in_{name}"] = a
        args[name] = nc.dram_tensor(f"in_{name}", a.shape, mybir.dt.from_np(a.dtype), kind="ExternalInput").ap()
    args["out"] = nc.dram_tensor("out_0", (1, SEQ, D), F32, kind="ExternalOutput").ap()
    build(nc, **args)
    r = run_bass_kernel_spmd(nc, [arrays], core_ids=[0])
    return r.results[0]["out_0"]
```
